# Optimizing a Trainium2 kernel written in Bass

```python
import jax, jax.numpy as jnp
from jax import lax
import numpy as np

D_MODEL = 1024
BATCH = 1
SEQ = 1024
DEPTH = 1

PLE_DIM = 256
MLA_HEADS = 4
QK_NOPE_DIM = 128
QK_ROPE_DIM = 64
QK_HEAD_DIM = QK_NOPE_DIM + QK_ROPE_DIM
V_HEAD_DIM = 128
Q_LORA_RANK = 256
KV_LORA_RANK = 128
ROPE_THETA = 10000.0
MLA_WIDTH = MLA_HEADS * V_HEAD_DIM
Q_BLOCK = 128
MLSTM_HEADS = 4
MLSTM_HEAD_DIM = 128
MLSTM_WIDTH = MLSTM_HEADS * MLSTM_HEAD_DIM
CONV_WIDTH = 4
CHUNK = 64
D_MIX = MLA_WIDTH + MLSTM_WIDTH
IN_SIZES = (Q_LORA_RANK, KV_LORA_RANK, QK_ROPE_DIM, MLSTM_WIDTH, MLSTM_WIDTH, MLSTM_WIDTH, MLSTM_WIDTH, MLSTM_HEADS, MLSTM_HEADS)
D_IN = sum(IN_SIZES)
D_FF = ((8 * D_MODEL + 3 * 256 - 1) // (3 * 256)) * 256
EPS = 1e-6


def rms_norm(x, g):
    xf = x.astype(jnp.float32)
    y = xf * lax.rsqrt(jnp.mean(xf * xf, axis=-1, keepdims=True) + EPS)
    return (y * g.astype(jnp.float32)).astype(x.dtype)

def split_cols(z, sizes):
    offs = np.cumsum(sizes)[:-1].tolist()
    return jnp.split(z, offs, axis=-1)

def rope_cos_sin(positions):
    inv_freq = ROPE_THETA ** (-jnp.arange(0, QK_ROPE_DIM, 2, dtype=jnp.float32) / QK_ROPE_DIM)
    ang = positions.astype(jnp.float32)[..., None] * inv_freq
    return jnp.cos(ang), jnp.sin(ang)

def apply_rope(t, cos, sin):
    tf = t.astype(jnp.float32)
    t1, t2 = tf[..., :QK_ROPE_DIM // 2], tf[..., QK_ROPE_DIM // 2:]
    return jnp.concatenate([t1 * cos - t2 * sin, t2 * cos + t1 * sin], axis=-1).astype(t.dtype)

def causal_mla(q, k, v):
    B, S, H, _ = q.shape
    nb = S // Q_BLOCK
    qb = (q * (QK_HEAD_DIM ** -0.5)).reshape(B, nb, Q_BLOCK, H, QK_HEAD_DIM).transpose(1, 0, 3, 2, 4)
    key_pos = jnp.arange(S)

    def one_block(args):
        q_blk, blk = args
        s = jnp.einsum('bhqd,bkhd->bhqk', q_blk, k).astype(jnp.float32)
        q_pos = blk * Q_BLOCK + jnp.arange(Q_BLOCK)
        s = jnp.where(key_pos[None, :] <= q_pos[:, None], s, -jnp.inf)
        pr = jax.nn.softmax(s, axis=-1).astype(v.dtype)
        return jnp.einsum('bhqk,bkhv->bqhv', pr, v)

    out = lax.map(one_block, (qb, jnp.arange(nb)))
    return out.transpose(1, 0, 2, 3, 4).reshape(B, S, H * V_HEAD_DIM)

def causal_dwconv(t, w, b):
    S = t.shape[1]
    tp = jnp.pad(t, ((0, 0), (CONV_WIDTH - 1, 0), (0, 0)))
    acc = b
    for j in range(CONV_WIDTH):
        acc = acc + w[j] * tp[:, j:j + S]
    return acc

def mlstm_chunkwise(q, k, v, i_pre, f_pre):
    out_dtype = q.dtype
    B, S, NH, DH = q.shape
    nc = S // CHUNK
    f32 = jnp.float32

    def chunks4(t):
        return t.astype(f32).reshape(B, nc, CHUNK, NH, DH).transpose(1, 0, 3, 2, 4)

    def chunks3(t):
        return t.astype(f32).reshape(B, nc, CHUNK, NH).transpose(1, 0, 3, 2)

    qc_all = chunks4(q)
    kc_all = chunks4(k) * (DH ** -0.5)
    vc_all = chunks4(v)
    ic_all = chunks3(i_pre)
    fc_all = jax.nn.log_sigmoid(chunks3(f_pre))
    tril = jnp.tril(jnp.ones((CHUNK, CHUNK), dtype=bool))

    def step(carry, xs):
        C, n, m = carry
        qc, kc, vc, ic, fc = xs
        b = jnp.cumsum(fc, axis=-1)
        g = b[..., -1]
        d = b[..., :, None] - b[..., None, :] + ic[..., None, :]
        d = jnp.where(tril, d, -jnp.inf)
        m_inter = b + m[..., None]
        m_j = jnp.maximum(m_inter, d.max(axis=-1))
        s = jnp.einsum('bhld,bhsd->bhls', qc, kc) * jnp.exp(d - m_j[..., None])
        inter = jnp.exp(m_inter - m_j)
        num = jnp.einsum('bhls,bhsv->bhlv', s, vc) + inter[..., None] * jnp.einsum('bhld,bhdv->bhlv', qc, C)
        den = s.sum(axis=-1) + inter * jnp.einsum('bhld,bhd->bhl', qc, n)
        h = num / jnp.maximum(jnp.abs(den), jnp.exp(-m_j))[..., None]
        a = g[..., None] - b + ic
        m_new = jnp.maximum(g + m, a.max(axis=-1))
        decay = jnp.exp(g + m - m_new)
        w = jnp.exp(a - m_new[..., None])
        C_new = decay[..., None, None] * C + jnp.einsum('bhs,bhsd,bhsv->bhdv', w, kc, vc)
        n_new = decay[..., None] * n + jnp.einsum('bhs,bhsd->bhd', w, kc)
        return (C_new, n_new, m_new), h

    init = (jnp.zeros((B, NH, DH, DH), f32), jnp.zeros((B, NH, DH), f32), jnp.zeros((B, NH), f32))
    _, h = lax.scan(step, init, (qc_all, kc_all, vc_all, ic_all, fc_all))
    return h.transpose(1, 0, 3, 2, 4).reshape(B, S, NH, DH).astype(out_dtype)

def first_inputs(seed: int = 0) -> dict:
    key = jax.random.key(seed)
    ks = jax.random.split(key, 26)
    f32 = jnp.float32

    def nrm(k, shape, scale):
        return jax.random.normal(k, shape, f32) * scale

    def gain(k, shape):
        return 1.0 + 0.05 * jax.random.normal(k, shape, f32)

    L = DEPTH
    x = nrm(ks[0], (BATCH, SEQ, D_MODEL), 1.0)
    p = nrm(ks[1], (DEPTH, BATCH, SEQ, PLE_DIM), 1.0)
    offset = jax.random.randint(ks[2], (BATCH, 1), 0, 1024, dtype=jnp.int32)
    positions = (offset + jnp.arange(SEQ, dtype=jnp.int32)[None, :]).astype(jnp.int32)
    return {
        "x": x,
        "p": p,
        "positions": positions,
        "attn_pre_norm": gain(ks[3], (L, D_MODEL)),
        "attn_post_norm": gain(ks[4], (L, D_MODEL)),
        "w_in": nrm(ks[5], (L, D_MODEL, D_IN), D_MODEL ** -0.5),
        "q_norm": gain(ks[6], (L, Q_LORA_RANK)),
        "kv_norm": gain(ks[7], (L, KV_LORA_RANK)),
        "w_uq": nrm(ks[8], (L, Q_LORA_RANK, MLA_HEADS * QK_HEAD_DIM), Q_LORA_RANK ** -0.5),
        "w_ukv": nrm(ks[9], (L, KV_LORA_RANK, MLA_HEADS * (QK_NOPE_DIM + V_HEAD_DIM)), KV_LORA_RANK ** -0.5),
        "conv_w": nrm(ks[10], (L, CONV_WIDTH, 2 * MLSTM_WIDTH), CONV_WIDTH ** -0.5),
        "conv_b": nrm(ks[11], (L, 2 * MLSTM_WIDTH), 0.02),
        "gate_bias_i": nrm(ks[12], (L, MLSTM_HEADS), 0.1),
        "gate_bias_f": 3.0 + nrm(ks[13], (L, MLSTM_HEADS), 0.5),
        "mlstm_norm": gain(ks[14], (L, MLSTM_WIDTH)),
        "w_out": nrm(ks[15], (L, D_MIX, D_MODEL), D_MIX ** -0.5),
        "ffn_pre_norm": gain(ks[16], (L, D_MODEL)),
        "ffn_post_norm": gain(ks[17], (L, D_MODEL)),
        "w_gate": nrm(ks[18], (L, D_MODEL, D_FF), D_MODEL ** -0.5),
        "w_up": nrm(ks[19], (L, D_MODEL, D_FF), D_MODEL ** -0.5),
        "w_down": nrm(ks[20], (L, D_FF, D_MODEL), D_FF ** -0.5),
        "w_ple_proj": nrm(ks[21], (L, PLE_DIM, D_MODEL), PLE_DIM ** -0.5),
        "w_ple_gate": nrm(ks[22], (L, D_MODEL, D_MODEL), D_MODEL ** -0.5),
    }

def first_block(x, p, positions, attn_pre_norm, attn_post_norm, w_in, q_norm, kv_norm, w_uq, w_ukv,
              conv_w, conv_b, gate_bias_i, gate_bias_f, mlstm_norm, w_out, ffn_pre_norm, ffn_post_norm,
              w_gate, w_up, w_down, w_ple_proj, w_ple_gate):
    B, S, _ = x.shape
    cos, sin = rope_cos_sin(positions)
    hd = (B, S, MLSTM_HEADS, MLSTM_HEAD_DIM)
    h = x
    for i in range(DEPTH):
        u = rms_norm(h, attn_pre_norm[i])
        c_q, c_kv, k_rope, m_q, m_k, m_v, m_o, m_i, m_f = split_cols(u @ w_in[i], IN_SIZES)

        q = (rms_norm(c_q, q_norm[i]) @ w_uq[i]).reshape(B, S, MLA_HEADS, QK_HEAD_DIM)
        kv = (rms_norm(c_kv, kv_norm[i]) @ w_ukv[i]).reshape(B, S, MLA_HEADS, QK_NOPE_DIM + V_HEAD_DIM)
        q_nope, q_pe = q[..., :QK_NOPE_DIM], q[..., QK_NOPE_DIM:]
        k_nope, v = kv[..., :QK_NOPE_DIM], kv[..., QK_NOPE_DIM:]
        q_pe = apply_rope(q_pe, cos[:, :, None], sin[:, :, None])
        k_pe = apply_rope(k_rope, cos, sin)[:, :, None]
        q = jnp.concatenate([q_nope, q_pe], axis=-1)
        k = jnp.concatenate([k_nope, jnp.broadcast_to(k_pe, (B, S, MLA_HEADS, QK_ROPE_DIM))], axis=-1)
        mla_out = causal_mla(q, k, v)

        qk = jax.nn.silu(causal_dwconv(jnp.concatenate([m_q, m_k], axis=-1), conv_w[i], conv_b[i]))
        mq, mk = qk[..., :MLSTM_WIDTH], qk[..., MLSTM_WIDTH:]
        hm = mlstm_chunkwise(mq.reshape(hd), mk.reshape(hd), m_v.reshape(hd),
                             m_i + gate_bias_i[i], m_f + gate_bias_f[i])
        hm = rms_norm(hm, mlstm_norm[i].reshape(MLSTM_HEADS, MLSTM_HEAD_DIM)).reshape(B, S, MLSTM_WIDTH)
        mlstm_out = jax.nn.sigmoid(m_o) * hm

        mix = jnp.concatenate([mla_out, mlstm_out], axis=-1) @ w_out[i]
        h = h + rms_norm(mix, attn_post_norm[i])

        f = rms_norm(h, ffn_pre_norm[i])
        f = (jax.nn.silu(f @ w_gate[i]) * (f @ w_up[i])) @ w_down[i]
        h = h + rms_norm(f, ffn_post_norm[i])

        h = h + jax.nn.sigmoid(h @ w_ple_gate[i]) * (p[i] @ w_ple_proj[i])
    return h


N_MIXERS = 2
POOL_EXPAND = 2
D_POOL = POOL_EXPAND * D_MODEL
POOL_WINDOWS = (2, 4, 8, 16)
N_POOL_GROUPS = len(POOL_WINDOWS)
POOL_GROUP = D_POOL // N_POOL_GROUPS
HEAD_DIM = 64
N_HEADS = D_MODEL // HEAD_DIM
N_KV = 4
HPG = N_HEADS // N_KV
D_ATT = N_HEADS * HEAD_DIM
D_KV = N_KV * HEAD_DIM
N_BRANCH = 3
CMP_BLOCK = 32
CMP_STRIDE = 16
CMP_HIDDEN = 4 * HEAD_DIM
SEL_BLOCK = 64
SEL_TOPN = 8
WINDOW = 256
Q_BLOCK_2 = 64
NSA_SPLITS = (D_ATT, D_KV, D_KV, D_KV, D_KV, D_KV, D_KV, D_ATT, N_BRANCH * N_HEADS)
NSA_VALUE_SLOTS = (2, 4, 6)
D_NSA_IN = sum(NSA_SPLITS)

N_POOL_LAYERS = (DEPTH + N_MIXERS - 1) // N_MIXERS
N_NSA_LAYERS = DEPTH // N_MIXERS

DN_ALPHA = (2.0 * DEPTH) ** 0.25
DN_BETA = (8.0 * DEPTH) ** -0.25
LN_EPS = 1e-5
NEG_INF = -1e30
FORCE_SCORE = 1e9


def layer_norm(x, g, b):
    xf = x.astype(jnp.float32)
    mu = jnp.mean(xf, axis=-1, keepdims=True)
    var = jnp.mean(jnp.square(xf - mu), axis=-1, keepdims=True)
    y = (xf - mu) * lax.rsqrt(var + LN_EPS) * g.astype(jnp.float32) + b.astype(jnp.float32)
    return y.astype(x.dtype)

def alibi_slopes():
    h = jnp.arange(1, N_HEADS + 1, dtype=jnp.float32)
    return (2.0 ** (-8.0 * h / N_HEADS)).reshape(N_KV, HPG)

def masked_softmax(s, valid):
    p = jax.nn.softmax(jnp.where(valid, s, NEG_INF), axis=-1)
    return jnp.where(valid, p, 0.0)

def pool_mixer(x, w_in, w_grp, scale, w_out):
    B, S, _ = x.shape
    h = x @ w_in
    u, z = h[..., :D_POOL], h[..., D_POOL:]
    u = u.astype(jnp.float32).reshape(B, S, N_POOL_GROUPS, POOL_GROUP)
    csum = jnp.cumsum(u, axis=1)
    t = jnp.arange(S)
    outs = []
    for g, w in enumerate(POOL_WINDOWS):
        c = csum[:, :, g]
        lag = jnp.pad(c, ((0, 0), (w, 0), (0, 0)))[:, :S]
        cnt = jnp.minimum(t + 1, w).astype(jnp.float32)[None, :, None]
        outs.append((c - lag) / cnt - u[:, :, g])
    m = jnp.stack(outs, axis=2).astype(x.dtype)
    m = jnp.einsum('bsgc,gcd->bsgd', m, w_grp).reshape(B, S, D_POOL) * scale
    return (m * jax.nn.silu(z)) @ w_out

def nsa_mixer(x, w_in, pos_k, w1_k, w2_k, pos_v, w1_v, w2_v, w_out):
    B, S, _ = x.shape
    dt = x.dtype
    h = x @ w_in
    q, kc, vc, ks, vs, kw, vw, z, gl = jnp.split(h, np.cumsum(NSA_SPLITS)[:-1].tolist(), axis=-1)
    q = q.reshape(B, S, N_KV, HPG, HEAD_DIM) * (HEAD_DIM ** -0.5)
    kc, vc, ks, vs, kw, vw = [a.reshape(B, S, N_KV, HEAD_DIM) for a in (kc, vc, ks, vs, kw, vw)]
    gates = jax.nn.sigmoid(gl.astype(jnp.float32)).reshape(B, S, N_KV, HPG, N_BRANCH)
    slopes = alibi_slopes()[None, :, :, None, None]

    n_cmp = (S - CMP_BLOCK) // CMP_STRIDE + 1
    cmp_idx = np.arange(n_cmp)[:, None] * CMP_STRIDE + np.arange(CMP_BLOCK)[None, :]
    cmp_end = jnp.asarray(cmp_idx[:, -1], dtype=jnp.int32)

    def compress(a, pos, w1, w2):
        blk = a[:, cmp_idx] + pos[None, None, :, None, :]
        blk = blk.transpose(0, 1, 3, 2, 4).reshape(B, n_cmp, N_KV, CMP_BLOCK * HEAD_DIM)
        return jax.nn.silu(blk @ w1) @ w2

    k_cmp = compress(kc, pos_k, w1_k, w2_k)
    v_cmp = compress(vc, pos_v, w1_v, w2_v)

    n_sel = S // SEL_BLOCK
    top_n = min(SEL_TOPN, n_sel)
    c0 = np.arange(n_cmp)[:, None] * CMP_STRIDE
    j0 = np.arange(n_sel)[None, :] * SEL_BLOCK
    overlap = jnp.asarray((c0 < j0 + SEL_BLOCK) & (c0 + CMP_BLOCK > j0), dtype=jnp.float32)
    ks_blk = ks.reshape(B, n_sel, SEL_BLOCK, N_KV, HEAD_DIM).transpose(0, 3, 1, 2, 4)
    vs_blk = vs.reshape(B, n_sel, SEL_BLOCK, N_KV, HEAD_DIM).transpose(0, 3, 1, 2, 4)
    b_ix = jnp.arange(B)[:, None, None, None]
    g_ix = jnp.arange(N_KV)[None, :, None, None]
    blk_ids = jnp.arange(n_sel)
    in_blk = jnp.arange(SEL_BLOCK)

    kw_pad = jnp.pad(kw, ((0, 0), (WINDOW, 0), (0, 0), (0, 0)))
    vw_pad = jnp.pad(vw, ((0, 0), (WINDOW, 0), (0, 0), (0, 0)))
    win_off = jnp.arange(WINDOW + Q_BLOCK_2) - WINDOW

    def block(i):
        q0 = i * Q_BLOCK_2
        qb = lax.dynamic_slice_in_dim(q, q0, Q_BLOCK_2, axis=1)
        gb = lax.dynamic_slice_in_dim(gates, q0, Q_BLOCK_2, axis=1)
        t = q0 + jnp.arange(Q_BLOCK_2)

        dist = t[:, None] - cmp_end[None, :]
        s = jnp.einsum('bqghd,bcgd->bghqc', qb, k_cmp).astype(jnp.float32)
        s = s - slopes * dist.astype(jnp.float32)
        p_cmp = masked_softmax(s, dist >= 0)
        o_cmp = jnp.einsum('bghqc,bcgd->bqghd', p_cmp.astype(dt), v_cmp)

        imp = jnp.einsum('bghqc,cn->bgqn', p_cmp, overlap)
        cur = t // SEL_BLOCK
        forced = (blk_ids[None] == 0) | (blk_ids[None] == cur[:, None]) | (blk_ids[None] == cur[:, None] - 1)
        future = blk_ids[None] > cur[:, None]
        imp = jnp.where(forced, FORCE_SCORE, jnp.where(future, NEG_INF, imp))
        _, sel = lax.top_k(imp, top_n)
        k_g = ks_blk[b_ix, g_ix, sel].reshape(B, N_KV, Q_BLOCK_2, top_n * SEL_BLOCK, HEAD_DIM)
        v_g = vs_blk[b_ix, g_ix, sel].reshape(B, N_KV, Q_BLOCK_2, top_n * SEL_BLOCK, HEAD_DIM)
        pos = (sel[..., None] * SEL_BLOCK + in_blk).reshape(B, N_KV, Q_BLOCK_2, top_n * SEL_BLOCK)
        dist = t[None, None, :, None] - pos
        s = jnp.einsum('bqghd,bgqkd->bghqk', qb, k_g).astype(jnp.float32)
        s = s - slopes * dist[:, :, None].astype(jnp.float32)
        p = masked_softmax(s, (dist >= 0)[:, :, None])
        o_sel = jnp.einsum('bghqk,bgqkd->bqghd', p.astype(dt), v_g)

        kwb = lax.dynamic_slice_in_dim(kw_pad, q0, WINDOW + Q_BLOCK_2, axis=1)
        vwb = lax.dynamic_slice_in_dim(vw_pad, q0, WINDOW + Q_BLOCK_2, axis=1)
        spos = q0 + win_off
        dist = t[:, None] - spos[None, :]
        valid = (dist >= 0) & (dist < WINDOW) & (spos[None, :] >= 0)
        s = jnp.einsum('bqghd,bkgd->bghqk', qb, kwb).astype(jnp.float32)
        s = s - slopes * dist.astype(jnp.float32)
        p = masked_softmax(s, valid)
        o_win = jnp.einsum('bghqk,bkgd->bqghd', p.astype(dt), vwb)

        o = gb[..., 0:1] * o_cmp + gb[..., 1:2] * o_sel + gb[..., 2:3] * o_win
        return o.astype(dt).reshape(B, Q_BLOCK_2, D_ATT)

    o = lax.map(block, jnp.arange(S // Q_BLOCK_2))
    o = o.transpose(1, 0, 2, 3).reshape(B, S, D_ATT)
    return (o * jax.nn.silu(z)) @ w_out

def second_inputs(seed: int = 0) -> dict:
    key = jax.random.key(seed)
    k = jax.random.split(key, 16)
    nA, nB = N_POOL_LAYERS, N_NSA_LAYERS

    def nrm(kk, shape, scale):
        return jax.random.normal(kk, shape, jnp.float32) * scale

    pool_col = jnp.asarray(np.concatenate([np.full(D_POOL, DN_BETA), np.ones(D_POOL)]), dtype=jnp.float32)
    nsa_col = jnp.asarray(np.concatenate([np.full(n, DN_BETA if s in NSA_VALUE_SLOTS else 1.0)
                                          for s, n in enumerate(NSA_SPLITS)]), dtype=jnp.float32)
    return {
        'x': nrm(k[0], (BATCH, SEQ, D_MODEL), 1.0),
        'ln_g': 1.0 + nrm(k[1], (DEPTH, D_MODEL), 0.02),
        'ln_b': nrm(k[2], (DEPTH, D_MODEL), 0.02),
        'pool_w_in': nrm(k[3], (nA, D_MODEL, 2 * D_POOL), D_MODEL ** -0.5) * pool_col,
        'pool_w_grp': nrm(k[4], (nA, N_POOL_GROUPS, POOL_GROUP, POOL_GROUP), POOL_GROUP ** -0.5),
        'pool_scale': 1.0 + nrm(k[5], (nA, D_POOL), 0.02),
        'pool_w_out': nrm(k[6], (nA, D_POOL, D_MODEL), D_POOL ** -0.5 * DN_BETA),
        'nsa_w_in': nrm(k[7], (nB, D_MODEL, D_NSA_IN), D_MODEL ** -0.5) * nsa_col,
        'nsa_cmp_pos_k': nrm(k[8], (nB, CMP_BLOCK, HEAD_DIM), 0.02),
        'nsa_cmp_w1_k': nrm(k[9], (nB, CMP_BLOCK * HEAD_DIM, CMP_HIDDEN), (CMP_BLOCK * HEAD_DIM) ** -0.5),
        'nsa_cmp_w2_k': nrm(k[10], (nB, CMP_HIDDEN, HEAD_DIM), CMP_HIDDEN ** -0.5),
        'nsa_cmp_pos_v': nrm(k[11], (nB, CMP_BLOCK, HEAD_DIM), 0.02),
        'nsa_cmp_w1_v': nrm(k[12], (nB, CMP_BLOCK * HEAD_DIM, CMP_HIDDEN), (CMP_BLOCK * HEAD_DIM) ** -0.5),
        'nsa_cmp_w2_v': nrm(k[13], (nB, CMP_HIDDEN, HEAD_DIM), CMP_HIDDEN ** -0.5),
        'nsa_w_out': nrm(k[14], (nB, D_ATT, D_MODEL), D_ATT ** -0.5 * DN_BETA),
    }

def second_block(x, ln_g, ln_b, pool_w_in, pool_w_grp, pool_scale, pool_w_out,
              nsa_w_in, nsa_cmp_pos_k, nsa_cmp_w1_k, nsa_cmp_w2_k,
              nsa_cmp_pos_v, nsa_cmp_w1_v, nsa_cmp_w2_v, nsa_w_out):
    for i in range(DEPTH):
        j = i // N_MIXERS
        if i % N_MIXERS == 0:
            y = pool_mixer(x, pool_w_in[j], pool_w_grp[j], pool_scale[j], pool_w_out[j])
        else:
            y = nsa_mixer(x, nsa_w_in[j], nsa_cmp_pos_k[j], nsa_cmp_w1_k[j], nsa_cmp_w2_k[j],
                          nsa_cmp_pos_v[j], nsa_cmp_w1_v[j], nsa_cmp_w2_v[j], nsa_w_out[j])
        x = layer_norm(DN_ALPHA * x + y, ln_g[i], ln_b[i])
    return x


def setup_inputs(seed=0):
    out = dict(first_inputs(seed))
    for name, value in second_inputs(seed + 1).items():
        if name != "x":
            out[name + "_2"] = value
    return out


def reference(
    x, p, positions, attn_pre_norm, attn_post_norm, w_in, q_norm, kv_norm, w_uq, w_ukv, conv_w,
    conv_b, gate_bias_i, gate_bias_f, mlstm_norm, w_out, ffn_pre_norm, ffn_post_norm, w_gate,
    w_up, w_down, w_ple_proj, w_ple_gate, ln_g_2, ln_b_2, pool_w_in_2, pool_w_grp_2,
    pool_scale_2, pool_w_out_2, nsa_w_in_2, nsa_cmp_pos_k_2, nsa_cmp_w1_k_2, nsa_cmp_w2_k_2,
    nsa_cmp_pos_v_2, nsa_cmp_w1_v_2, nsa_cmp_w2_v_2, nsa_w_out_2,
):
    x = first_block(
        x, p, positions, attn_pre_norm, attn_post_norm, w_in, q_norm, kv_norm, w_uq, w_ukv,
        conv_w, conv_b, gate_bias_i, gate_bias_f, mlstm_norm, w_out, ffn_pre_norm,
        ffn_post_norm, w_gate, w_up, w_down, w_ple_proj, w_ple_gate,
    )
    return second_block(
        x, ln_g_2, ln_b_2, pool_w_in_2, pool_w_grp_2, pool_scale_2, pool_w_out_2, nsa_w_in_2,
        nsa_cmp_pos_k_2, nsa_cmp_w1_k_2, nsa_cmp_w2_k_2, nsa_cmp_pos_v_2, nsa_cmp_w1_v_2,
        nsa_cmp_w2_v_2, nsa_w_out_2,
    )


_drawn_inputs = setup_inputs


def setup_inputs(seed=0):
    import zlib

    import numpy as np

    out = dict(_drawn_inputs(seed))
    spreads = {}
    factors = {'q_norm': 5.979,
     'kv_norm': 3.629,
     'conv_b': 18.407,
     'gate_bias_i': 200.0,
     'ln_g_2': 21.896,
     'ln_b_2': 22.506,
     'pool_scale_2': 73.297,
     'mlstm_norm': 7.061}
    for name, (base, spread) in spreads.items():
        noise = np.random.default_rng([zlib.crc32(name.encode()), seed]).standard_normal(out[name].shape)
        drawn = base * np.exp(spread * noise) if base else spread * noise
        out[name] = __import__('jax').numpy.asarray(drawn.astype(out[name].dtype))
    for name, factor in factors.items():
        out[name] = (out[name] * factor).astype(out[name].dtype)
    return out
```

```python
from contextlib import ExitStack

import concourse.bass as bass
from concourse import mybir

F32 = mybir.dt.float32
F32R = mybir.dt.float32r
I32 = mybir.dt.int32
ACT = mybir.ActivationFunctionType
ALU = mybir.AluOpType
AX = mybir.AxisListType

P = 128
S = 1024
D = 1024
HALF = 512
TB = S // P
KD = D // P
EPS = 1e-6
LN_EPS = 1e-5
NEG = -1e30

PLE = 256
HEADS = 4
NOPE, ROPE, VH = 128, 64, 128
QLORA, KVLORA = 256, 128
QK_SCALE = float(NOPE + ROPE) ** -0.5
MW = 512
MH_SCALE = 128.0 ** -0.5
CONV = 4
DFF = 2816
FG = DFF // 256
DP = 2048
GROUPS = 4
GW = DP // GROUPS
WINDOWS = (2, 4, 8, 16)
HALO = 16
ALPHA = 2.0 ** 0.25

KB = 1024
PI_SAFE = 3.1415925
TWO_PI_A = 6.28125
TWO_PI_B = 0.0019350051879882812
TWO_PI_C = 2.0 * 3.141592653589793 - TWO_PI_A - TWO_PI_B
SMALL = {"allow_slow_non_contiguous": True}
ROUND = 12582912.0


class Chain:

    def __init__(self, sem):
        self.sem, self.at = sem, 0

    def mark(self, instruction):
        instruction.then_inc(self.sem, 1)
        self.at = self.at + 1

    def wait(self, engine):
        engine.wait_ge(self.sem, self.at)

    def do(self, engine, instruction):
        self.mark(instruction)
        self.wait(engine)


def build(nc, a, out):
    ctx = ExitStack()
    with ctx:
        def sem(name):
            return ctx.enter_context(nc.semaphore(name))

        ARENA = 200 * KB + 8000
        base = 16512
        ctx.enter_context(nc.sbuf_tensor("arena", [P, ARENA // 4], F32))

        def at(name, shape, offset, dt=F32):
            return nc.alloc_sbuf_tensor_at(name, shape, dt, offset=base + offset)

        A, B, C, E, M = 56 * KB, 120 * KB, 152 * KB, 184 * KB, 200 * KB
        SLOT = [0, 16 * KB, 32 * KB, C]
        S2 = SLOT[2]
        w_hi = [at(f"w_hi{s}", [P, 2048], SLOT[s], F32R) for s in range(4)]
        w_lo = [at(f"w_lo{s}", [P, 2048], SLOT[s] + 8 * KB, F32R) for s in range(4)]
        stage = at("stage", [P, 2, 1024], 48 * KB)

        ident = at("ident", [P, P], M)
        ident_r = at("ident_r", [P, P], M + 512, F32R)
        causal = at("causal", [P, P], M + 1024)
        causal_t = at("causal_t", [P, P], M + 1536)
        ones = at("ones", [P, P], M + 2048)
        SPARE = M + 2560
        cols = at("cols", [P, 304], SPARE + 4224)
        used = [0]

        def col(n):
            c = used[0]
            used[0] += n
            assert used[0] <= 304
            return cols[:, c:c + n]

        q_gain, kv_gain = col(2), col(1)
        conv_w, conv_b = col(32).rearrange("p (c j) -> p c j", j=CONV), col(8)
        inv_freq, sin_sign = col(1), col(1)
        gate_bias = col(2)
        pool_gain = col(16)
        inv_count = col(HALO)
        stat_a, stat_b, stat_c = col(8), col(8), col(8)
        stat_d, stat_e, stat_f = col(8), col(8), col(8)
        head_gain, token = col(1), col(1)
        u_col, floor_col, m_prev = col(8), col(8), col(8)
        neg_max, row_sum, row_inv = col(8), col(8), col(8)
        den, den_inv, var8, sd8, rs8, h_scale = col(8), col(8), col(8), col(8), col(8), col(8)
        bn = col(12).rearrange("p (c j) -> p c j", j=6)
        mv2 = col(2)

        x_nat = at("x_nat", [P, TB, D], C)
        pre_gain = at("pre_gain", [P, D], E)
        junk0 = at("junk0", [P, D], B + 16 * KB)
        u_hi = at("u_hi", [P, KD, S], A, F32R)
        u_lo = at("u_lo", [P, KD, S], A + 32 * KB, F32R)
        pos_i = at("pos_i", [P, S], E + 4 * KB, I32)
        ang = at("ang", [P, S], E + 8 * KB)
        turns = at("turns", [P, S], E + 12 * KB)
        rot = at("rot", [P, S], SPARE)
        c_q = at("c_q", [P, 2, S], S2)
        c_kv = at("c_kv", [P, S], S2 + 8 * KB)
        k_pe = at("k_pe", [P, S], S2 + 12 * KB)
        raw = at("raw", [P, 2, S + CONV - 1], B)
        sd_q = at("sd_q", [P, S], B + 8448)
        sd_kv = at("sd_kv", [P, S], B + 16 * KB)
        k_tmp = at("k_tmp", [P, S], B + 16 * KB)
        i_row = at("i_row", [HEADS, S], B + 20 * KB)
        f_row = at("f_row", [HEADS, S], B + 24 * KB)
        b_row = at("b_row", [HEADS, S], B + 28 * KB)
        e_row = at("e_row", [HEADS, S], E + 8 * KB)
        m_row = at("m_row", [HEADS, S], E + 12 * KB)
        sq = at("sq", [P, 2, S], E)
        m_qk = at("m_qk", [P, 8, S], C)
        m_v = at("m_v", [P, HEADS, S], E)
        mix = at("mix", [P, 8, S], B)
        wq_h = at("wq_h", [P, 2, NOPE + ROPE], B + 12544)
        wkv_h = at("wkv_h", [P, NOPE + VH], B + 14080)
        q_n = at("q_n", [P, S], A)
        q_pe = at("q_pe", [P, S], A + 4 * KB)
        k_n = at("k_n", [P, S], A + 8 * KB)
        v_n = at("v_n", [P, TB, P], A + 12 * KB)
        probs = at("probs", [P, 2, S], A + 16 * KB)
        probs_t = at("probs_t", [P, TB, P], A + 24 * KB)
        mq_h = at("mq_h", [P, S], A + 28 * KB)
        mk_h = at("mk_h", [P, S], A + 32 * KB)
        mv_h = at("mv_h", [P, S], A + 36 * KB)
        r_b = at("r_b", [P, S], A + 40 * KB)
        h_nat = at("h_nat", [P, TB, P + 1], A + 44 * KB)
        O1 = A + 49 * KB
        vo = at("vo", [P, 2, P + 1], O1)
        state = at("state", [P, P + 1], O1 + 1056)
        e_buf = at("e_buf", [P, 2, P], O1 + 2 * KB)
        d_t = at("d_t", [P, 2, P], O1 + 3 * KB)
        inter = at("inter", [P, 2, P], O1 + 4 * KB)
        s_t = at("s_t", [P, 2, P], O1 + 5 * KB)
        q_in = at("q_in", [P, 2, P], O1 + 6 * KB)
        k_w = at("k_w", [P, 2, P], O1 + 7 * KB)
        mix_hi = [at(f"mix_hi{b}", [P, 8, P], E + 8 * KB * b, F32R) for b in range(2)]
        mix_lo = [at(f"mix_lo{b}", [P, 8, P], E + 8 * KB * b + 4 * KB, F32R) for b in range(2)]
        x_blk = at("x_blk", [P, D], C + 16 * KB)
        h1_blk = at("h1_blk", [P, D], C + 20 * KB)
        f_blk = at("f_blk", [P, D], C + 24 * KB)
        ffn_gain = at("ffn_gain", [P, D], C + 28 * KB)
        post_gain = at("post_gain", [P, D], SPARE)
        f_hi = at("f_hi", [P, KD, S], A, F32R)
        f_lo = at("f_lo", [P, KD, S], A + 32 * KB, F32R)
        y = at("y", [P, TB, D], B)
        silu_g = at("silu_g", [P, 4, HALF], C)
        hid = at("hid", [P, 2, HALF], C + 8 * KB)
        hid_hi = at("hid_hi", [P, 2, S], E, F32R)
        hid_lo = at("hid_lo", [P, 2, S], E + 8 * KB, F32R)
        p_nat = at("p_nat", [P, TB, PLE], A)
        p_hi = at("p_hi", [P, 2, S], A + 8 * KB, F32R)
        p_lo = at("p_lo", [P, 2, S], A + 16 * KB, F32R)
        junk2 = at("junk2", [P, D], S2)
        h1_in = [at(f"h1_in{b}", [P, D], S2 + 4 * KB * (1 + b)) for b in range(3)]
        ffn_post_gain = at("ffn_post_gain", [P, D], SPARE)
        pp = at("pp", [P, KD, S], C)
        h2_hi = at("h2_hi", [P, KD, S], A, F32R)
        h2_lo = at("h2_lo", [P, KD, S], A + 32 * KB, F32R)
        sig = at("sig", [P, 2, HALF], S2)
        x3 = at("x3", [P, 2, HALF], S2 + 4 * KB)
        x3_hi = at("x3_hi", [P, KD, S], C, F32R)
        x3_lo = at("x3_lo", [P, KD, S], B, F32R)
        y2 = at("y2", [P, TB, D], A)
        m_hi = at("m_hi", [P, 4, S], A + 32 * KB, F32R)
        m_lo = at("m_lo", [P, 4, S], A + 48 * KB, F32R)
        z = at("z", [P, 4, S], E)
        g_hi = at("g_hi", [P, 4, S], E, F32R)
        g_lo0 = at("g_lo0", [P, 4, HALF], S2, F32R)
        W1 = HALO + HALF
        u_buf = at("u_buf", [P, 2, W1], SPARE)
        win = at("win", [P, 2, W1], S2 + 8 * KB)
        gt = at("gt", [P, HALF], S2 + 8 * KB + 4352)
        ln_gain = at("ln_gain", [P, D], C)
        ln_bias = at("ln_bias", [P, D], C + 4 * KB)

        ps = ctx.enter_context(nc.psum_tensor("ps", [P, 8, HALF], F32))
        psf = ps[:].rearrange("p b n -> p (b n)")

        gate_dram = nc.dram_tensor("gate_rows", [4, HEADS, S], F32, kind="Internal").ap()
        h1_dram = nc.dram_tensor("h1_rows", [S, D], F32, kind="Internal").ap()

        staged = [sem("staged0"), sem("staged1")]
        parted = [sem("parted0"), sem("parted1")]
        pool_hi = Chain(sem("pool_hi"))
        consts = sem("consts")
        cols_in = sem("cols_in")
        pre_gain_in = sem("pre_gain_in")
        pos_in = sem("pos_in")
        x_in = [sem(f"x_in{t}") for t in range(TB)]
        x_sd, xn_ready, ut_full, u_hi_ready, u_split = map(sem, (
            "x_sd", "xn_ready", "ut_full", "u_hi_ready", "u_split"))
        in_full, in_taken = sem("in_full"), sem("in_taken")
        sq_ready, gates_abs, gates_log, gates_rows, gates_spilled = map(sem, (
            "sq_ready", "gates_abs", "gates_log", "gates_rows", "gates_spilled"))
        kpe_prod, kpe_shift, kpe_sum = map(sem, ("kpe_prod", "kpe_shift", "kpe_sum"))
        rot_ang, rot_sin = sem("rot_ang"), sem("rot_sin")
        conv_done, silu_done, latent_ready = map(sem, ("conv_done", "silu_done", "latent_ready"))
        head_w, head_g = sem("head_w"), sem("head_g")
        act_head, dve_head = sem("act_head"), sem("dve_head")
        up_full, up_taken, qp_ready, mqkv_ready = map(sem, (
            "up_full", "up_taken", "qp_ready", "mqkv_ready"))
        s_full, nm_ready, probs_done, p_ready = map(sem, (
            "s_full", "nm_ready", "probs_done", "p_ready"))
        pt_full, pt_taken, o_full, o_taken = map(sem, ("pt_full", "pt_taken", "o_full", "o_taken"))
        st_full, kv_full, e_ready, dt_ready, ib_ready, st_ready, kv_nat = map(sem, (
            "st_full", "kv_full", "e_ready", "dt_ready", "ib_ready", "st_ready", "kv_nat"))
        num_full, num_taken, cn_full, cn_done = map(sem, (
            "num_full", "num_taken", "cn_full", "cn_done"))
        hvar_ready, hs_ready, ht_full = map(sem, ("hvar_ready", "hs_ready", "ht_full"))
        msplit_ready, mix_full, mix_taken = map(sem, ("msplit_ready", "mix_full", "mix_taken"))
        gains_in, xblk_in, h1_ready, h1_spilled = map(sem, (
            "gains_in", "xblk_in", "h1_ready", "h1_spilled"))
        sd1_ready, sd2_ready, f_ready, ft_full, f_hi_ready, f_split = map(sem, (
            "sd1_ready", "sd2_ready", "f_ready", "ft_full", "f_hi_ready", "f_split"))
        gate_full, up2_full, down_full, silu_ready, hid_ready, hid_hi_ready, hid_split, y_added = map(sem, (
            "gate_full", "ffn_up_full", "down_full", "silu_ready", "hid_ready", "hid_hi_ready",
            "hid_split", "y_added"))
        p_in, pt2_full, p_hi_ready, p_split, pp_full, pp_taken = map(sem, (
            "p_in", "ple_t_full", "p_hi_ready", "p_split", "pp_full", "pp_taken"))
        fpg_in = sem("fpg_in")
        h1_back = [sem(f"h1_back{b}") for b in range(3)]
        h2_sd, h2_ready, h2t_full, h2_hi_ready, h2_split = map(sem, (
            "h2_sd", "h2_ready", "h2t_full", "h2_hi_ready", "h2_split"))
        pg_full, sig_ready, x3_ready, x3_hi_ready, x3_split = map(sem, (
            "pg_full", "sig_ready", "x3_ready", "x3_hi_ready", "x3_split"))
        out_full, y2_added = sem("out_full"), sem("y2_added")
        pu_full, pu_taken, pm_ready, pm_hi_ready, pm_split = map(sem, (
            "pu_full", "pu_taken", "pm_ready", "pm_hi_ready", "pm_split"))
        z_full, z_taken, grp_full, gt_ready, g_hi_ready, g_split = map(sem, (
            "z_full", "z_taken", "grp_full", "gt_ready", "g_hi_ready", "g_split"))
        ln_in, ln_var, ln_sd, out_ready, out_stored = map(sem, (
            "ln_in", "ln_var", "ln_sd", "out_ready", "out_stored"))
        dve_own = Chain(sem("dve_own"))
        act_own = Chain(sem("act_own"))

        T_OUT, T_FFN, T_PLE, T_PG, T_POOL = 10, 14, 47, 48, 52

        def k_rows(w):
            return w.rearrange("(k p) n -> p k n", p=P)

        w_in, w_out, w_gate, w_up, w_down = a["w_in"][0], a["w_out"][0], a["w_gate"][0], a["w_up"][0], a["w_down"][0]
        w_pp, w_pg = a["w_ple_proj"][0], a["w_ple_gate"][0]
        pw_in, pw_grp, pw_out = a["pool_w_in_2"][0], a["pool_w_grp_2"][0], a["pool_w_out_2"][0]

        def half_cols(w, h, c0):
            return k_rows(w)[:, 4 * h:4 * h + 4, bass.ds(c0, 256)]

        def half_rows(w, h, r0):
            return w[bass.ds(r0 + P * h, P), :]

        def wcols(s, k, m):
            c = k * 256 + m * P
            return w_hi[s][:, c:c + P], w_lo[s][:, c:c + P]

        def sp_program(sp):
            def load(t, sources):
                for h in range(2):
                    if not (isinstance(t, int) and t == 0):
                        sp.wait_ge(parted[h], t)
                    src, view = sources(h)
                    sp.dma_start(view, src).then_inc(staged[h], 16)

            def cols_tile(w, c0):
                return lambda h: (half_cols(w, h, c0), stage[:, h, :].rearrange("p (k n) -> p k n", k=4))

            def rows_tile(w, r0):
                return lambda h: (half_rows(w, h, r0), stage[:, h, :])

            for t in range(TB):
                sp.dma_start(x_nat[:, t, :], a["x"][0, t * P:(t + 1) * P, :]).then_inc(x_in[t], 16)
            load(0, cols_tile(w_in, 0))
            for h in range(2):
                sp.wait_ge(parted[h], 1)
                view = stage[:, h, :].rearrange("p (k n) -> p k n", k=4)
                rows = k_rows(w_in)[:, 4 * h:4 * h + 4, :]
                sp.dma_start(view[:, :, 0:192], rows[:, :, 256:448]).then_inc(staged[h], 16)
                sp.dma_start(view[:, :, 192:196], rows[:, :, 2496:2500]).then_inc(staged[h], 16)
                sp.dma_start(view[:, :, 224:228], rows[:, :, 2500:2504]).then_inc(staged[h], 16)
            with sp.Fori(1, 5, 1) as i:
                for e in range(2):
                    load(2 * i + e, cols_tile(w_in, 512 * i - 64 + 256 * e))
            load(T_OUT, rows_tile(w_out, 0))

            def head_weights(h):
                wq = a["w_uq"][0].rearrange("(k p) n -> p k n", p=P)
                sp.dma_start(wq_h[:], wq[:, :, bass.ds(h * (NOPE + ROPE), NOPE + ROPE)]).then_inc(head_w, 16)
                sp.dma_start(wkv_h[:], a["w_ukv"][0][:, bass.ds(h * (NOPE + VH), NOPE + VH)]).then_inc(head_w, 16)

            def head_gates(h):
                r0, u0, e0, m0 = (gate_dram[j] for j in range(4))
                sp.dma_start(r_b[:], r0[bass.ds(h, 1), :].rearrange("a t -> (a t)").partition_broadcast(P)).then_inc(head_g, 16)
                sp.dma_start(u_col, u0[bass.ds(h, 1), :].rearrange("a (c p) -> p (a c)", p=P), **SMALL).then_inc(head_g, 16)
                sp.dma_start(floor_col, e0[bass.ds(h, 1), :].rearrange("a (c p) -> p (a c)", p=P), **SMALL).then_inc(head_g, 16)
                last = m0[bass.ds(h, 1), :].rearrange("a (c p) -> (a c) p", p=P)[0:TB - 1, P - 1]
                sp.dma_start(m_prev[:, 1:TB], last.partition_broadcast(P), **SMALL).then_inc(head_g, 16)
                gain = a["mlstm_norm"][0].rearrange("(h p) -> p h", p=P)
                sp.dma_start(head_gain, gain[:, bass.ds(h, 1)], **SMALL).then_inc(head_g, 16)

            sp.wait_ge(in_taken, 24)
            head_weights(0)
            load(T_OUT + 1, rows_tile(w_out, 256))
            sp.wait_ge(gates_spilled, 64)
            sp.wait_ge(in_full, 44)
            head_gates(0)
            load(T_OUT + 2, rows_tile(w_out, 512))
            with sp.Fori(0, HEADS - 1, 1) as h:
                sp.wait_ge(up_full, 8 * h + 8)
                head_weights(h + 1)
                sp.wait_ge(dve_head, h + 2)
                sp.wait_ge(act_head, h + 2)
                head_gates(h + 1)

            sp.wait_ge(dve_head, HEADS + 1)
            sp.wait_ge(act_head, HEADS + 1)
            sp.dma_start(post_gain[:], a["attn_post_norm"][0].partition_broadcast(P)).then_inc(gains_in, 16)
            sp.dma_start(ffn_gain[:], a["ffn_pre_norm"][0].partition_broadcast(P)).then_inc(gains_in, 16)
            sp.dma_start(x_blk[:], a["x"][0, 0:P, :]).then_inc(xblk_in, 16)
            load(T_OUT + 3, rows_tile(w_out, 768))
            for t in range(TB):
                sp.wait_ge(h1_ready, t + 1)
                sp.dma_start(h1_dram[t * P:(t + 1) * P, :], h1_blk[:]).then_inc(h1_spilled, 16)
                if t + 1 < TB:
                    sp.dma_start(x_blk[:], a["x"][0, (t + 1) * P:(t + 2) * P, :]).then_inc(xblk_in, 16)
                if t == 1:
                    load(T_FFN, cols_tile(w_gate, 0))
            sp.wait_ge(f_ready, TB)
            sp.dma_start(ffn_post_gain[:], a["ffn_post_norm"][0].partition_broadcast(P)).then_inc(fpg_in, 16)
            with sp.Fori(0, FG - 1, 1) as g:
                load(T_FFN + 3 * g + 1, cols_tile(w_up, 256 * g))
                load(T_FFN + 3 * g + 2, rows_tile(w_down, 256 * g))
                load(T_FFN + 3 * g + 3, cols_tile(w_gate, 256 * g + 256))
            load(T_PLE - 2, cols_tile(w_up, 256 * (FG - 1)))
            load(T_PLE - 1, rows_tile(w_down, 256 * (FG - 1)))
            load(T_PLE, rows_tile(w_pp, 0))
            sp.wait_ge(up2_full, 4 * FG)
            sp.dma_start(p_nat[:], a["p"][0, 0].rearrange("(t p) c -> p t c", p=P)).then_inc(p_in, 16)
            load(T_PG, cols_tile(w_pg, 0))
            sp.wait_ge(down_full, 16 * FG)
            sp.wait_ge(h1_spilled, 16 * TB)
            for t in range(TB):
                if t >= 3:
                    sp.wait_ge(h2_ready, t - 2)
                sp.dma_start(h1_in[t % 3][:], h1_dram[t * P:(t + 1) * P, :]).then_inc(h1_back[t % 3], 16)
            for j in range(1, 4):
                load(T_PG + j, cols_tile(w_pg, 256 * j))
            with sp.Fori(0, 2, 1) as i:
                for e in range(2):
                    t0, c0 = T_POOL + 14 * i + 7 * e, 1024 * i + GW * e
                    load(t0, cols_tile(pw_in, c0))
                    load(t0 + 1, cols_tile(pw_in, c0 + 256))
                    load(t0 + 2, cols_tile(pw_in, c0 + DP))
                    load(t0 + 3, cols_tile(pw_in, c0 + DP + 256))
                    grp = pw_grp.rearrange("g c d -> (g c) d")
                    load(t0 + 4, lambda h: (
                        grp[bass.ds(c0 + 256 * h, 256), :].rearrange("(k p) n -> p k n", p=P),
                        stage[:, h, :].rearrange("p (k n) -> p k n", k=2)))
                    load(t0 + 5, rows_tile(pw_out, c0))
                    load(t0 + 6, rows_tile(pw_out, c0 + 256))
            sp.wait_ge(z_full, 32)
            sp.dma_start(ln_gain[:], a["ln_g_2"][0].partition_broadcast(P)).then_inc(ln_in, 16)
            sp.dma_start(ln_bias[:], a["ln_b_2"][0].partition_broadcast(P)).then_inc(ln_in, 16)
            for t in range(TB):
                sp.wait_ge(out_ready, t + 1)
                sp.dma_start(out[0, t * P:(t + 1) * P, :], y2[:, t, :]).then_inc(out_stored, 16)
            sp.wait_ge(out_stored, 16 * TB)

        def pool_program(pool):
            g = nc.gpsimd
            own = Chain(consts)
            g.memset(ones[:], 1.0).then_inc(consts, 1)
            own.at = 1
            own.do(pool, g.memset(ident[:], 0.0))
            own.do(pool, g.memset(causal[:], 0.0))
            own.do(pool, g.memset(causal_t[:], 0.0))
            own.do(pool, g.affine_select(out=ident[:], in_=ident[:], compare_op=ALU.not_equal, fill=1.0,
                                         base=0, pattern=[[-1, P]], channel_multiplier=1))
            own.mark(g.affine_select(out=causal[:], in_=causal[:], compare_op=ALU.is_ge, fill=NEG,
                                     base=0, pattern=[[-1, P]], channel_multiplier=1))
            own.mark(g.affine_select(out=causal_t[:], in_=causal_t[:], compare_op=ALU.is_ge, fill=NEG,
                                     base=0, pattern=[[1, P]], channel_multiplier=-1))
            own.mark(g.tensor_copy(ident_r[:], ident[:]))
            own.mark(g.memset(sin_sign[0:96, :], -1.0))
            own.wait(pool)
            own.do(pool, g.memset(sin_sign[96:P, :], 1.0))
            own.mark(g.memset(m_prev[:, 0:1], 0.0))
            for t in range(HALO):
                own.mark(g.memset(inv_count[:, t:t + 1], 1.0 / (t + 1)))
            assert own.at == N_CONSTS

            def part(t, slot, staged_at):
                for h in range(2):
                    pool.wait_ge(staged[h], staged_at)
                    g.tensor_tensor(token, ones[:, 0:1], ones[:, 0:1], ALU.mult)
                    hi, lo = w_hi[slot][:, 1024 * h:1024 * h + 1024], w_lo[slot][:, 1024 * h:1024 * h + 1024]
                    pool_hi.do(pool, g.tensor_scalar(hi, stage[:, h, :], 1.0, 0.0, ALU.mult, ALU.add))
                    g.tensor_tensor(lo, stage[:, h, :], hi.bitcast(F32), ALU.subtract).then_inc(parted[h], 1)

            def landed(t):
                return 16 * t + 48

            part(0, 0, 16)
            part(1, 1, 64)
            start = pool_hi.at
            with pool.Fori(1, 4, 1) as i:
                pool_hi.at = start + 4 * (i - 1)
                for e in range(2):
                    pool.wait_ge(in_full, 8 * i + 4 * e - 4)
                    part(2 * i + e, e, landed(2 * i + e))
            pool_hi.at = start + 12
            for t in (8, 9, 10, 11):
                pool.wait_ge(in_full, 4 * t)
                part(t, t % 2, landed(t))
            pool.wait_ge(ht_full, 2 * HEADS)
            part(12, 2, landed(12))
            part(13, 3, landed(13))
            pool.wait_ge(mix_full, 2 * TB)
            for j in range(3):
                part(T_FFN + j, j, landed(T_FFN + j))
            start = pool_hi.at
            with pool.Fori(1, FG, 1) as i:
                pool_hi.at = start + 6 * (i - 1)
                pool.wait_ge(gate_full, 4 * i)
                part(T_FFN + 3 * i, 0, landed(T_FFN + 3 * i))
                pool.wait_ge(up2_full, 4 * i)
                part(T_FFN + 3 * i + 1, 1, landed(T_FFN + 3 * i + 1))
                pool.wait_ge(down_full, 16 * i)
                part(T_FFN + 3 * i + 2, 2, landed(T_FFN + 3 * i + 2))
            pool_hi.at = start + 6 * (FG - 1)
            pool.wait_ge(gate_full, 4 * FG)
            part(T_PLE, 0, landed(T_PLE))
            pool.wait_ge(up2_full, 4 * FG)
            part(T_PG, 1, landed(T_PG))
            pool.wait_ge(pp_full, 16)
            part(T_PG + 1, 0, landed(T_PG + 1))
            pool.wait_ge(pg_full, 4)
            part(T_PG + 2, 1, landed(T_PG + 2))
            pool.wait_ge(pg_full, 8)
            part(T_PG + 3, 0, landed(T_PG + 3))
            start = pool_hi.at
            with pool.Fori(0, 2, 1) as i:
                pool_hi.at = start + 28 * i
                for e in range(2):
                    before = [(out_full, 64 * i + 32 * e + 1), (out_full, 64 * i + 32 * e + 16),
                              (pu_full, 16 * i + 8 * e + 4), (pu_full, 16 * i + 8 * e + 8),
                              (z_full, 16 * i + 8 * e + 4), (z_full, 16 * i + 8 * e + 8),
                              (grp_full, 16 * i + 8 * e + 8)]
                    for j, (s, n) in enumerate(before):
                        pool.wait_ge(s, n)
                        t = T_POOL + 14 * i + 7 * e + j
                        part(t, (1 + 7 * e + j) % 2, landed(t))

        def pe_program(pe):
            mm, tr = nc.tensor.matmul, nc.tensor.transpose

            def tile_ready(t):
                pe.wait_ge(parted[0], t + 1)
                pe.wait_ge(parted[1], t + 1)

            def three(out_ap, terms):
                n = 3 * len(terms)
                j = 0
                for lh, ll, rh, rl in terms:
                    for l, r in ((lh, rh), (lh, rl), (ll, rh)):
                        last = mm(out_ap, l, r, start=(j == 0), stop=(j == n - 1))
                        j += 1
                return last

            def proj_t(bank, s, m, n, x_h, x_l):
                ts = slice(n * HALF, n * HALF + HALF)
                return three(ps[:, bank, :], [(*wcols(s, k, m), x_h[:, k, ts], x_l[:, k, ts]) for k in range(KD)])

            pe.wait_ge(consts, N_CONSTS)
            for t in range(TB):
                pe.wait_ge(xn_ready, t + 1)
                if t >= 4:
                    pe.wait_ge(u_split, 2 * (t - 4) + 2)
                for k in range(KD):
                    b, c = 2 * (t % 4) + k // 4, (k % 4) * P
                    last = tr(ps[:, b, c:c + P], x_nat[:, t, k * P:(k + 1) * P], ident[:])
                    if k % 4 == 3:
                        last.then_inc(ut_full, 1)

            def in_tile(t, s, q0, bank0, first=False):
                tile_ready(t)
                for m in range(2):
                    for n in range(2):
                        j = 2 * m + n
                        if not first:
                            pe.wait_ge(in_taken, q0 + j - 7)
                        proj_t(bank0 + j, s, m, n, u_hi, u_lo).then_inc(in_full, 1)

            pe.wait_ge(u_split, 2 * TB)
            in_tile(0, 0, 0, 0, first=True)
            in_tile(1, 1, 4, 4, first=True)
            with pe.Fori(1, 3, 1) as i:
                in_tile(2 * i, 0, 8 * i, 0)
                in_tile(2 * i + 1, 1, 8 * i + 4, 4)
            pe.wait_ge(sq_ready, 2)
            for j in range(4):
                pe.wait_ge(in_taken, 24 + j - 7)
                mm(ps[:, j, :], ones[:], sq[:, j // 2, (j % 2) * HALF:(j % 2 + 1) * HALF],
                   start=True, stop=True).then_inc(in_full, 1)
            with pe.Fori(3, 5, 1) as i:
                in_tile(2 * i, 0, 8 * i + 4, 4)
                in_tile(2 * i + 1, 1, 8 * i + 8, 0)

            pe.wait_ge(in_taken, 44)
            pe.wait_ge(latent_ready, 1)
            with pe.Fori(0, HEADS, 1) as h:
                n8 = 8 * h
                pe.wait_ge(head_w, 32 * h + 32)
                pe.wait_ge(act_head, h + 1)
                pe.wait_ge(dve_head, h + 1)
                for j in range(4):
                    n, rope = j % 2, j // 2
                    rows = ROPE if rope else P
                    for k in range(2):
                        last = mm(ps[0:rows, j, :], wq_h[:, k, rope * NOPE:rope * NOPE + rows],
                                  c_q[:, k, n * HALF:(n + 1) * HALF], start=(k == 0), stop=(k == 1))
                    last.then_inc(up_full, 1)
                for n in range(2):
                    mm(ps[:, 4 + n, :], wkv_h[:, 0:NOPE], c_kv[:, n * HALF:(n + 1) * HALF],
                       start=True, stop=True).then_inc(up_full, 1)
                for t in range(TB):
                    last = mm(ps[:, 6 + t // 4, (t % 4) * P:(t % 4 + 1) * P], c_kv[:, t * P:(t + 1) * P],
                              wkv_h[:, NOPE:NOPE + VH], start=True, stop=True)
                    if t % 4 == 3:
                        last.then_inc(up_full, 1)

                def probs_transposed(i):
                    pe.wait_ge(p_ready, n8 + i + 1)
                    if i >= 1:
                        pe.wait_ge(pt_taken, n8 + i)
                    for j in range(i + 1):
                        last = tr(psf[:, 1024 + j * P:1024 + (j + 1) * P],
                                  probs[:, i % 2, j * P:(j + 1) * P], ident[:])
                    last.then_inc(pt_full, 1)

                def values(i):
                    pe.wait_ge(pt_taken, n8 + i + 1)
                    if i >= 1:
                        pe.wait_ge(o_taken, n8 + i)
                    for j in range(i + 1):
                        last = mm(ps[:, 4, 0:P], v_n[:, j, :], probs_t[:, j, :], start=(j == 0), stop=(j == i))
                    last.then_inc(o_full, 1)

                for i in range(TB):
                    blk = slice(i * P, (i + 1) * P)
                    if i >= 1:
                        probs_transposed(i - 1)
                    if i == 0:
                        pe.wait_ge(up_taken, 6 * h + 6)
                        pe.wait_ge(qp_ready, h + 1)
                    else:
                        pe.wait_ge(probs_done, n8 + i)
                    for c0 in range(0, (i + 1) * P, HALF):
                        c1 = min(c0 + HALF, (i + 1) * P)
                        mm(psf[:, c0:c1], q_n[:, blk], k_n[:, c0:c1], start=True, stop=False)
                        last = mm(psf[:, c0:c1], q_pe[:, blk], k_pe[:, c0:c1], start=False, stop=True)
                    last.then_inc(s_full, 1)
                    if i == 0:
                        pe.wait_ge(mqkv_ready, 3 * h + 3)
                    else:
                        pe.wait_ge(cn_done, n8 + i)
                        pe.wait_ge(kv_nat, 2 * n8 + 2 * i)
                    mm(ps[:, 5, 0:P], mk_h[:, blk], mq_h[:, blk], start=True, stop=True).then_inc(st_full, 1)
                    tr(ps[:, 6, 0:P], mk_h[:, blk], ident[:])
                    tr(ps[:, 6, P:2 * P], mv_h[:, blk], ident[:]).then_inc(kv_full, 1)
                    if i >= 1:
                        values(i - 1)
                    pe.wait_ge(st_ready, n8 + i + 1)
                    pe.wait_ge(kv_nat, 2 * n8 + 2 * i + 2)
                    if i >= 1:
                        pe.wait_ge(num_taken, n8 + i)
                    last = mm(ps[:, 7, 0:P + 1], s_t[:, i % 2, :], vo[:, i % 2, :], start=True, stop=(i == 0))
                    if i >= 1:
                        last = mm(ps[:, 7, 0:P + 1], q_in[:, i % 2, :], state[:], start=False, stop=True)
                    last.then_inc(num_full, 1)
                    mm(ps[:, 5, 0:P + 1], k_w[:, i % 2, :], vo[:, i % 2, :], start=True, stop=True).then_inc(cn_full, 1)
                probs_transposed(TB - 1)
                values(TB - 1)
                pe.wait_ge(hs_ready, h + 1)
                pe.wait_ge(pt_taken, n8 + 8)
                for t in range(TB):
                    last = tr(ps[:, 2 + t // 4, (t % 4) * P:(t % 4 + 1) * P], h_nat[:, t, 0:P], ident[:])
                    if t % 4 == 3:
                        last.then_inc(ht_full, 1)

            pe.wait_ge(dve_head, HEADS + 1)
            pe.wait_ge(act_head, HEADS + 1)

            def f_transposed(t):
                pe.wait_ge(f_ready, t + 1)
                if t >= 2:
                    pe.wait_ge(f_split, 2 * t - 2)
                for k in range(KD):
                    b = 4 + 2 * (t % 2) + k // 4
                    last = tr(ps[:, b, (k % 4) * P:(k % 4 + 1) * P], f_blk[:, k * P:(k + 1) * P], ident[:])
                    if k % 4 == 3:
                        last.then_inc(ft_full, 1)

            for t in range(TB):
                pe.wait_ge(msplit_ready, t + 1)
                if t >= 2:
                    pe.wait_ge(mix_taken, t - 1)
                for n in range(2):
                    terms = []
                    for k in range(8):
                        c = (k % 2) * 1024 + n * HALF
                        terms.append((mix_hi[t % 2][:, k, :], mix_lo[t % 2][:, k, :],
                                      w_hi[k // 2][:, c:c + HALF], w_lo[k // 2][:, c:c + HALF]))
                    if t == 0 and n == 0:
                        tile_ready(T_OUT + 3)
                    three(ps[:, 2 * (t % 2) + n, :], terms).then_inc(mix_full, 1)
                if t >= 1:
                    f_transposed(t - 1)
            f_transposed(TB - 1)

            pe.wait_ge(mix_taken, TB)
            pe.wait_ge(f_split, 2 * TB)
            with pe.Fori(0, FG, 1) as g:
                tile_ready(T_FFN + 3 * g)
                for b in range(4):
                    pe.wait_ge(y_added, 16 * g + b + 9)
                    proj_t(b, 0, b % 2, b // 2, f_hi, f_lo).then_inc(gate_full, 1)
                tile_ready(T_FFN + 3 * g + 1)
                for b in range(4):
                    pe.wait_ge(y_added, 16 * g + b + 13)
                    proj_t(4 + b, 1, b % 2, b // 2, f_hi, f_lo).then_inc(up2_full, 1)
                tile_ready(T_FFN + 3 * g + 2)
                for t in range(TB):
                    if t % 4 == 0:
                        pe.wait_ge(hid_split, 4 * g + 2 + t // 2)
                    for n in range(2):
                        j = 2 * t + n
                        if j < 4:
                            pe.wait_ge(silu_ready, 4 * g + j + 1)
                        elif j < 8:
                            pe.wait_ge(hid_split, 4 * g + 4)
                        else:
                            pe.wait_ge(y_added, 16 * g + 16 + j - 7)
                        terms = [(hid_hi[:, k, t * P:(t + 1) * P], hid_lo[:, k, t * P:(t + 1) * P],
                                  w_hi[2][:, k * 1024 + n * HALF:k * 1024 + (n + 1) * HALF],
                                  w_lo[2][:, k * 1024 + n * HALF:k * 1024 + (n + 1) * HALF]) for k in range(2)]
                        three(ps[:, j % 8, :], terms).then_inc(down_full, 1)

            pe.wait_ge(p_in, 16)
            for c in range(2):
                for t in range(TB):
                    b = 2 * c + t // 4
                    if t % 4 == 0:
                        pe.wait_ge(y_added, 16 * FG + 9 + b)
                    last = tr(ps[:, b, (t % 4) * P:(t % 4 + 1) * P], p_nat[:, t, c * P:(c + 1) * P], ident[:])
                    if t % 4 == 3:
                        last.then_inc(pt2_full, 1)
            tile_ready(T_PLE)
            pe.wait_ge(p_split, 4)
            pe.wait_ge(y_added, 16 * FG + 16)
            for m in range(KD):
                for n in range(2):
                    j = 2 * m + n
                    if j >= 8:
                        pe.wait_ge(pp_taken, j - 7)
                    ts = slice(n * HALF, (n + 1) * HALF)
                    terms = [(w_hi[0][:, k * 1024 + m * P:k * 1024 + (m + 1) * P],
                              w_lo[0][:, k * 1024 + m * P:k * 1024 + (m + 1) * P],
                              p_hi[:, k, ts], p_lo[:, k, ts]) for k in range(2)]
                    three(ps[:, j % 8, :], terms).then_inc(pp_full, 1)
            for t in range(TB):
                pe.wait_ge(h2_ready, t + 1)
                if t < 4:
                    pe.wait_ge(pp_taken, 8 + 2 * t + 2)
                else:
                    pe.wait_ge(h2_split, 2 * (t - 4) + 2)
                for k in range(KD):
                    b = 2 * (t % 4) + k // 4
                    last = tr(ps[:, b, (k % 4) * P:(k % 4 + 1) * P], y[:, t, k * P:(k + 1) * P], ident[:])
                    if k % 4 == 3:
                        last.then_inc(h2t_full, 1)
            pe.wait_ge(h2_split, 2 * TB)
            for i in range(4):
                tile_ready(T_PG + i)
                for j in range(4):
                    b = 4 * (i % 2) + j
                    if i >= 2:
                        pe.wait_ge(sig_ready, 4 * (i - 2) + j + 1)
                    proj_t(b, (1 + i) % 2, j % 2, j // 2, h2_hi, h2_lo).then_inc(pg_full, 1)

            pe.wait_ge(sig_ready, 16)
            for t in range(TB):
                if t % 4 == 0:
                    pe.wait_ge(x3_split, 14 + t // 2)
                for n in range(2):
                    j = 2 * t + n
                    if j >= 8:
                        pe.wait_ge(y2_added, j - 7)
                    for k in range(4):
                        ts = slice(t * P, (t + 1) * P)
                        o = ps[:, j % 8, k * P:(k + 1) * P]
                        mm(o, x3_hi[:, 4 * n + k, ts], ident_r[:], start=True, stop=False)
                        last = mm(o, x3_lo[:, 4 * n + k, ts], ident_r[:], start=False, stop=True)
                    last.then_inc(out_full, 1)
            with pe.Fori(0, 2, 1) as i:
                for e in range(2):
                    t0 = T_POOL + 14 * i + 7 * e
                    n8, n32 = 16 * i + 8 * e, 64 * i + 32 * e
                    for j in range(2):
                        tile_ready(t0 + j)
                        for m in range(2):
                            for n in range(2):
                                b = 4 * j + 2 * m + n
                                pe.wait_ge(y2_added, n32 + b + 9)
                                proj_t(b, (1 + e + j) % 2, m, n, x3_hi, x3_lo).then_inc(pu_full, 1)
                    for j in range(2):
                        tile_ready(t0 + 2 + j)
                        for m in range(2):
                            for n in range(2):
                                b = 4 * j + 2 * m + n
                                pe.wait_ge(pu_taken, n8 + b + 1)
                                proj_t(b, (1 + e + j) % 2, m, n, x3_hi, x3_lo).then_inc(z_full, 1)
                    tile_ready(t0 + 4)
                    s = (1 + e) % 2
                    pe.wait_ge(pm_split, n8 + 8)
                    for n in range(2):
                        for m in range(4):
                            b = 4 * n + m
                            pe.wait_ge(z_taken, n8 + b + 1)
                            ts = slice(n * HALF, (n + 1) * HALF)
                            terms = [(w_hi[s][:, k * 512 + m * P:k * 512 + (m + 1) * P],
                                      w_lo[s][:, k * 512 + m * P:k * 512 + (m + 1) * P],
                                      m_hi[:, k, ts], m_lo[:, k, ts]) for k in range(4)]
                            three(ps[:, b, :], terms).then_inc(grp_full, 1)
                    for r in range(2):
                        tile_ready(t0 + 5 + r)
                        s = (e + r) % 2
                        for t in range(TB):
                            if r == 0 and t % 4 == 0:
                                pe.wait_ge(g_split, n8 + 4 + t)
                            for n in range(2):
                                j = 2 * t + n
                                if r == 0 and j < 8:
                                    pe.wait_ge(gt_ready, n8 + j + 1)
                                else:
                                    pe.wait_ge(y2_added, n32 + 16 + 16 * r + j - 7)
                                terms = []
                                for k in range(2):
                                    ts = slice(t * P, (t + 1) * P)
                                    lo = (g_lo0[:, 2 * r + k, ts] if t < 4
                                          else m_lo[:, 2 * r + k, t * P - HALF:(t + 1) * P - HALF])
                                    c = k * 1024 + n * HALF
                                    terms.append((g_hi[:, 2 * r + k, ts], lo,
                                                  w_hi[s][:, c:c + HALF], w_lo[s][:, c:c + HALF]))
                                three(ps[:, j % 8, :], terms).then_inc(out_full, 1)

        def act_program(act):
            f = nc.scalar.activation
            dma = act.dma_start

            def dma_col(dst, src):
                return dma(dst, src, **SMALL)

            dma(pre_gain[:], a["attn_pre_norm"][0].partition_broadcast(P)).then_inc(pre_gain_in, 16)
            dma(pos_i[:], a["positions"][0].partition_broadcast(P)).then_inc(pos_in, 16)
            dma(inv_freq, a["inv_freq"]).then_inc(cols_in, 16)
            dma_col(q_gain, a["q_norm"][0].rearrange("(c p) -> p c", p=P)).then_inc(cols_in, 16)
            dma_col(kv_gain, a["kv_norm"][0].rearrange("(c p) -> p c", p=P)).then_inc(cols_in, 16)
            for j in range(CONV):
                dma_col(conv_w[:, :, j], a["conv_w"][0, j].rearrange("(c p) -> p c", p=P)).then_inc(cols_in, 16)
            dma_col(conv_b, a["conv_b"][0].rearrange("(c p) -> p c", p=P)).then_inc(cols_in, 16)
            dma_col(pool_gain, a["pool_scale_2"][0].rearrange("(c p) -> p c", p=P)).then_inc(cols_in, 16)
            dma_col(gate_bias[0:HEADS, 0:1], a["gate_bias_i"][0].rearrange("(h c) -> h c", c=1)).then_inc(cols_in, 16)
            dma_col(gate_bias[0:HEADS, 1:2], a["gate_bias_f"][0].rearrange("(h c) -> h c", c=1)).then_inc(cols_in, 16)

            def x_norm(t):
                act.wait_ge(x_in[t], 16)
                act_own.do(act, f(junk0[:], x_nat[:, t, :], ACT.Square, accum_out=stat_a[:, t:t + 1]))
                f(stat_b[:, t:t + 1], stat_a[:, t:t + 1], ACT.Sqrt, bias=EPS, scale=1.0 / D).then_inc(x_sd, 1)

            act.wait_ge(consts, N_CONSTS)
            x_norm(0)
            x_norm(1)
            for t in range(TB):
                if t + 2 < TB:
                    x_norm(t + 2)
                for j in range(2):
                    act.wait_ge(ut_full, 2 * t + j + 1)
                    f(u_hi[:, 4 * j:4 * j + 4, t * P:(t + 1) * P],
                      ps[:, 2 * (t % 4) + j, :].rearrange("p (k n) -> p k n", k=4), ACT.Copy).then_inc(u_hi_ready, 1)
            act.wait_ge(rot_ang, 1)
            f(rot[0:64, :], ang[0:64, :], ACT.Sin, scale=0.5).then_inc(rot_sin, 1)
            f(rot[64:P, :], ang[64:P, :], ACT.Sin).then_inc(rot_sin, 1)

            def half(n):
                return slice(n * HALF, (n + 1) * HALF)

            for m in range(2):
                for n in range(2):
                    act.wait_ge(in_full, 2 * m + n + 1)
                    f(c_q[:, m, half(n)], ps[:, 2 * m + n, :], ACT.Copy).then_inc(in_taken, 1)
            for n in range(2):
                act.wait_ge(in_full, 5 + n)
                f(c_kv[:, half(n)], ps[:, 4 + n, :], ACT.Copy).then_inc(in_taken, 1)
            for n in range(2):
                act.wait_ge(in_full, 7 + n)
                b = 6 + n
                f(k_pe[0:64, half(n)], ps[0:64, b, :], ACT.Copy)
                f(k_pe[64:96, half(n)], ps[32:64, b, :], ACT.Copy)
                f(k_pe[96:P, half(n)], ps[0:32, b, :], ACT.Copy)
                f(i_row[:, half(n)], ps[64:64 + HEADS, b, :], ACT.Copy)
                f(f_row[:, half(n)], ps[96:96 + HEADS, b, :], ACT.Copy).then_inc(in_taken, 1)
            act.wait_ge(gates_abs, 1)
            act_own.do(act, f(e_row[:], e_row[:], ACT.Exp, scale=-1.0))
            f(e_row[:], e_row[:], ACT.Ln, bias=1.0).then_inc(gates_log, 1)
            act.wait_ge(kpe_prod, 1)
            f(k_tmp[0:64, :], k_pe[64:P, :], ACT.Copy).then_inc(kpe_shift, 1)

            def raw_rows(c):
                for n in range(2):
                    q = 8 + 2 * c + n
                    act.wait_ge(in_full, q + 1)
                    if c >= 2:
                        act.wait_ge(conv_done, c - 1)
                    f(raw[:, c % 2, CONV - 1 + n * HALF:CONV - 1 + (n + 1) * HALF], ps[:, q % 8, :],
                      ACT.Copy).then_inc(in_taken, 1)

            def silu_rows(c):
                act.wait_ge(conv_done, c + 1)
                f(m_qk[:, c, :], m_qk[:, c, :], ACT.Silu).then_inc(silu_done, 1)

            raw_rows(0)
            raw_rows(1)
            act.wait_ge(gates_rows, 1)
            act_own.do(act, f(e_row[:], m_row[:], ACT.Exp, scale=-1.0))
            for j, row in enumerate((b_row, i_row, e_row, m_row)):
                dma(gate_dram[j], row[:]).then_inc(gates_spilled, 16)
            act.wait_ge(kpe_sum, 1)
            f(k_pe[64:P, :], k_pe[0:64, :], ACT.Copy).then_inc(act_head, 1)
            silu_rows(0)
            for c in range(2, 8):
                raw_rows(c)
                silu_rows(c - 1)
            silu_rows(7)
            for j in range(4):
                act.wait_ge(in_full, 24 + j + 1)
                width = QLORA if j < 2 else KVLORA
                sd = sd_q if j < 2 else sd_kv
                f(sd[:, half(j % 2)], ps[:, j, :], ACT.Sqrt, bias=EPS, scale=1.0 / width).then_inc(in_taken, 1)
            act.wait_ge(gates_spilled, 64)
            for c in range(HEADS):
                for n in range(2):
                    q = 28 + 2 * c + n
                    act.wait_ge(in_full, q + 1)
                    f(m_v[:, c, half(n)], ps[:, q % 8, :], ACT.Copy).then_inc(in_taken, 1)
            act.wait_ge(latent_ready, 1)
            for c in range(HEADS):
                for n in range(2):
                    q = 36 + 2 * c + n
                    act.wait_ge(in_full, q + 1)
                    f(mix[:, 4 + c, half(n)], ps[:, q % 8, :], ACT.Sigmoid).then_inc(in_taken, 1)

            act.wait_ge(in_full, 44)
            act.wait_ge(in_taken, 44)
            with act.Fori(0, HEADS, 1) as h:
                n8 = 8 * h
                act.wait_ge(dve_head, h + 1)
                f(mq_h[:], m_qk[:, bass.ds(h, 1), :], ACT.Copy).then_inc(mqkv_ready, 1)
                f(mk_h[:], m_qk[:, bass.ds(h + 4, 1), :], ACT.Copy, scale=MH_SCALE).then_inc(mqkv_ready, 1)
                f(mv_h[:], m_v[:, bass.ds(h, 1), :], ACT.Copy).then_inc(mqkv_ready, 1)
                for j in (0, 1):
                    act.wait_ge(up_full, n8 + j + 1)
                    f(q_n[:, half(j)], ps[:, j, :], ACT.Copy, scale=QK_SCALE).then_inc(up_taken, 1)
                for j in (0, 1):
                    act.wait_ge(up_full, n8 + j + 5)
                    f(k_n[:, half(j)], ps[:, 4 + j, :], ACT.Copy).then_inc(up_taken, 1)
                for j in (0, 1):
                    act.wait_ge(up_full, n8 + j + 7)
                    f(v_n[:, 4 * j:4 * j + 4, :], ps[:, 6 + j, :].rearrange("p (t n) -> p t n", t=4),
                      ACT.Copy).then_inc(up_taken, 1)

                def take_probs_t(i):
                    act.wait_ge(pt_full, n8 + i + 1)
                    if i >= 1:
                        act.wait_ge(o_full, n8 + i)
                    f(probs_t[:, 0:i + 1, :], psf[:, 1024:1024 + (i + 1) * P].rearrange("p (t n) -> p t n", n=P),
                      ACT.Copy).then_inc(pt_taken, 1)

                def take_out(i):
                    act.wait_ge(o_full, n8 + i + 1)
                    f(mix[:, bass.ds(h, 1), i * P:(i + 1) * P], ps[:, 4, 0:P], ACT.Copy).then_inc(o_taken, 1)

                for i in range(TB):
                    w = i % 2
                    if i >= 1:
                        take_probs_t(i - 1)
                    act.wait_ge(e_ready, n8 + i + 1)
                    if i >= 2:
                        act.wait_ge(cn_done, n8 + i - 1)
                    f(d_t[:, w, :], e_buf[:, w, :], ACT.Exp).then_inc(dt_ready, 1)
                    f(inter[:, w, :], r_b[:, i * P:(i + 1) * P], ACT.Exp, bias=m_prev[:, i:i + 1]).then_inc(ib_ready, 1)
                    act.wait_ge(kv_full, n8 + i + 1)
                    f(vo[:, w, 0:P], ps[:, 6, P:2 * P], ACT.Copy).then_inc(kv_nat, 1)
                    act.wait_ge(dt_ready, n8 + i + 1)
                    f(k_w[:, w, :], ps[:, 6, 0:P], ACT.Copy, scale=d_t[:, w, P - 1:P]).then_inc(kv_nat, 1)
                    act.wait_ge(nm_ready, n8 + i + 1)
                    if i >= 2:
                        act.wait_ge(pt_full, n8 + i - 1)
                    f(probs[:, w, 0:(i + 1) * P], psf[:, 0:(i + 1) * P], ACT.Exp, bias=neg_max[:, i:i + 1],
                      accum_out=row_sum[:, i:i + 1]).then_inc(probs_done, 1)
                    if i >= 1:
                        take_out(i - 1)
                take_probs_t(TB - 1)
                take_out(TB - 1)
                act.wait_ge(hvar_ready, h + 1)
                f(sd8, var8, ACT.Sqrt, bias=EPS, scale=1.0 / P).then_inc(act_head, 1)

            act.wait_ge(dve_head, HEADS + 1)

            def take_f(t):
                for j in range(2):
                    act.wait_ge(ft_full, 2 * t + j + 1)
                    f(f_hi[:, 4 * j:4 * j + 4, t * P:(t + 1) * P],
                      ps[:, 4 + 2 * (t % 2) + j, :].rearrange("p (k n) -> p k n", k=4),
                      ACT.Copy).then_inc(f_hi_ready, 1)

            for t in range(TB):
                b = 2 * (t % 2)
                act.wait_ge(mix_full, 2 * t + 2)
                if t >= 1:
                    act.wait_ge(h1_spilled, 16 * t)
                    act.wait_ge(f_ready, t)
                act_own.do(act, f(h1_blk[:], psf[:, b * HALF:(b + 2) * HALF], ACT.Square,
                                  accum_out=stat_a[:, t:t + 1]))
                f(stat_b[:, t:t + 1], stat_a[:, t:t + 1], ACT.Sqrt, bias=EPS, scale=1.0 / D).then_inc(sd1_ready, 1)
                act.wait_ge(h1_ready, t + 1)
                if t >= 1:
                    act.wait_ge(ft_full, 2 * t)
                act_own.do(act, f(f_blk[:], h1_blk[:], ACT.Square, accum_out=stat_c[:, t:t + 1]))
                f(stat_d[:, t:t + 1], stat_c[:, t:t + 1], ACT.Sqrt, bias=EPS, scale=1.0 / D).then_inc(sd2_ready, 1)
                if t >= 1:
                    take_f(t - 1)
            take_f(TB - 1)

            with act.Fori(0, FG, 1) as g:
                for b in range(4):
                    act.wait_ge(gate_full, 4 * g + b + 1)
                    act.wait_ge(hid_ready, 4 * g + b + 1)
                    f(silu_g[:, b, :], ps[:, b, :], ACT.Silu).then_inc(silu_ready, 1)
                act.wait_ge(y_added, 16 * g + 16)
                for b in range(4):
                    m, n = b % 2, b // 2
                    act.wait_ge(hid_ready, 4 * g + b + 5)
                    f(hid_hi[:, m, half(n)], hid[:, b % 2, :], ACT.Copy).then_inc(hid_hi_ready, 1)

            for j in range(4):
                act.wait_ge(pt2_full, j + 1)
                f(p_hi[:, j // 2, half(j % 2)], ps[:, j, :], ACT.Copy).then_inc(p_hi_ready, 1)

            def h2_norm(t):
                act.wait_ge(y_added, 16 * FG + 2 * t + 2)
                if t == 0:
                    act.wait_ge(down_full, 16 * FG)
                act_own.do(act, f(junk2[:], y[:, t, :], ACT.Square, accum_out=stat_a[:, t:t + 1]))
                f(stat_b[:, t:t + 1], stat_a[:, t:t + 1], ACT.Sqrt, bias=EPS, scale=1.0 / D).then_inc(h2_sd, 1)

            for t in range(TB):
                h2_norm(t)
                for n in range(2):
                    j = 2 * t + n
                    act.wait_ge(pp_full, j + 1)
                    f(pp[:, t, half(n)], ps[:, j % 8, :], ACT.Copy).then_inc(pp_taken, 1)
            for t in range(TB):
                for j in range(2):
                    act.wait_ge(h2t_full, 2 * t + j + 1)
                    f(h2_hi[:, 4 * j:4 * j + 4, t * P:(t + 1) * P],
                      ps[:, 2 * (t % 4) + j, :].rearrange("p (k n) -> p k n", k=4),
                      ACT.Copy).then_inc(h2_hi_ready, 1)
            act.wait_ge(h2_ready, TB)

            def x3_part(j):
                act.wait_ge(x3_ready, j + 1)
                m, n = 2 * (j // 4) + j % 2, (j // 2) % 2
                f(x3_hi[:, m, half(n)], x3[:, j % 2, :], ACT.Copy).then_inc(x3_hi_ready, 1)

            for j in range(16):
                act.wait_ge(pg_full, j + 1)
                if j >= 2:
                    act.wait_ge(x3_ready, j - 1)
                f(sig[:, j % 2, :], ps[:, j % 8, :], ACT.Sigmoid).then_inc(sig_ready, 1)
                if j >= 1:
                    x3_part(j - 1)
            x3_part(15)

            with act.Fori(0, GROUPS, 1) as g:
                n8 = 8 * g
                for j in range(8):
                    n = j % 2
                    act.wait_ge(pu_full, n8 + j + 1)
                    act.wait_ge(pm_ready, n8 + j + 1)
                    f(u_buf[:, n, HALO:W1], ps[:, j, :], ACT.Copy).then_inc(pu_taken, 1)
                    if j >= 1:
                        act.wait_ge(pm_ready, n8 + j + 2)
                        f(m_hi[:, (j - 1) // 2, half((j - 1) % 2)], win[:, 0, HALO:W1], ACT.Copy).then_inc(pm_hi_ready, 1)
                act.wait_ge(pm_ready, n8 + 10)
                f(m_hi[:, 3, half(1)], win[:, 0, HALO:W1], ACT.Copy).then_inc(pm_hi_ready, 1)
                act.wait_ge(out_full, 32 * g + 16)
                for j in range(8):
                    act.wait_ge(z_full, n8 + j + 1)
                    f(z[:, j // 2, half(j % 2)], ps[:, j, :], ACT.Silu).then_inc(z_taken, 1)
                for j in range(8):
                    m, n = j % 4, j // 4
                    act.wait_ge(gt_ready, n8 + j + 1)
                    f(g_hi[:, m, half(n)], gt[:], ACT.Copy).then_inc(g_hi_ready, 1)
            for t in range(TB):
                act.wait_ge(ln_var, t + 1)
                f(stat_b[:, t:t + 1], mv2[:, 1:2], ACT.Sqrt, bias=LN_EPS).then_inc(ln_sd, 1)

        def dve_program(dve):
            v = nc.vector
            own = dve_own

            def half(n):
                return slice(n * HALF, (n + 1) * HALF)

            def x_scale(t):
                dve.wait_ge(x_sd, t + 1)
                own.do(dve, v.reciprocal(stat_c[:, t:t + 1], stat_b[:, t:t + 1]))
                v.scalar_tensor_tensor(x_nat[:, t, :], x_nat[:, t, :], stat_c[:, t:t + 1], pre_gain[:],
                                       ALU.mult, ALU.mult).then_inc(xn_ready, 1)

            dve.wait_ge(pre_gain_in, 16)
            x_scale(0)
            x_scale(1)
            for t in range(TB):
                if t + 2 < TB:
                    x_scale(t + 2)
                for j in range(2):
                    dve.wait_ge(u_hi_ready, 2 * t + j + 1)
                    ts = slice(t * P, (t + 1) * P)
                    v.tensor_tensor(u_lo[:, 4 * j:4 * j + 4, ts],
                                    ps[:, 2 * (t % 4) + j, :].rearrange("p (k n) -> p k n", k=4),
                                    u_hi[:, 4 * j:4 * j + 4, ts].bitcast(F32), ALU.subtract).then_inc(u_split, 1)
            dve.wait_ge(pos_in, 16)
            dve.wait_ge(cols_in, 16 * 11)
            dve.wait_ge(consts, N_CONSTS)
            own.do(dve, v.tensor_copy(ang[:], pos_i[:]))
            own.do(dve, v.tensor_scalar(ang[:], ang[:], inv_freq, None, ALU.mult))
            own.do(dve, v.tensor_scalar(turns[:], ang[:], 1.0 / (2.0 * 3.141592653589793), ROUND, ALU.mult, ALU.add))
            own.do(dve, v.tensor_scalar(turns[:], turns[:], ROUND, None, ALU.subtract))
            for part in (TWO_PI_A, TWO_PI_B, TWO_PI_C):
                own.do(dve, v.scalar_tensor_tensor(ang[:], turns[:], -part, ang[:], ALU.mult, ALU.add))
            v.tensor_scalar(ang[:], ang[:], PI_SAFE, -PI_SAFE, ALU.min, ALU.max).then_inc(rot_ang, 1)
            dve.wait_ge(rot_sin, 2)
            own.do(dve, v.tensor_tensor(rot[0:64, :], rot[0:64, :], rot[0:64, :], ALU.mult))
            own.do(dve, v.tensor_scalar(rot[0:64, :], rot[0:64, :], -2.0, 1.0, ALU.mult, ALU.add))
            own.do(dve, v.tensor_scalar(rot[64:P, :], rot[64:P, :], sin_sign[64:P, :], None, ALU.mult))

            dve.wait_ge(in_taken, 4)
            for m in range(2):
                own.do(dve, v.tensor_tensor(sq[:, m, :], c_q[:, m, :], c_q[:, m, :], ALU.mult))
            own.mark(v.tensor_tensor(sq[:, 0, :], sq[:, 0, :], sq[:, 1, :], ALU.add))
            own.wait(dve)
            v.memset(raw[:, :, 0:CONV - 1], 0.0).then_inc(sq_ready, 1)
            dve.wait_ge(in_taken, 6)
            v.tensor_tensor(sq[:, 1, :], c_kv[:], c_kv[:], ALU.mult).then_inc(sq_ready, 1)
            dve.wait_ge(in_taken, 8)
            own.do(dve, v.tensor_scalar(f_row[:], f_row[:], gate_bias[0:HEADS, 1:2], None, ALU.add))
            v.scalar_tensor_tensor(e_row[:], f_row[:], -1.0, f_row[:], ALU.mult, ALU.max).then_inc(gates_abs, 1)
            own.mark(v.tensor_scalar(i_row[:], i_row[:], gate_bias[0:HEADS, 0:1], None, ALU.add))
            v.tensor_tensor(k_pe[:], k_pe[:], rot[:], ALU.mult).then_inc(kpe_prod, 1)
            dve.wait_ge(gates_log, 1)
            own.do(dve, v.scalar_tensor_tensor(f_row[:], f_row[:], 0.0, e_row[:], ALU.min, ALU.subtract))
            for c in range(TB):
                cs = slice(c * P, (c + 1) * P)
                own.mark(v.tensor_tensor_scan(b_row[:, cs], ones[0:HEADS, :], f_row[:, cs], 0.0, ALU.mult, ALU.add))
            own.do(dve, v.tensor_tensor_scan(m_row[:], f_row[:], i_row[:], 0.0, ALU.add, ALU.max))
            own.do(dve, v.tensor_tensor(i_row[:], i_row[:], b_row[:], ALU.subtract))
            v.tensor_tensor(b_row[:], b_row[:], m_row[:], ALU.subtract).then_inc(gates_rows, 1)
            dve.wait_ge(kpe_shift, 1)
            v.tensor_tensor(k_pe[0:64, :], k_pe[0:64, :], k_tmp[0:64, :], ALU.add).then_inc(kpe_sum, 1)

            for c in range(8):
                dve.wait_ge(in_taken, 8 + 2 * c + 2)
                rows, o = raw[:, c % 2, :], m_qk[:, c, :]
                own.do(dve, v.tensor_scalar(o, rows[:, 0:S], conv_w[:, c, 0:1], conv_b[:, c:c + 1], ALU.mult, ALU.add))
                for j in range(1, CONV):
                    ins = v.scalar_tensor_tensor(o, rows[:, j:j + S], conv_w[:, c, j:j + 1], o, ALU.mult, ALU.add)
                    if j < CONV - 1:
                        own.do(dve, ins)
                    else:
                        ins.then_inc(conv_done, 1)
            dve.wait_ge(in_taken, 26)
            own.do(dve, v.reciprocal(sd_q[:], sd_q[:]))
            for m in range(2):
                own.mark(v.scalar_tensor_tensor(c_q[:, m, :], c_q[:, m, :], q_gain[:, m:m + 1], sd_q[:],
                                                ALU.mult, ALU.mult))
            dve.wait_ge(in_taken, 28)
            own.do(dve, v.reciprocal(sd_kv[:], sd_kv[:]))
            v.scalar_tensor_tensor(c_kv[:], c_kv[:], kv_gain, sd_kv[:], ALU.mult, ALU.mult).then_inc(latent_ready, 1)

            dve.wait_ge(in_full, 44)
            v.memset(vo[:, :, P:P + 1], 1.0).then_inc(dve_head, 1)
            start = own.at
            with dve.Fori(0, HEADS, 1) as h:
                own.at = start + OWN_HEAD * h
                n8 = 8 * h
                for n in range(2):
                    dve.wait_ge(up_full, n8 + 3 + n)
                    own.mark(v.tensor_scalar(q_pe[0:64, half(n)], ps[0:64, 2 + n, :], QK_SCALE, None, ALU.mult))
                    own.mark(v.tensor_scalar(q_pe[64:96, half(n)], ps[32:64, 2 + n, :], QK_SCALE, None, ALU.mult))
                    own.mark(v.tensor_scalar(q_pe[96:P, half(n)], ps[0:32, 2 + n, :], QK_SCALE, None, ALU.mult))
                own.wait(dve)
                v.tensor_tensor(q_pe[:], q_pe[:], rot[:], ALU.mult).then_inc(qp_ready, 1)
                dve.wait_ge(head_g, 80 * h + 80)
                for i in range(TB):
                    w, cs, wide = i % 2, slice(i * P, (i + 1) * P), (i + 1) * P
                    if i >= 2:
                        dve.wait_ge(dt_ready, n8 + i - 1)
                    v.scalar_tensor_tensor(e_buf[:, w, :], r_b[:, cs], u_col[:, i:i + 1], causal_t[:],
                                           ALU.add, ALU.add).then_inc(e_ready, 1)
                    dve.wait_ge(s_full, n8 + i + 1)
                    own.do(dve, v.tensor_tensor(psf[:, i * P:wide], psf[:, i * P:wide], causal[:], ALU.add))
                    v.tensor_reduce(neg_max[:, i:i + 1], psf[:, 0:wide], AX.X, ALU.max, negate=True).then_inc(nm_ready, 1)
                    dve.wait_ge(st_full, n8 + i + 1)
                    dve.wait_ge(dt_ready, n8 + i + 1)
                    if i >= 2:
                        dve.wait_ge(num_full, n8 + i - 1)
                    weigh = v.tensor_tensor(s_t[:, w, :], ps[:, 5, 0:P], d_t[:, w, :], ALU.mult)
                    if i >= 1:
                        own.mark(weigh)
                        dve.wait_ge(ib_ready, n8 + i + 1)
                        weigh = v.tensor_tensor(q_in[:, w, :], mq_h[:, cs], inter[:, w, :], ALU.mult)
                    weigh.then_inc(st_ready, 1)
                    dve.wait_ge(probs_done, n8 + i + 1)
                    own.do(dve, v.reciprocal(row_inv[:, i:i + 1], row_sum[:, i:i + 1]))
                    v.tensor_scalar(probs[:, w, 0:wide], probs[:, w, 0:wide], row_inv[:, i:i + 1], None,
                                    ALU.mult).then_inc(p_ready, 1)
                    dve.wait_ge(num_full, n8 + i + 1)
                    v.tensor_copy(h_nat[:, i, :], ps[:, 7, 0:P + 1]).then_inc(num_taken, 1)
                    dve.wait_ge(cn_full, n8 + i + 1)
                    if i == 0:
                        v.tensor_copy(state[:], ps[:, 5, 0:P + 1]).then_inc(cn_done, 1)
                    else:
                        dve.wait_ge(cn_done, n8 + i)
                        v.scalar_tensor_tensor(state[:], state[:], inter[:, w, P - 1:P], ps[:, 5, 0:P + 1],
                                               ALU.mult, ALU.add).then_inc(cn_done, 1)
                dve.wait_ge(num_taken, n8 + 8)
                own.do(dve, v.scalar_tensor_tensor(den, h_nat[:, :, P], -1.0, h_nat[:, :, P], ALU.mult, ALU.max))
                own.do(dve, v.tensor_tensor(den, den, floor_col, ALU.max))
                own.do(dve, v.reciprocal(den_inv, den))
                dve.wait_ge(pt_full, n8 + 7)
                squares = probs[:, 0, :].rearrange("p (t n) -> p t n", n=P)
                own.do(dve, v.tensor_tensor(squares, h_nat[:, :, 0:P], h_nat[:, :, 0:P], ALU.mult))
                own.do(dve, v.tensor_reduce(var8, squares, AX.X, ALU.add))
                own.do(dve, v.tensor_tensor(var8, var8, den_inv, ALU.mult))
                v.tensor_tensor(var8, var8, den_inv, ALU.mult).then_inc(hvar_ready, 1)
                dve.wait_ge(act_head, h + 2)
                own.do(dve, v.reciprocal(rs8, sd8))
                own.do(dve, v.tensor_tensor(h_scale, rs8, den_inv, ALU.mult))
                scale = h_scale.rearrange("p (t n) -> p t n", n=1).to_broadcast([P, TB, P])
                v.tensor_tensor(h_nat[:, :, 0:P], h_nat[:, :, 0:P], scale, ALU.mult).then_inc(hs_ready, 1)
                for n in range(2):
                    dve.wait_ge(ht_full, 2 * h + n + 1)
                    rows = mix[:, bass.ds(h + 4, 1), half(n)].rearrange("p a n -> p (a n)")
                    ins = v.scalar_tensor_tensor(rows, ps[:, 2 + n, :], head_gain, rows, ALU.mult, ALU.mult)
                    if n == 0:
                        own.mark(ins)
                    else:
                        ins.then_inc(dve_head, 1)
            own.at = start + OWN_HEAD * HEADS

            dve.wait_ge(o_taken, 8 * HEADS)
            dve.wait_ge(dve_head, HEADS + 1)
            dve.wait_ge(gains_in, 32)

            def split_mix(t):
                rows = mix[:, :, t * P:(t + 1) * P]
                if t >= 2:
                    dve.wait_ge(mix_full, 2 * t - 2)
                own.do(dve, v.tensor_copy(mix_hi[t % 2][:], rows))
                v.tensor_tensor(mix_lo[t % 2][:], rows, mix_hi[t % 2][:].bitcast(F32),
                                ALU.subtract).then_inc(msplit_ready, 1)

            def split_f(t):
                for j in range(2):
                    dve.wait_ge(f_hi_ready, 2 * t + j + 1)
                    ts = slice(t * P, (t + 1) * P)
                    v.tensor_tensor(f_lo[:, 4 * j:4 * j + 4, ts],
                                    ps[:, 4 + 2 * (t % 2) + j, :].rearrange("p (k n) -> p k n", k=4),
                                    f_hi[:, 4 * j:4 * j + 4, ts].bitcast(F32), ALU.subtract).then_inc(f_split, 1)

            split_mix(0)
            split_mix(1)
            for t in range(TB):
                b = 2 * (t % 2)
                dve.wait_ge(sd1_ready, t + 1)
                own.do(dve, v.reciprocal(stat_e[:, t:t + 1], stat_b[:, t:t + 1]))
                v.scalar_tensor_tensor(h1_blk[:], psf[:, b * HALF:(b + 2) * HALF], stat_e[:, t:t + 1], post_gain[:],
                                       ALU.mult, ALU.mult).then_inc(mix_taken, 1)
                dve.wait_ge(mix_taken, t + 1)
                dve.wait_ge(xblk_in, 16 * t + 16)
                v.tensor_tensor(h1_blk[:], h1_blk[:], x_blk[:], ALU.add).then_inc(h1_ready, 1)
                if t + 2 < TB:
                    split_mix(t + 2)
                if t == TB - 2:
                    dve.wait_ge(msplit_ready, TB)
                    for j in range(16):
                        v.memset(y[:, j // 2, half(j % 2)], 0.0).then_inc(y_added, 1)
                dve.wait_ge(sd2_ready, t + 1)
                own.do(dve, v.reciprocal(stat_f[:, t:t + 1], stat_d[:, t:t + 1]))
                v.scalar_tensor_tensor(f_blk[:], h1_blk[:], stat_f[:, t:t + 1], ffn_gain[:],
                                       ALU.mult, ALU.mult).then_inc(f_ready, 1)
                if t >= 1:
                    split_f(t - 1)
            split_f(TB - 1)

            dve.wait_ge(f_ready, TB)
            for j in range(4):
                v.memset(hid[:, 0, j:j + 1], 0.0).then_inc(hid_ready, 1)
            dve.wait_ge(hid_ready, 4)
            start = own.at
            with dve.Fori(0, FG, 1) as g:
                for b in range(4):
                    m, n = b % 2, b // 2
                    dve.wait_ge(up2_full, 4 * g + b + 1)
                    dve.wait_ge(silu_ready, 4 * g + b + 1)
                    v.tensor_tensor(hid[:, b % 2, :], ps[:, 4 + b, :], silu_g[:, b, :], ALU.mult).then_inc(hid_ready, 1)
                    dve.wait_ge(hid_hi_ready, 4 * g + b + 1)
                    v.tensor_tensor(hid_lo[:, m, half(n)], hid[:, b % 2, :], hid_hi[:, m, half(n)].bitcast(F32),
                                    ALU.subtract).then_inc(hid_split, 1)
                for j in range(16):
                    dve.wait_ge(down_full, 16 * g + j + 1)
                    rows = y[:, j // 2, half(j % 2)]
                    v.tensor_tensor(rows, ps[:, j % 8, :], rows, ALU.add).then_inc(y_added, 1)

            for j in range(4):
                dve.wait_ge(p_hi_ready, j + 1)
                o = (slice(None), j // 2, half(j % 2))
                v.tensor_tensor(p_lo[o], ps[:, j, :], p_hi[o].bitcast(F32), ALU.subtract).then_inc(p_split, 1)
            dve.wait_ge(fpg_in, 16)
            for t in range(TB):
                dve.wait_ge(h2_sd, t + 1)
                own.do(dve, v.reciprocal(stat_c[:, t:t + 1], stat_b[:, t:t + 1]))
                own.do(dve, v.scalar_tensor_tensor(y[:, t, :], y[:, t, :], stat_c[:, t:t + 1], ffn_post_gain[:],
                                                   ALU.mult, ALU.mult))
                dve.wait_ge(h1_back[t % 3], 16 * (t // 3) + 16)
                v.tensor_tensor(y[:, t, :], y[:, t, :], h1_in[t % 3][:], ALU.add).then_inc(h2_ready, 1)
            for t in range(TB):
                for j in range(2):
                    dve.wait_ge(h2_hi_ready, 2 * t + j + 1)
                    ts = slice(t * P, (t + 1) * P)
                    v.tensor_tensor(h2_lo[:, 4 * j:4 * j + 4, ts],
                                    ps[:, 2 * (t % 4) + j, :].rearrange("p (k n) -> p k n", k=4),
                                    h2_hi[:, 4 * j:4 * j + 4, ts].bitcast(F32), ALU.subtract).then_inc(h2_split, 1)
            for j in range(16):
                m, n = 2 * (j // 4) + j % 2, (j // 2) % 2
                o = (slice(None), m, half(n))
                dve.wait_ge(sig_ready, j + 1)
                if j >= 2:
                    dve.wait_ge(x3_hi_ready, j - 1)
                t = x3[:, j % 2, :]
                own.do(dve, v.tensor_tensor(t, sig[:, j % 2, :], pp[o], ALU.mult))
                own.do(dve, v.tensor_tensor(t, t, h2_lo[o].bitcast(F32), ALU.add))
                v.tensor_tensor(t, t, h2_hi[o].bitcast(F32), ALU.add).then_inc(x3_ready, 1)
                dve.wait_ge(x3_hi_ready, j + 1)
                v.tensor_tensor(x3_lo[o], t, x3_hi[o].bitcast(F32), ALU.subtract).then_inc(x3_split, 1)

            for j in range(16):
                dve.wait_ge(out_full, j + 1)
                v.tensor_scalar(y2[:, j // 2, half(j % 2)], ps[:, j % 8, :], ALPHA, None, ALU.mult).then_inc(y2_added, 1)
            dve.wait_ge(x3_split, 16)
            v.memset(u_buf[:, 0, 0:HALO], 0.0).then_inc(pm_ready, 1)
            v.memset(u_buf[:, 1, 0:HALO], 0.0).then_inc(pm_ready, 1)
            dve.wait_ge(pm_ready, 2)
            for g, width in enumerate(WINDOWS):
                n8 = 8 * g
                for j in range(8):
                    n, m = j % 2, j // 2
                    dve.wait_ge(pu_taken, n8 + j + 1)
                    u = u_buf[:, n, :]
                    if n == 0:
                        own.do(dve, v.tensor_copy(u_buf[:, 1, 0:HALO], u[:, HALF:W1]))
                    if n8 + j >= 1:
                        dve.wait_ge(pm_split, n8 + j)
                    src, reach, steps = u, 1, g + 1
                    for step in range(steps):
                        dst = win[:, (steps - step) % 2, :]
                        own.do(dve, v.tensor_tensor(dst[:, reach * 2 - 1:W1], src[:, reach * 2 - 1:W1],
                                                    src[:, reach - 1:W1 - reach], ALU.add))
                        src, reach = dst, reach * 2
                    ins = v.scalar_tensor_tensor(win[:, 0, HALO:W1], src[:, HALO:W1], 1.0 / width, u[:, HALO:W1],
                                                 ALU.mult, ALU.subtract)
                    if n == 0:
                        own.do(dve, ins)
                        first = slice(HALO, HALO + width)
                        own.do(dve, v.tensor_tensor(win[:, 0, first], src[:, first], inv_count[:, 0:width], ALU.mult))
                        ins = v.tensor_tensor(win[:, 0, first], win[:, 0, first], u[:, first], ALU.subtract)
                    ins.then_inc(pm_ready, 1)
                    dve.wait_ge(pm_hi_ready, n8 + j + 1)
                    o = (slice(None), m, half(n))
                    v.tensor_tensor(m_lo[o], win[:, 0, HALO:W1], m_hi[o].bitcast(F32), ALU.subtract).then_inc(pm_split, 1)
                for j in range(8):
                    m, n = j % 4, j // 4
                    dve.wait_ge(grp_full, n8 + j + 1)
                    dve.wait_ge(z_taken, n8 + 2 * m + n + 1)
                    if n8 + j >= 1:
                        dve.wait_ge(g_split, n8 + j)
                    v.scalar_tensor_tensor(gt[:], ps[:, j, :], pool_gain[:, 4 * g + m:4 * g + m + 1], z[:, m, half(n)],
                                           ALU.mult, ALU.mult).then_inc(gt_ready, 1)
                    dve.wait_ge(g_hi_ready, n8 + j + 1)
                    lo = g_lo0[:, m, :] if n == 0 else m_lo[:, m, 0:HALF]
                    v.tensor_tensor(lo, gt[:], g_hi[:, m, half(n)].bitcast(F32), ALU.subtract).then_inc(g_split, 1)
                for j in range(32):
                    q = 32 * g + j
                    dve.wait_ge(out_full, 16 + q + 1)
                    rows = y2[:, (j % 16) // 2, half(j % 2)]
                    if j >= 16 or g >= 1:
                        dve.wait_ge(y2_added, q + 1)
                    v.tensor_tensor(rows, ps[:, j % 8, :], rows, ALU.add).then_inc(y2_added, 1)
                    if g == GROUPS - 1 and j >= 16 and j % 2 == 1:
                        layer_norm(dve, v, own, (j - 16) // 2)

        def layer_norm(dve, v, own, t):
            if t == 0:
                dve.wait_ge(ln_in, 32)
            dve.wait_ge(y2_added, 16 + 32 * (GROUPS - 1) + 16 + 2 * t + 2)
            for n in range(2):
                own.do(dve, v.bn_stats(bn[:, n, :], y2[:, t, n * HALF:(n + 1) * HALF]))
            v.bn_aggr(mv2, bn.rearrange("p c j -> p (c j)")).then_inc(ln_var, 1)
            dve.wait_ge(ln_sd, t + 1)
            own.do(dve, v.reciprocal(stat_c[:, t:t + 1], stat_b[:, t:t + 1]))
            own.do(dve, v.scalar_tensor_tensor(y2[:, t, :], y2[:, t, :], mv2[:, 0:1], ln_gain[:],
                                               ALU.subtract, ALU.mult))
            v.scalar_tensor_tensor(y2[:, t, :], y2[:, t, :], stat_c[:, t:t + 1], ln_bias[:],
                                   ALU.mult, ALU.add).then_inc(out_ready, 1)

        N_CONSTS = 11 + HALO
        OWN_HEAD = 6 + 8 + 7 + 8 + 6 + 2 + 1

        block = ctx.enter_context(nc.Block())

        @block.sync
        def _(sp):
            sp_program(sp)

        @block.gpsimd
        def _(pool):
            pool_program(pool)

        @block.tensor
        def _(pe):
            pe_program(pe)

        @block.scalar
        def _(act):
            act_program(act)

        @block.vector
        def _(dve):
            dve_program(dve)


_INS = ["x", "p", "positions", "attn_pre_norm", "attn_post_norm", "w_in", "q_norm", "kv_norm", "w_uq", "w_ukv",
        "conv_w", "conv_b", "gate_bias_i", "gate_bias_f", "mlstm_norm", "w_out", "ffn_pre_norm", "ffn_post_norm",
        "w_gate", "w_up", "w_down", "w_ple_proj", "w_ple_gate", "ln_g_2", "ln_b_2", "pool_w_in_2", "pool_w_grp_2",
        "pool_scale_2", "pool_w_out_2"]


def kernel(**inputs):
    import numpy as _np
    import concourse.bacc as _bacc
    from concourse import mybir as _mybir
    from concourse.bass_utils import run_bass_kernel_spmd as _run

    nc = _bacc.Bacc("TRN2", target_bir_lowering=False, num_devices=1)
    arrays, aps = {}, {}
    given = {name: _np.ascontiguousarray(inputs[name]) for name in _INS}
    freq = _np.float32(10000.0) ** (-_np.arange(0, ROPE, 2, dtype=_np.float32) / _np.float32(ROPE))
    given["inv_freq"] = _np.ascontiguousarray(_np.tile(freq.astype(_np.float32), 4)[:, None])
    for name, x in given.items():
        arrays[f"in_{name}"] = x
        aps[name] = nc.dram_tensor(f"in_{name}", x.shape, _mybir.dt.from_np(x.dtype), kind="ExternalInput").ap()
    out = nc.dram_tensor("out_0", (1, S, D), _mybir.dt.float32, kind="ExternalOutput").ap()
    build(nc, aps, out)
    r = _run(nc, [arrays], core_ids=[0])
    return r.results[0]["out_0"]
```

```python
from contextlib import ExitStack

import concourse.bass as bass
from concourse import mybir

F32 = mybir.dt.float32
F32R = mybir.dt.float32r
I32 = mybir.dt.int32
ACT = mybir.ActivationFunctionType
ALU = mybir.AluOpType
AX = mybir.AxisListType

P = 128
S = 1024
D = 1024
HALF = 512
TB = S // P
KD = D // P
EPS = 1e-6
LN_EPS = 1e-5
NEG = -1e30

Q_ORDER = (0, 7, 1, 6, 2, 5, 3, 4)
PLE = 256
HEADS = 4
NOPE, ROPE, VH = 128, 64, 128
QLORA, KVLORA = 256, 128
QK_SCALE = float(NOPE + ROPE) ** -0.5
MW = 512
MH_SCALE = 128.0 ** -0.5
CONV = 4
DFF = 2816
FG = DFF // 256
DP = 2048
GROUPS = 4
GW = DP // GROUPS
WINDOWS = (2, 4, 8, 16)
HALO = 16
ALPHA = 2.0 ** 0.25

KB = 1024
PI_SAFE = 3.1415925
TWO_PI_A = 6.28125
TWO_PI_B = 0.0019350051879882812
TWO_PI_C = 2.0 * 3.141592653589793 - TWO_PI_A - TWO_PI_B
SMALL = {"allow_slow_non_contiguous": True}
ROUND = 12582912.0


class Chain:

    def __init__(self, sem):
        self.sem, self.at = sem, 0

    def mark(self, instruction):
        instruction.then_inc(self.sem, 1)
        self.at = self.at + 1

    def wait(self, engine):
        engine.wait_ge(self.sem, self.at)

    def do(self, engine, instruction):
        self.mark(instruction)
        self.wait(engine)


def build(nc, a, out):
    ctx = ExitStack()
    with ctx:
        def sem(name):
            return ctx.enter_context(nc.semaphore(name))

        ARENA = 200 * KB + 8000
        base = 16512
        ctx.enter_context(nc.sbuf_tensor("arena", [P, ARENA // 4], F32))

        def at(name, shape, offset, dt=F32):
            return nc.alloc_sbuf_tensor_at(name, shape, dt, offset=base + offset)

        A, B, C, E, M = 56 * KB, 120 * KB, 152 * KB, 184 * KB, 200 * KB
        SLOT = [0, 16 * KB, 32 * KB, C, C + 16 * KB]
        S2 = SLOT[2]
        w_hi = [at(f"w_hi{s}", [P, 2048], SLOT[s], F32R) for s in range(5)]
        w_lo = [at(f"w_lo{s}", [P, 2048], SLOT[s] + 8 * KB, F32R) for s in range(5)]
        stage = at("stage", [P, 2, 1024], 48 * KB)

        ident = at("ident", [P, P], M)
        ident_r = at("ident_r", [P, P], M + 512, F32R)
        causal = at("causal", [P, P], M + 1024)
        causal_t = at("causal_t", [P, P], M + 1536)
        ones = at("ones", [P, P], M + 2048)
        SPARE = M + 2560
        cols = at("cols", [P, 304], SPARE + 4224)
        used = [0]

        def col(n):
            c = used[0]
            used[0] += n
            assert used[0] <= 304
            return cols[:, c:c + n]

        q_gain, kv_gain = col(2), col(1)
        conv_at = used[0]
        conv_w, conv_b = col(32).rearrange("p (c j) -> p c j", j=CONV), col(8)
        inv_freq, sin_sign = col(1), col(1)
        gate_bias = col(2)
        pool_gain = col(16)
        inv_count = col(HALO)
        stat_a, stat_b, stat_c = col(8), col(8), col(8)
        stat_d, stat_e, stat_f = col(8), col(8), col(8)
        token = col(1)
        u_col, m_prev = col(8), col(8)
        floor_col = cols[:, conv_at:conv_at + HEADS * TB]
        head_gain = cols[:, conv_at + HEADS * TB:conv_at + HEADS * TB + HEADS]
        neg_max, row_sum, row_inv = col(8), col(8), col(8)
        den, den_inv, var8, sd8, rs8, h_scale = col(8), col(8), col(8), col(8), col(8), col(8)
        row_sums, neg_mean, shift = col(16), stat_e, stat_f

        x_nat = at("x_nat", [P, TB, D], C)
        pre_gain = at("pre_gain", [P, D], E)
        junk0 = at("junk0", [P, D], B + 16 * KB)
        u_hi = at("u_hi", [P, KD, S], A, F32R)
        u_lo = at("u_lo", [P, KD, S], A + 32 * KB, F32R)
        pos_i = at("pos_i", [P, S], E + 4 * KB, I32)
        ang = at("ang", [P, S], E + 8 * KB)
        turns = at("turns", [P, S], E + 12 * KB)
        rot = at("rot", [P, S], SPARE)
        c_q = at("c_q", [P, 2, S], S2)
        c_kv = at("c_kv", [P, S], S2 + 8 * KB)
        k_pe = at("k_pe", [P, S], S2 + 12 * KB)
        raw = at("raw", [P, 2, S + CONV - 1], B)
        sd_q = at("sd_q", [P, S], B + 8448)
        sd_kv = at("sd_kv", [P, S], B + 16 * KB)
        k_tmp = at("k_tmp", [P, S], B + 16 * KB)
        i_row = at("i_row", [HEADS, S], B + 20 * KB)
        f_row = at("f_row", [HEADS, S], B + 24 * KB)
        b_row = at("b_row", [HEADS, S], B + 28 * KB)
        e_row = at("e_row", [HEADS, S], E + 8 * KB)
        m_row = at("m_row", [HEADS, S], E + 12 * KB)
        sq = at("sq", [P, 2, S], E)
        m_qk = at("m_qk", [P, 8, S], C)
        m_v = at("m_v", [P, HEADS, S], E)
        mix = at("mix", [P, 8, S], B)
        wq_h = at("wq_h", [P, 2, NOPE + ROPE], B + 12544)
        wkv_h = at("wkv_h", [P, NOPE + VH], B + 14080)
        q_n = at("q_n", [P, S], A)
        q_pe = at("q_pe", [P, S], A + 4 * KB)
        k_n = at("k_n", [P, S], A + 8 * KB)
        v_n = at("v_n", [P, TB, P], A + 12 * KB)
        probs = at("probs", [P, 2, S], A + 16 * KB)
        probs_t = at("probs_t", [P, TB, P], A + 24 * KB)
        mq_h = at("mq_h", [P, S], A + 28 * KB)
        mk_h = at("mk_h", [P, S], A + 32 * KB)
        mv_h = at("mv_h", [P, S], A + 36 * KB)
        r_b = at("r_b", [P, S], A + 40 * KB)
        h_nat = at("h_nat", [P, TB, P + 1], A + 44 * KB)
        sink = at("sink", [P, P], A + 44 * KB + 4 * TB * (P + 1))
        O1 = A + 49 * KB
        vo = at("vo", [P, TB, P + 1], O1)
        k_nat = at("k_nat", [P, TB, P], O1 + 4 * TB * (P + 1))
        O2 = O1 + 4 * TB * (2 * P + 1)
        state = at("state", [P, P + 1], O2)
        e_buf, d_t, inter, s_t, q_in, k_w = (
            at(name, [P, 2, P], O2 + 544 + KB * j)
            for j, name in enumerate(("e_buf", "d_t", "inter", "s_t", "q_in", "k_w")))
        mix_hi = [at(f"mix_hi{b}", [P, 8, P], E + 8 * KB * b, F32R) for b in range(2)]
        mix_lo = [at(f"mix_lo{b}", [P, 8, P], E + 8 * KB * b + 4 * KB, F32R) for b in range(2)]
        x_blk = at("x_blk", [P, D], S2)
        h1_blk = at("h1_blk", [P, D], S2 + 4 * KB)
        f_blk = at("f_blk", [P, D], S2 + 8 * KB)
        ffn_gain = at("ffn_gain", [P, D], S2 + 12 * KB)
        post_gain = at("post_gain", [P, D], SPARE)
        f_hi = at("f_hi", [P, KD, S], A, F32R)
        f_lo = at("f_lo", [P, KD, S], A + 32 * KB, F32R)
        y = at("y", [P, TB, D], B)
        silu_g = at("silu_g", [P, 4, HALF], C)
        hid = at("hid", [P, 2, HALF], C + 8 * KB)
        hid_hi = at("hid_hi", [P, 2, S], E, F32R)
        hid_lo = at("hid_lo", [P, 2, S], E + 8 * KB, F32R)
        p_nat = at("p_nat", [P, TB, PLE], A)
        p_hi = at("p_hi", [P, 2, S], A + 8 * KB, F32R)
        p_lo = at("p_lo", [P, 2, S], A + 16 * KB, F32R)
        junk2 = at("junk2", [P, D], S2)
        h1_in = [at(f"h1_in{b}", [P, D], S2 + 4 * KB * (1 + b)) for b in range(3)]
        ffn_post_gain = at("ffn_post_gain", [P, D], SPARE)
        pp = at("pp", [P, KD, S], C)
        h2_hi = at("h2_hi", [P, KD, S], A, F32R)
        h2_lo = at("h2_lo", [P, KD, S], A + 32 * KB, F32R)
        sig = at("sig", [P, 2, HALF], S2)
        x3 = at("x3", [P, 2, HALF], S2 + 4 * KB)
        x3_hi = at("x3_hi", [P, KD, S], C, F32R)
        x3_lo = at("x3_lo", [P, KD, S], B, F32R)
        y2 = at("y2", [P, TB, D], A)
        m_hi = at("m_hi", [P, 4, S], A + 32 * KB, F32R)
        m_lo = at("m_lo", [P, 4, S], A + 48 * KB, F32R)
        z = at("z", [P, 4, S], E)
        g_hi = at("g_hi", [P, 4, S], E, F32R)
        g_lo0 = at("g_lo0", [P, 4, HALF], S2, F32R)
        W1 = HALO + HALF
        u_buf = at("u_buf", [P, 2, W1], SPARE)
        win = at("win", [P, 2, W1], S2 + 8 * KB)
        gt = at("gt", [P, HALF], S2 + 8 * KB + 4352)
        ln_gain = at("ln_gain", [P, D], C)
        ln_bias = at("ln_bias", [P, D], C + 4 * KB)
        ln_sink = at("ln_sink", [P, D], C + 8 * KB)

        ps = ctx.enter_context(nc.psum_tensor("ps", [P, 8, HALF], F32))
        psf = ps[:].rearrange("p b n -> p (b n)")

        gate_dram = nc.dram_tensor("gate_rows", [4, HEADS, S], F32, kind="Internal").ap()
        h1_dram = nc.dram_tensor("h1_rows", [S, D], F32, kind="Internal").ap()

        staged = [sem("staged0"), sem("staged1")]
        parted = [sem("parted0"), sem("parted1")]
        pool_hi = Chain(sem("pool_hi"))
        consts = sem("consts")
        cols_in = sem("cols_in")
        pre_gain_in = sem("pre_gain_in")
        pos_in = sem("pos_in")
        x_in = [sem(f"x_in{t}") for t in range(TB)]
        x_sd, xn_ready, ut_full, u_hi_ready, u_split = map(sem, (
            "x_sd", "xn_ready", "ut_full", "u_hi_ready", "u_split"))
        in_full, in_taken = sem("in_full"), sem("in_taken")
        sq_ready, gates_abs, gates_log, gates_rows, gates_spilled = map(sem, (
            "sq_ready", "gates_abs", "gates_log", "gates_rows", "gates_spilled"))
        kpe_prod, kpe_shift, kpe_sum = map(sem, ("kpe_prod", "kpe_shift", "kpe_sum"))
        rot_ang, rot_sin = sem("rot_ang"), sem("rot_sin")
        conv_done, silu_done, latent_ready = map(sem, ("conv_done", "silu_done", "latent_ready"))
        head_w, head_g, heads_in = sem("head_w"), sem("head_g"), sem("heads_in")
        act_head, dve_head = sem("act_head"), sem("dve_head")
        up_full, up_taken, qp_ready, mqkv_ready = map(sem, (
            "up_full", "up_taken", "qp_ready", "mqkv_ready"))
        s_full, nm_ready, probs_done, p_ready = map(sem, (
            "s_full", "nm_ready", "probs_done", "p_ready"))
        pt_full, pt_taken, o_full, o_taken = map(sem, ("pt_full", "pt_taken", "o_full", "o_taken"))
        st_full, kv_full, e_ready, dt_ready, ib_ready, st_ready, kv_nat, kw_ready = map(sem, (
            "st_full", "kv_full", "e_ready", "dt_ready", "ib_ready", "st_ready", "kv_nat", "kw_ready"))
        num_full, num_taken, cn_full, cn_done = map(sem, (
            "num_full", "num_taken", "cn_full", "cn_done"))
        hsq_ready, hvar_ready, hs_ready, ht_full = map(sem, ("hsq_ready", "hvar_ready", "hs_ready", "ht_full"))
        msplit_ready, mix_full, mix_taken, mix_used = map(sem, (
            "msplit_ready", "mix_full", "mix_taken", "mix_used"))
        gains_in, xblk_in, h1_ready, h1_spilled = map(sem, (
            "gains_in", "xblk_in", "h1_ready", "h1_spilled"))
        sd1_ready, sd2_ready, f_ready, ft_full, f_hi_ready, f_split = map(sem, (
            "sd1_ready", "sd2_ready", "f_ready", "ft_full", "f_hi_ready", "f_split"))
        gate_full, up2_full, down_full, silu_ready, hid_ready, hid_hi_ready, hid_split, y_added = map(sem, (
            "gate_full", "ffn_up_full", "down_full", "silu_ready", "hid_ready", "hid_hi_ready",
            "hid_split", "y_added"))
        p_in, pt2_full, p_hi_ready, p_split, pp_full, pp_taken = map(sem, (
            "p_in", "ple_t_full", "p_hi_ready", "p_split", "pp_full", "pp_taken"))
        fpg_in = sem("fpg_in")
        h1_back = [sem(f"h1_back{b}") for b in range(3)]
        h2_sd, h2_ready, h2t_full, h2_hi_ready, h2_split = map(sem, (
            "h2_sd", "h2_ready", "h2t_full", "h2_hi_ready", "h2_split"))
        pg_full, sig_ready, x3_ready, x3_hi_ready, x3_split = map(sem, (
            "pg_full", "sig_ready", "x3_ready", "x3_hi_ready", "x3_split"))
        out_full, y2_added = sem("out_full"), sem("y2_added")
        pu_full, pu_taken, pm_ready, pm_hi_ready, pm_split = map(sem, (
            "pu_full", "pu_taken", "pm_ready", "pm_hi_ready", "pm_split"))
        z_full, z_taken, grp_full, gt_ready, g_hi_ready, g_split = map(sem, (
            "z_full", "z_taken", "grp_full", "gt_ready", "g_hi_ready", "g_split"))
        ln_in, ln_mean, ln_sd, ln_shift, ln_normed, ln_gained, out_ready, out_stored = map(sem, (
            "ln_in", "ln_mean", "ln_sd", "ln_shift", "ln_normed", "ln_gained", "out_ready", "out_stored"))
        dve_own = Chain(sem("dve_own"))
        act_own = Chain(sem("act_own"))

        T_OUT, T_FFN, T_PLE, T_PG, T_POOL = 10, 14, 47, 48, 52

        def k_rows(w):
            return w.rearrange("(k p) n -> p k n", p=P)

        w_in, w_out, w_gate, w_up, w_down = a["w_in"][0], a["w_out"][0], a["w_gate"][0], a["w_up"][0], a["w_down"][0]
        w_pp, w_pg = a["w_ple_proj"][0], a["w_ple_gate"][0]
        pw_in, pw_grp, pw_out = a["pool_w_in_2"][0], a["pool_w_grp_2"][0], a["pool_w_out_2"][0]

        def half_cols(w, h, c0):
            return k_rows(w)[:, 4 * h:4 * h + 4, bass.ds(c0, 256)]

        def half_rows(w, h, r0):
            return w[bass.ds(r0 + P * h, P), :]

        def wcols(s, k, m):
            c = k * 256 + m * P
            return w_hi[s][:, c:c + P], w_lo[s][:, c:c + P]

        def score_bank(i):
            return 0 if i >= 4 else 6 * HALF

        def sp_program(sp):
            def load(t, sources):
                for h in range(2):
                    if not (isinstance(t, int) and t == 0):
                        sp.wait_ge(parted[h], t)
                    src, view = sources(h)
                    sp.dma_start(view, src).then_inc(staged[h], 16)

            def cols_tile(w, c0):
                return lambda h: (half_cols(w, h, c0), stage[:, h, :].rearrange("p (k n) -> p k n", k=4))

            def rows_tile(w, r0):
                return lambda h: (half_rows(w, h, r0), stage[:, h, :])

            def x_rows(t):
                sp.dma_start(x_nat[:, t, :], a["x"][0, t * P:(t + 1) * P, :]).then_inc(x_in[t], 16)

            def column(dst, src):
                sp.dma_start(dst, src, **SMALL).then_inc(cols_in, 16)

            x_rows(0)
            x_rows(1)
            x_rows(2)
            load(0, cols_tile(w_in, 0))
            for t in range(3, TB):
                x_rows(t)
            sp.dma_start(pos_i[:], a["positions"][0].partition_broadcast(P)).then_inc(pos_in, 16)
            sp.dma_start(inv_freq, a["inv_freq"]).then_inc(pos_in, 16)
            column(gate_bias[0:HEADS, 0:1], a["gate_bias_i"][0].rearrange("(h c) -> h c", c=1))
            column(gate_bias[0:HEADS, 1:2], a["gate_bias_f"][0].rearrange("(h c) -> h c", c=1))
            column(q_gain, a["q_norm"][0].rearrange("(c p) -> p c", p=P))
            column(kv_gain, a["kv_norm"][0].rearrange("(c p) -> p c", p=P))
            for h in range(2):
                sp.wait_ge(parted[h], 1)
                view = stage[:, h, :].rearrange("p (k n) -> p k n", k=4)
                rows = k_rows(w_in)[:, 4 * h:4 * h + 4, :]
                sp.dma_start(view[:, :, 0:192], rows[:, :, 256:448]).then_inc(staged[h], 16)
                sp.dma_start(view[:, :, 192:196], rows[:, :, 2496:2500]).then_inc(staged[h], 16)
                sp.dma_start(view[:, :, 224:228], rows[:, :, 2500:2504]).then_inc(staged[h], 16)
            for j in range(CONV):
                column(conv_w[:, :, j], a["conv_w"][0, j].rearrange("(c p) -> p c", p=P))
            column(conv_b, a["conv_b"][0].rearrange("(c p) -> p c", p=P))
            column(pool_gain, a["pool_scale_2"][0].rearrange("(c p) -> p c", p=P))
            with sp.Fori(1, 5, 1) as i:
                for e in range(2):
                    load(2 * i + e, cols_tile(w_in, 512 * i - 64 + 256 * e))
            load(T_OUT, rows_tile(w_out, 0))

            def head_weights(h):
                wq = a["w_uq"][0].rearrange("(k p) n -> p k n", p=P)
                sp.dma_start(wq_h[:], wq[:, :, bass.ds(h * (NOPE + ROPE), NOPE + ROPE)]).then_inc(head_w, 16)
                sp.dma_start(wkv_h[:], a["w_ukv"][0][:, bass.ds(h * (NOPE + VH), NOPE + VH)]).then_inc(head_w, 16)

            def head_gates(h):
                r0, u0, m0 = (gate_dram[j] for j in (0, 1, 3))
                sp.dma_start(r_b[:], r0[bass.ds(h, 1), :].rearrange("a t -> (a t)").partition_broadcast(P)).then_inc(head_g, 16)
                sp.dma_start(u_col, u0[bass.ds(h, 1), :].rearrange("a (c p) -> p (a c)", p=P), **SMALL).then_inc(head_g, 16)
                last = m0[bass.ds(h, 1), :].rearrange("a (c p) -> (a c) p", p=P)[0:TB - 1, P - 1]
                sp.dma_start(m_prev[:, 1:TB], last.partition_broadcast(P), **SMALL).then_inc(head_g, 16)

            sp.wait_ge(in_taken, 24)
            head_weights(0)
            load(T_OUT + 1, rows_tile(w_out, 256))
            sp.wait_ge(gates_spilled, 64)
            sp.wait_ge(in_full, 44)
            head_gates(0)
            sp.wait_ge(conv_done, 8)
            sp.dma_start(floor_col, gate_dram[2].rearrange("h (c p) -> p (h c)", p=P), **SMALL).then_inc(heads_in, 16)
            sp.dma_start(head_gain, a["mlstm_norm"][0].rearrange("(h p) -> p h", p=P), **SMALL).then_inc(heads_in, 16)
            load(T_OUT + 2, rows_tile(w_out, 512))
            with sp.Fori(0, HEADS - 1, 1) as h:
                sp.wait_ge(up_full, 8 * h + 8)
                head_weights(h + 1)
                sp.wait_ge(dt_ready, 8 * h + 8)
                sp.wait_ge(ib_ready, 8 * h + 8)
                head_gates(h + 1)

            load(T_OUT + 3, rows_tile(w_out, 768))
            sp.wait_ge(qp_ready, HEADS)
            sp.dma_start(post_gain[:], a["attn_post_norm"][0].partition_broadcast(P)).then_inc(gains_in, 16)
            sp.wait_ge(up_full, 8 * HEADS)
            sp.dma_start(x_blk[:], a["x"][0, 0:P, :]).then_inc(xblk_in, 16)
            sp.wait_ge(s_full, 8 * HEADS)
            sp.dma_start(ffn_gain[:], a["ffn_pre_norm"][0].partition_broadcast(P)).then_inc(gains_in, 16)
            load(T_FFN, cols_tile(w_gate, 0))
            for t in range(TB):
                sp.wait_ge(h1_ready, t + 1)
                sp.dma_start(h1_dram[t * P:(t + 1) * P, :], h1_blk[:]).then_inc(h1_spilled, 16)
                if t + 1 < TB:
                    sp.dma_start(x_blk[:], a["x"][0, (t + 1) * P:(t + 2) * P, :]).then_inc(xblk_in, 16)
            sp.wait_ge(f_ready, TB)
            sp.dma_start(ffn_post_gain[:], a["ffn_post_norm"][0].partition_broadcast(P)).then_inc(fpg_in, 16)
            with sp.Fori(0, FG - 1, 1) as g:
                load(T_FFN + 3 * g + 1, cols_tile(w_up, 256 * g))
                load(T_FFN + 3 * g + 2, rows_tile(w_down, 256 * g))
                load(T_FFN + 3 * g + 3, cols_tile(w_gate, 256 * g + 256))
            load(T_PLE - 2, cols_tile(w_up, 256 * (FG - 1)))
            load(T_PLE - 1, rows_tile(w_down, 256 * (FG - 1)))
            load(T_PLE, rows_tile(w_pp, 0))
            sp.wait_ge(up2_full, 4 * FG)
            sp.dma_start(p_nat[:], a["p"][0, 0].rearrange("(t p) c -> p t c", p=P)).then_inc(p_in, 16)
            load(T_PG, cols_tile(w_pg, 0))
            sp.wait_ge(down_full, 16 * FG)
            sp.wait_ge(h1_spilled, 16 * TB)
            for t in range(TB):
                if t >= 3:
                    sp.wait_ge(h2_ready, t - 2)
                sp.dma_start(h1_in[t % 3][:], h1_dram[t * P:(t + 1) * P, :]).then_inc(h1_back[t % 3], 16)
            for j in range(1, 4):
                load(T_PG + j, cols_tile(w_pg, 256 * j))
            with sp.Fori(0, 2, 1) as i:
                for e in range(2):
                    t0, c0 = T_POOL + 14 * i + 7 * e, 1024 * i + GW * e
                    load(t0, cols_tile(pw_in, c0))
                    load(t0 + 1, cols_tile(pw_in, c0 + 256))
                    load(t0 + 2, cols_tile(pw_in, c0 + DP))
                    load(t0 + 3, cols_tile(pw_in, c0 + DP + 256))
                    grp = pw_grp.rearrange("g c d -> (g c) d")
                    load(t0 + 4, lambda h: (
                        grp[bass.ds(c0 + 256 * h, 256), :].rearrange("(k p) n -> p k n", p=P),
                        stage[:, h, :].rearrange("p (k n) -> p k n", k=2)))
                    load(t0 + 5, rows_tile(pw_out, c0))
                    load(t0 + 6, rows_tile(pw_out, c0 + 256))
            sp.wait_ge(z_full, 32)
            sp.dma_start(ln_gain[:], a["ln_g_2"][0].partition_broadcast(P)).then_inc(ln_in, 16)
            sp.dma_start(ln_bias[:], a["ln_b_2"][0].partition_broadcast(P)).then_inc(ln_in, 16)
            for t in range(TB):
                sp.wait_ge(out_ready, t + 1)
                sp.dma_start(out[0, t * P:(t + 1) * P, :], y2[:, t, :]).then_inc(out_stored, 16)
            sp.wait_ge(out_stored, 16 * TB)

        def pool_program(pool):
            g = nc.gpsimd
            own = Chain(consts)
            g.memset(ones[:], 1.0).then_inc(consts, 1)
            own.at = 1
            own.do(pool, g.memset(ident[:], 0.0))
            own.do(pool, g.memset(causal[:], 0.0))
            own.do(pool, g.memset(causal_t[:], 0.0))
            own.do(pool, g.affine_select(out=ident[:], in_=ident[:], compare_op=ALU.not_equal, fill=1.0,
                                         base=0, pattern=[[-1, P]], channel_multiplier=1))
            own.mark(g.affine_select(out=causal[:], in_=causal[:], compare_op=ALU.is_ge, fill=NEG,
                                     base=0, pattern=[[-1, P]], channel_multiplier=1))
            own.mark(g.affine_select(out=causal_t[:], in_=causal_t[:], compare_op=ALU.is_ge, fill=NEG,
                                     base=0, pattern=[[1, P]], channel_multiplier=-1))
            own.mark(g.tensor_copy(ident_r[:], ident[:]))
            own.mark(g.memset(sin_sign[0:96, :], -1.0))
            own.wait(pool)
            own.do(pool, g.memset(sin_sign[96:P, :], 1.0))
            own.mark(g.memset(m_prev[:, 0:1], 0.0))
            for t in range(HALO):
                own.mark(g.memset(inv_count[:, t:t + 1], 1.0 / (t + 1)))
            assert own.at == N_CONSTS

            def part(t, slot, staged_at):
                for h in range(2):
                    pool.wait_ge(staged[h], staged_at)
                    g.tensor_tensor(token, ones[:, 0:1], ones[:, 0:1], ALU.mult)
                    hi, lo = w_hi[slot][:, 1024 * h:1024 * h + 1024], w_lo[slot][:, 1024 * h:1024 * h + 1024]
                    pool_hi.do(pool, g.tensor_scalar(hi, stage[:, h, :], 1.0, 0.0, ALU.mult, ALU.add))
                    g.tensor_tensor(lo, stage[:, h, :], hi.bitcast(F32), ALU.subtract).then_inc(parted[h], 1)

            def landed(t):
                return 16 * t + 48

            part(0, 0, 16)
            part(1, 1, 64)
            start = pool_hi.at
            with pool.Fori(1, 4, 1) as i:
                pool_hi.at = start + 4 * (i - 1)
                for e in range(2):
                    pool.wait_ge(in_full, 8 * i + 4 * e - 4)
                    part(2 * i + e, e, landed(2 * i + e))
            pool_hi.at = start + 12
            for t in (8, 9, 10, 11):
                pool.wait_ge(in_full, 4 * t)
                part(t, t % 2, landed(t))
            pool.wait_ge(mqkv_ready, 3 * HEADS)
            part(12, 4, landed(12))
            part(13, 3, landed(13))
            for j in range(2):
                pool.wait_ge(mix_used, j + 1)
                part(T_FFN + j, j, landed(T_FFN + j))
            pool.wait_ge(ft_full, 2 * TB)
            pool.wait_ge(h1_spilled, 16 * TB)
            part(T_FFN + 2, 2, landed(T_FFN + 2))
            start = pool_hi.at
            with pool.Fori(1, FG, 1) as i:
                pool_hi.at = start + 6 * (i - 1)
                pool.wait_ge(gate_full, 4 * i)
                part(T_FFN + 3 * i, 0, landed(T_FFN + 3 * i))
                pool.wait_ge(up2_full, 4 * i)
                part(T_FFN + 3 * i + 1, 1, landed(T_FFN + 3 * i + 1))
                pool.wait_ge(down_full, 16 * i)
                part(T_FFN + 3 * i + 2, 2, landed(T_FFN + 3 * i + 2))
            pool_hi.at = start + 6 * (FG - 1)
            pool.wait_ge(gate_full, 4 * FG)
            part(T_PLE, 0, landed(T_PLE))
            pool.wait_ge(up2_full, 4 * FG)
            part(T_PG, 1, landed(T_PG))
            pool.wait_ge(pp_full, 16)
            part(T_PG + 1, 0, landed(T_PG + 1))
            pool.wait_ge(pg_full, 4)
            part(T_PG + 2, 1, landed(T_PG + 2))
            pool.wait_ge(pg_full, 8)
            part(T_PG + 3, 0, landed(T_PG + 3))
            start = pool_hi.at
            with pool.Fori(0, 2, 1) as i:
                pool_hi.at = start + 28 * i
                for e in range(2):
                    before = [(out_full, 64 * i + 32 * e + 1), (out_full, 64 * i + 32 * e + 16),
                              (pu_full, 16 * i + 8 * e + 4), (pu_full, 16 * i + 8 * e + 8),
                              (z_full, 16 * i + 8 * e + 4), (z_full, 16 * i + 8 * e + 8),
                              (grp_full, 16 * i + 8 * e + 8)]
                    for j, (s, n) in enumerate(before):
                        pool.wait_ge(s, n)
                        t = T_POOL + 14 * i + 7 * e + j
                        part(t, (1 + 7 * e + j) % 2, landed(t))
            pool.wait_ge(ln_in, 32)
            for t in range(TB - 1):
                pool.wait_ge(ln_normed, t + 1)
                g.tensor_tensor(y2[:, t, :], y2[:, t, :], ln_gain[:], ALU.mult).then_inc(ln_gained, 1)

        def pe_program(pe):
            mm, tr = nc.tensor.matmul, nc.tensor.transpose

            def tile_ready(t):
                pe.wait_ge(parted[0], t + 1)
                pe.wait_ge(parted[1], t + 1)

            def three(out_ap, terms):
                n = 3 * len(terms)
                j = 0
                for lh, ll, rh, rl in terms:
                    for l, r in ((lh, rh), (lh, rl), (ll, rh)):
                        last = mm(out_ap, l, r, start=(j == 0), stop=(j == n - 1))
                        j += 1
                return last

            def proj_t(bank, s, m, n, x_h, x_l):
                ts = slice(n * HALF, n * HALF + HALF)
                return three(ps[:, bank, :], [(*wcols(s, k, m), x_h[:, k, ts], x_l[:, k, ts]) for k in range(KD)])

            def x_transposed(t):
                pe.wait_ge(xn_ready, t + 1)
                if t >= 2:
                    pe.wait_ge(u_split, 2 * (t - 2) + 2)
                for k in range(KD):
                    b, c = 4 + 2 * (t % 2) + k // 4, (k % 4) * P
                    last = tr(ps[:, b, c:c + P], x_nat[:, t, k * P:(k + 1) * P], ident[:])
                    if k % 4 == 3:
                        last.then_inc(ut_full, 1)

            def in_tile(t, s, q0, bank0, first=False):
                tile_ready(t)
                for m in range(2):
                    for n in range(2):
                        j = 2 * m + n
                        if not first:
                            pe.wait_ge(in_taken, q0 + j - 7)
                        proj_t(bank0 + j, s, m, n, u_hi, u_lo).then_inc(in_full, 1)

            pe.wait_ge(consts, N_CONSTS)
            for t in range(TB // 2):
                x_transposed(t)
            tile_ready(0)
            for m in range(2):
                pe.wait_ge(u_split, TB)
                proj_t(m, 0, m, 0, u_hi, u_lo).then_inc(in_full, 1)
                x_transposed(TB // 2 + 2 * m)
                x_transposed(TB // 2 + 2 * m + 1)
            pe.wait_ge(u_split, 2 * TB)
            for m in range(2):
                proj_t(2 + m, 0, m, 1, u_hi, u_lo).then_inc(in_full, 1)
            in_tile(1, 1, 4, 4, first=True)
            with pe.Fori(1, 3, 1) as i:
                in_tile(2 * i, 0, 8 * i, 0)
                in_tile(2 * i + 1, 1, 8 * i + 4, 4)
            pe.wait_ge(sq_ready, 2)
            for j in range(4):
                pe.wait_ge(in_taken, 24 + j - 7)
                mm(ps[:, j, :], ones[:], sq[:, j // 2, (j % 2) * HALF:(j % 2 + 1) * HALF],
                   start=True, stop=True).then_inc(in_full, 1)
            with pe.Fori(3, 5, 1) as i:
                in_tile(2 * i, 0, 8 * i + 4, 4)
                in_tile(2 * i + 1, 1, 8 * i + 8, 0)

            def up_queries(h, first=False):
                pe.wait_ge(head_w, 32 * h + 32)
                if not first:
                    pe.wait_ge(probs_done, 8 * h)
                for n in range(2):
                    for k in range(2):
                        last = mm(ps[:, n, :], wq_h[:, k, 0:NOPE], c_q[:, k, n * HALF:(n + 1) * HALF],
                                  start=(k == 0), stop=(k == 1))
                    last.then_inc(up_full, 1)

            def up_rotary(h, first=False):
                if not first:
                    pe.wait_ge(st_ready, 8 * h)
                for n in range(2):
                    for k in range(2):
                        last = mm(ps[0:ROPE, 6 - n, :], wq_h[:, k, NOPE:NOPE + ROPE], c_q[:, k, n * HALF:(n + 1) * HALF],
                                  start=(k == 0), stop=(k == 1))
                    last.then_inc(up_full, 1)

            def up_keys_values(h, first=False):
                for n, b in enumerate((7, 4)):
                    if not first and n == 0:
                        pe.wait_ge(num_taken, 8 * h)
                        pe.wait_ge(cn_done, 8 * h)
                    if not first and n == 1:
                        pe.wait_ge(o_taken, 8 * h)
                    mm(ps[:, b, :], wkv_h[:, 0:NOPE], c_kv[:, n * HALF:(n + 1) * HALF],
                       start=True, stop=True).then_inc(up_full, 1)
                if not first:
                    pe.wait_ge(pt_taken, 8 * h)
                for t in range(TB):
                    last = mm(ps[:, 2 + t // 4, (t % 4) * P:(t % 4 + 1) * P], c_kv[:, t * P:(t + 1) * P],
                              wkv_h[:, NOPE:NOPE + VH], start=True, stop=True)
                    if t % 4 == 3:
                        last.then_inc(up_full, 1)

            def chunk_rows(h):
                pe.wait_ge(mqkv_ready, 3 * h + 3)
                pe.wait_ge(up_taken, 6 * h + 2)
                for rows, banks in ((mk_h, (0, 1)), (mv_h, (6, 5))):
                    if rows is mv_h:
                        pe.wait_ge(qp_ready, h + 1)
                    for t in range(TB):
                        last = tr(ps[:, banks[t // 4], (t % 4) * P:(t % 4 + 1) * P], rows[:, t * P:(t + 1) * P], ident[:])
                        if t % 4 == 3:
                            last.then_inc(kv_full, 1)

            def head_rows(h):
                pe.wait_ge(hs_ready, h + 1)
                for t in range(TB):
                    last = tr(ps[:, 2 + t // 4, (t % 4) * P:(t % 4 + 1) * P], h_nat[:, t, 0:P], ident[:])
                    if t % 4 == 3:
                        last.then_inc(ht_full, 1)

            def scores(h, s):
                i = Q_ORDER[s]
                blk, o = slice(i * P, (i + 1) * P), score_bank(i)
                if s >= 2:
                    pe.wait_ge(probs_done, 8 * h + s - 1)
                for c0 in range(0, (i + 1) * P, HALF):
                    c1 = min(c0 + HALF, (i + 1) * P)
                    mm(psf[:, o + c0:o + c1], q_n[:, blk], k_n[:, c0:c1], start=True, stop=False)
                    last = mm(psf[:, o + c0:o + c1], q_pe[:, blk], k_pe[:, c0:c1], start=False, stop=True)
                last.then_inc(s_full, 1)

            def probs_transposed(h, s):
                pe.wait_ge(p_ready, 8 * h + s + 1)
                if s == 0:
                    pe.wait_ge(dve_head, h + 1)
                else:
                    pe.wait_ge(pt_taken, 8 * h + s)
                for j in range(Q_ORDER[s] + 1):
                    last = tr(psf[:, 1024 + j * P:1024 + (j + 1) * P],
                              probs[:, s % 2, j * P:(j + 1) * P], ident[:])
                last.then_inc(pt_full, 1)

            def values(h, s):
                i = Q_ORDER[s]
                pe.wait_ge(pt_taken, 8 * h + s + 1)
                if s >= 1:
                    pe.wait_ge(o_taken, 8 * h + s)
                for j in range(i + 1):
                    last = mm(ps[:, 4, 0:P], v_n[:, j, :], probs_t[:, j, :], start=(j == 0), stop=(j == i))
                last.then_inc(o_full, 1)

            def chunk_scores(h, i):
                blk = slice(i * P, (i + 1) * P)
                mm(ps[:, 5, 0:P], mk_h[:, blk], mq_h[:, blk], start=True, stop=True).then_inc(st_full, 1)

            def chunk_state(h, i):
                pe.wait_ge(st_ready, 8 * h + i + 1)
                pe.wait_ge(kw_ready, 8 * h + i + 1)
                if i >= 1:
                    pe.wait_ge(num_taken, 8 * h + i)
                    pe.wait_ge(cn_done, 8 * h + i)
                last = mm(ps[:, 7, 0:P + 1], s_t[:, i % 2, :], vo[:, i, :], start=True, stop=(i == 0))
                if i >= 1:
                    last = mm(ps[:, 7, 0:P + 1], q_in[:, i % 2, :], state[:], start=False, stop=True)
                last.then_inc(num_full, 1)
                mm(ps[:, 7, 2 * P:3 * P + 1], k_w[:, i % 2, :], vo[:, i, :], start=True, stop=True).then_inc(cn_full, 1)

            def head_steps(h):
                pe.wait_ge(up_taken, 6 * h + 6)
                pe.wait_ge(kv_nat, 4 * h + 4)
                chunk_scores(h, 0)
                for s in range(TB):
                    scores(h, s)
                    if s >= 1:
                        probs_transposed(h, s - 1)
                    chunk_state(h, s)
                    if s + 1 < TB:
                        chunk_scores(h, s + 1)
                    if s >= 1:
                        values(h, s - 1)

            pe.wait_ge(in_taken, 44)
            pe.wait_ge(latent_ready, 1)
            pe.wait_ge(act_head, 1)
            up_queries(0, first=True)
            up_rotary(0, first=True)
            up_keys_values(0, first=True)
            chunk_rows(0)
            with pe.Fori(0, HEADS - 1, 1) as h:
                head_steps(h)
                up_queries(h + 1)
                probs_transposed(h, TB - 1)
                up_rotary(h + 1)
                values(h, TB - 1)
                up_keys_values(h + 1)
                pe.wait_ge(up_taken, 6 * h + 12)
                chunk_rows(h + 1)
                head_rows(h)
            head_steps(HEADS - 1)
            probs_transposed(HEADS - 1, TB - 1)
            values(HEADS - 1, TB - 1)

            def f_transposed(t):
                pe.wait_ge(f_ready, t + 1)
                if t >= 2:
                    pe.wait_ge(f_split, 2 * t - 2)
                for k in range(KD):
                    b = 4 + 2 * (t % 2) + k // 4
                    last = tr(ps[:, b, (k % 4) * P:(k % 4 + 1) * P], f_blk[:, k * P:(k + 1) * P], ident[:])
                    if k % 4 == 3:
                        last.then_inc(ft_full, 1)

            slot_of = (0, 1, 4, 3)
            for t in range(TB):
                if t >= 2:
                    pe.wait_ge(mix_taken, t - 1)
                if t == 0:
                    tile_ready(T_OUT + 3)
                if t == 1:
                    pe.wait_ge(dve_head, HEADS + 1)
                for k in range(8):
                    if t == 0 and k == 4:
                        head_rows(HEADS - 1)
                    if k % 4 == 0:
                        pe.wait_ge(msplit_ready, 2 * t + k // 4 + 1)
                    s = slot_of[k // 2]
                    for n in range(2):
                        o, c = ps[:, 2 * (t % 2) + n, :], (k % 2) * 1024 + n * HALF
                        l_hi, l_lo = mix_hi[t % 2][:, k, :], mix_lo[t % 2][:, k, :]
                        mm(o, l_hi, w_hi[s][:, c:c + HALF], start=(k == 0), stop=False)
                        mm(o, l_hi, w_lo[s][:, c:c + HALF], start=False, stop=False)
                        last = mm(o, l_lo, w_hi[s][:, c:c + HALF], start=False, stop=(k == 7))
                        if k == 7:
                            last.then_inc(mix_full, 1)
                    if t == TB - 1 and k in (1, 3):
                        last.then_inc(mix_used, 1)
                if t >= 1:
                    f_transposed(t - 1)

            def gate_rows(g, b):
                pe.wait_ge(y_added, 16 * g + b + 9)
                proj_t(b, 0, b % 2, b // 2, f_hi, f_lo).then_inc(gate_full, 1)

            def up_and_down(g):
                tile_ready(T_FFN + 3 * g + 1)
                for b in range(4):
                    pe.wait_ge(y_added, 16 * g + b + 13)
                    proj_t(4 + b, 1, b % 2, b // 2, f_hi, f_lo).then_inc(up2_full, 1)
                tile_ready(T_FFN + 3 * g + 2)
                for t in range(TB):
                    if t % 4 == 0:
                        pe.wait_ge(hid_split, 4 * g + 2 + t // 2)
                    for n in range(2):
                        j = 2 * t + n
                        if j < 4:
                            pe.wait_ge(silu_ready, 4 * g + j + 1)
                        elif j < 8:
                            pe.wait_ge(hid_split, 4 * g + 4)
                        else:
                            pe.wait_ge(y_added, 16 * g + 16 + j - 7)
                        terms = [(hid_hi[:, k, t * P:(t + 1) * P], hid_lo[:, k, t * P:(t + 1) * P],
                                  w_hi[2][:, k * 1024 + n * HALF:k * 1024 + (n + 1) * HALF],
                                  w_lo[2][:, k * 1024 + n * HALF:k * 1024 + (n + 1) * HALF]) for k in range(2)]
                        three(ps[:, j % 8, :], terms).then_inc(down_full, 1)

            tile_ready(T_FFN)
            pe.wait_ge(f_split, TB)
            pe.wait_ge(mix_taken, TB - 1)
            for b in range(4):
                if b == 2:
                    f_transposed(TB - 1)
                    pe.wait_ge(mix_taken, TB)
                    pe.wait_ge(f_split, 2 * TB)
                gate_rows(0, b)
            up_and_down(0)
            with pe.Fori(1, FG, 1) as g:
                tile_ready(T_FFN + 3 * g)
                for b in range(4):
                    gate_rows(g, b)
                up_and_down(g)

            pe.wait_ge(p_in, 16)
            for c in range(2):
                for t in range(TB):
                    b = 2 * c + t // 4
                    if t % 4 == 0:
                        pe.wait_ge(y_added, 16 * FG + 9 + b)
                    last = tr(ps[:, b, (t % 4) * P:(t % 4 + 1) * P], p_nat[:, t, c * P:(c + 1) * P], ident[:])
                    if t % 4 == 3:
                        last.then_inc(pt2_full, 1)
            tile_ready(T_PLE)
            pe.wait_ge(p_split, 4)
            pe.wait_ge(y_added, 16 * FG + 16)
            for m in range(KD):
                for n in range(2):
                    j = 2 * m + n
                    if j >= 8:
                        pe.wait_ge(pp_taken, j - 7)
                    ts = slice(n * HALF, (n + 1) * HALF)
                    terms = [(w_hi[0][:, k * 1024 + m * P:k * 1024 + (m + 1) * P],
                              w_lo[0][:, k * 1024 + m * P:k * 1024 + (m + 1) * P],
                              p_hi[:, k, ts], p_lo[:, k, ts]) for k in range(2)]
                    three(ps[:, j % 8, :], terms).then_inc(pp_full, 1)
            for t in range(TB):
                pe.wait_ge(h2_ready, t + 1)
                if t < 4:
                    pe.wait_ge(pp_taken, 8 + 2 * t + 2)
                else:
                    pe.wait_ge(h2_split, 2 * (t - 4) + 2)
                for k in range(KD):
                    b = 2 * (t % 4) + k // 4
                    last = tr(ps[:, b, (k % 4) * P:(k % 4 + 1) * P], y[:, t, k * P:(k + 1) * P], ident[:])
                    if k % 4 == 3:
                        last.then_inc(h2t_full, 1)
            pe.wait_ge(h2_split, 2 * TB)
            for i in range(4):
                tile_ready(T_PG + i)
                for j in range(4):
                    b = 4 * (i % 2) + j
                    if i >= 2:
                        pe.wait_ge(sig_ready, 4 * (i - 2) + j + 1)
                    proj_t(b, (1 + i) % 2, j % 2, j // 2, h2_hi, h2_lo).then_inc(pg_full, 1)

            pe.wait_ge(sig_ready, 16)
            for t in range(TB):
                if t % 4 == 0:
                    pe.wait_ge(x3_split, 14 + t // 2)
                for n in range(2):
                    j = 2 * t + n
                    if j >= 8:
                        pe.wait_ge(y2_added, j - 7)
                    for k in range(4):
                        ts = slice(t * P, (t + 1) * P)
                        o = ps[:, j % 8, k * P:(k + 1) * P]
                        mm(o, x3_hi[:, 4 * n + k, ts], ident_r[:], start=True, stop=False)
                        last = mm(o, x3_lo[:, 4 * n + k, ts], ident_r[:], start=False, stop=True)
                    last.then_inc(out_full, 1)
            with pe.Fori(0, 2, 1) as i:
                for e in range(2):
                    t0 = T_POOL + 14 * i + 7 * e
                    n8, n32 = 16 * i + 8 * e, 64 * i + 32 * e
                    for j in range(2):
                        tile_ready(t0 + j)
                        for m in range(2):
                            for n in range(2):
                                b = 4 * j + 2 * m + n
                                pe.wait_ge(y2_added, n32 + b + 9)
                                proj_t(b, (1 + e + j) % 2, m, n, x3_hi, x3_lo).then_inc(pu_full, 1)
                    for j in range(2):
                        tile_ready(t0 + 2 + j)
                        for m in range(2):
                            for n in range(2):
                                b = 4 * j + 2 * m + n
                                pe.wait_ge(pu_taken, n8 + b + 1)
                                proj_t(b, (1 + e + j) % 2, m, n, x3_hi, x3_lo).then_inc(z_full, 1)
                    tile_ready(t0 + 4)
                    s = (1 + e) % 2
                    pe.wait_ge(pm_split, n8 + 8)
                    for n in range(2):
                        for m in range(4):
                            b = 4 * n + m
                            pe.wait_ge(z_taken, n8 + b + 1)
                            ts = slice(n * HALF, (n + 1) * HALF)
                            terms = [(w_hi[s][:, k * 512 + m * P:k * 512 + (m + 1) * P],
                                      w_lo[s][:, k * 512 + m * P:k * 512 + (m + 1) * P],
                                      m_hi[:, k, ts], m_lo[:, k, ts]) for k in range(4)]
                            three(ps[:, b, :], terms).then_inc(grp_full, 1)
                    for r in range(2):
                        tile_ready(t0 + 5 + r)
                        s = (e + r) % 2
                        for t in range(TB):
                            if r == 0 and t % 4 == 0:
                                pe.wait_ge(g_split, n8 + 4 + t)
                            for n in range(2):
                                j = 2 * t + n
                                if r == 0 and j < 8:
                                    pe.wait_ge(gt_ready, n8 + j + 1)
                                else:
                                    pe.wait_ge(y2_added, n32 + 16 + 16 * r + j - 7)
                                terms = []
                                for k in range(2):
                                    ts = slice(t * P, (t + 1) * P)
                                    lo = (g_lo0[:, 2 * r + k, ts] if t < 4
                                          else m_lo[:, 2 * r + k, t * P - HALF:(t + 1) * P - HALF])
                                    c = k * 1024 + n * HALF
                                    terms.append((g_hi[:, 2 * r + k, ts], lo,
                                                  w_hi[s][:, c:c + HALF], w_lo[s][:, c:c + HALF]))
                                three(ps[:, j % 8, :], terms).then_inc(out_full, 1)

        def act_program(act):
            f = nc.scalar.activation
            dma = act.dma_start

            dma(pre_gain[:], a["attn_pre_norm"][0].partition_broadcast(P)).then_inc(pre_gain_in, 16)

            def x_norm(t):
                act.wait_ge(x_in[t], 16)
                act_own.do(act, f(junk0[:], x_nat[:, t, :], ACT.Square, accum_out=stat_a[:, t:t + 1]))
                f(stat_b[:, t:t + 1], stat_a[:, t:t + 1], ACT.Sqrt, bias=EPS, scale=1.0 / D).then_inc(x_sd, 1)

            act.wait_ge(consts, N_CONSTS)
            x_norm(0)
            x_norm(1)
            for t in range(TB):
                if t + 2 < TB:
                    x_norm(t + 2)
                for j in range(2):
                    act.wait_ge(ut_full, 2 * t + j + 1)
                    f(u_hi[:, 4 * j:4 * j + 4, t * P:(t + 1) * P],
                      ps[:, 4 + 2 * (t % 2) + j, :].rearrange("p (k n) -> p k n", k=4), ACT.Copy).then_inc(u_hi_ready, 1)
            act.wait_ge(rot_ang, 1)
            f(rot[0:64, :], ang[0:64, :], ACT.Sin, scale=0.5).then_inc(rot_sin, 1)
            f(rot[64:P, :], ang[64:P, :], ACT.Sin).then_inc(rot_sin, 1)

            def half(n):
                return slice(n * HALF, (n + 1) * HALF)

            for n in range(2):
                for m in range(2):
                    act.wait_ge(in_full, 2 * n + m + 1)
                    f(c_q[:, m, half(n)], ps[:, 2 * n + m, :], ACT.Copy).then_inc(in_taken, 1)
            for n in range(2):
                act.wait_ge(in_full, 5 + n)
                f(c_kv[:, half(n)], ps[:, 4 + n, :], ACT.Copy).then_inc(in_taken, 1)
            for n in range(2):
                act.wait_ge(in_full, 7 + n)
                b = 6 + n
                f(k_pe[0:64, half(n)], ps[0:64, b, :], ACT.Copy)
                f(k_pe[64:96, half(n)], ps[32:64, b, :], ACT.Copy)
                f(k_pe[96:P, half(n)], ps[0:32, b, :], ACT.Copy)
                f(i_row[:, half(n)], ps[64:64 + HEADS, b, :], ACT.Copy)
                f(f_row[:, half(n)], ps[96:96 + HEADS, b, :], ACT.Copy).then_inc(in_taken, 1)
            act.wait_ge(gates_abs, 1)
            act_own.do(act, f(e_row[:], e_row[:], ACT.Exp, scale=-1.0))
            f(e_row[:], e_row[:], ACT.Ln, bias=1.0).then_inc(gates_log, 1)
            act.wait_ge(kpe_prod, 1)
            f(k_tmp[0:64, :], k_pe[64:P, :], ACT.Copy).then_inc(kpe_shift, 1)

            def raw_rows(c):
                for n in range(2):
                    q = 8 + 2 * c + n
                    act.wait_ge(in_full, q + 1)
                    if c >= 2:
                        act.wait_ge(conv_done, c - 1)
                    f(raw[:, c % 2, CONV - 1 + n * HALF:CONV - 1 + (n + 1) * HALF], ps[:, q % 8, :],
                      ACT.Copy).then_inc(in_taken, 1)

            def silu_rows(c):
                act.wait_ge(conv_done, c + 1)
                f(m_qk[:, c, :], m_qk[:, c, :], ACT.Silu).then_inc(silu_done, 1)

            raw_rows(0)
            raw_rows(1)
            act.wait_ge(gates_rows, 1)
            act_own.do(act, f(e_row[:], m_row[:], ACT.Exp, scale=-1.0))
            for j, row in enumerate((b_row, i_row, e_row, m_row)):
                dma(gate_dram[j], row[:]).then_inc(gates_spilled, 16)
            act.wait_ge(kpe_sum, 1)
            f(k_pe[64:P, :], k_pe[0:64, :], ACT.Copy).then_inc(act_head, 1)
            silu_rows(0)
            for c in range(2, 8):
                raw_rows(c)
                silu_rows(c - 1)
            silu_rows(7)
            for j in range(4):
                act.wait_ge(in_full, 24 + j + 1)
                width = QLORA if j < 2 else KVLORA
                sd = sd_q if j < 2 else sd_kv
                f(sd[:, half(j % 2)], ps[:, j, :], ACT.Sqrt, bias=EPS, scale=1.0 / width).then_inc(in_taken, 1)
            act.wait_ge(gates_spilled, 64)
            for c in range(HEADS):
                for n in range(2):
                    q = 28 + 2 * c + n
                    act.wait_ge(in_full, q + 1)
                    f(m_v[:, c, half(n)], ps[:, q % 8, :], ACT.Copy).then_inc(in_taken, 1)
            act.wait_ge(latent_ready, 1)
            for c in range(HEADS):
                for n in range(2):
                    q = 36 + 2 * c + n
                    act.wait_ge(in_full, q + 1)
                    f(mix[:, 4 + c, half(n)], ps[:, q % 8, :], ACT.Sigmoid).then_inc(in_taken, 1)

            act.wait_ge(in_full, 44)
            act.wait_ge(in_taken, 44)
            def head_copies(h, first=False):
                if not first:
                    act.wait_ge(st_ready, 8 * h)
                f(mq_h[:], m_qk[:, bass.ds(h, 1), :], ACT.Copy).then_inc(mqkv_ready, 1)
                f(mk_h[:], m_qk[:, bass.ds(h + 4, 1), :], ACT.Copy, scale=MH_SCALE).then_inc(mqkv_ready, 1)
                f(mv_h[:], m_v[:, bass.ds(h, 1), :], ACT.Copy).then_inc(mqkv_ready, 1)

            def take_queries(h):
                for j in (0, 1):
                    act.wait_ge(up_full, 8 * h + j + 1)
                    f(q_n[:, half(j)], ps[:, j, :], ACT.Copy, scale=QK_SCALE).then_inc(up_taken, 1)

            def take_keys_values(h):
                for j in (0, 1):
                    act.wait_ge(up_full, 8 * h + j + 5)
                    f(k_n[:, half(j)], ps[:, (7, 4)[j], :], ACT.Copy).then_inc(up_taken, 1)
                for j in (0, 1):
                    act.wait_ge(up_full, 8 * h + j + 7)
                    f(v_n[:, 4 * j:4 * j + 4, :], ps[:, 2 + j, :].rearrange("p (t n) -> p t n", t=4),
                      ACT.Copy).then_inc(up_taken, 1)

            def take_chunk_rows(h):
                for j in range(2):
                    act.wait_ge(kv_full, 4 * h + j + 1)
                    f(k_nat[:, 4 * j:4 * j + 4, :], ps[:, j, :].rearrange("p (t n) -> p t n", t=4),
                      ACT.Copy).then_inc(kv_nat, 1)
                for j in range(2):
                    act.wait_ge(kv_full, 4 * h + j + 3)
                    f(vo[:, 4 * j:4 * j + 4, 0:P], ps[:, 6 - j, :].rearrange("p (t n) -> p t n", t=4),
                      ACT.Copy).then_inc(kv_nat, 1)

            def take_probs_t(h, s):
                i = Q_ORDER[s]
                act.wait_ge(pt_full, 8 * h + s + 1)
                if s >= 1:
                    act.wait_ge(o_full, 8 * h + s)
                f(probs_t[:, 0:i + 1, :], psf[:, 1024:1024 + (i + 1) * P].rearrange("p (t n) -> p t n", n=P),
                  ACT.Copy).then_inc(pt_taken, 1)

            def take_out(h, s):
                i = Q_ORDER[s]
                act.wait_ge(o_full, 8 * h + s + 1)
                f(mix[:, bass.ds(h, 1), i * P:(i + 1) * P], ps[:, 4, 0:P], ACT.Copy).then_inc(o_taken, 1)

            def chunk_weights(h, i):
                act.wait_ge(e_ready, 8 * h + i + 1)
                if i >= 2:
                    act.wait_ge(cn_done, 8 * h + i - 1)
                f(d_t[:, i % 2, :], e_buf[:, i % 2, :], ACT.Exp).then_inc(dt_ready, 1)
                f(inter[:, i % 2, :], r_b[:, i * P:(i + 1) * P], ACT.Exp, bias=m_prev[:, i:i + 1]).then_inc(ib_ready, 1)

            def row_squares(h, i):
                act.wait_ge(num_taken, 8 * h + i + 1)
                return f(sink[:], h_nat[:, i, 0:P], ACT.Square, accum_out=var8[:, i:i + 1])

            def head_steps(h):
                chunk_weights(h, 0)
                for s in range(TB):
                    w, i = s % 2, Q_ORDER[s]
                    act.wait_ge(dt_ready, 8 * h + s + 1)
                    if s >= 2:
                        act.wait_ge(cn_full, 8 * h + s - 1)
                    f(k_w[:, w, :], k_nat[:, s, :], ACT.Copy, scale=d_t[:, w, P - 1:P]).then_inc(kw_ready, 1)
                    if s >= 1:
                        take_probs_t(h, s - 1)
                    act.wait_ge(nm_ready, 8 * h + s + 1)
                    if s >= 2:
                        act.wait_ge(pt_full, 8 * h + s - 1)
                    o = score_bank(i)
                    f(probs[:, w, 0:(i + 1) * P], psf[:, o:o + (i + 1) * P], ACT.Exp, bias=neg_max[:, i:i + 1],
                      accum_out=row_sum[:, i:i + 1]).then_inc(probs_done, 1)
                    if s + 1 < TB:
                        chunk_weights(h, s + 1)
                    if s >= 1:
                        take_out(h, s - 1)
                        act_own.mark(row_squares(h, s - 1))
                        act_own.wait(act)

            def finish_head(h):
                act.wait_ge(hvar_ready, h + 1)
                f(sd8, var8, ACT.Sqrt, bias=EPS, scale=1.0 / P).then_inc(act_head, 1)

            act.wait_ge(dve_head, 1)
            head_copies(0, first=True)
            take_queries(0)
            take_keys_values(0)
            take_chunk_rows(0)
            own_start = act_own.at
            with act.Fori(0, HEADS - 1, 1) as h:
                act_own.at = own_start + (TB - 1) * h
                head_steps(h)
                head_copies(h + 1)
                take_queries(h + 1)
                take_probs_t(h, TB - 1)
                row_squares(h, TB - 1).then_inc(hsq_ready, 1)
                take_out(h, TB - 1)
                finish_head(h)
                take_keys_values(h + 1)
                take_chunk_rows(h + 1)
            act_own.at = own_start + (TB - 1) * (HEADS - 1)
            head_steps(HEADS - 1)
            take_probs_t(HEADS - 1, TB - 1)
            row_squares(HEADS - 1, TB - 1).then_inc(hsq_ready, 1)
            take_out(HEADS - 1, TB - 1)
            finish_head(HEADS - 1)

            act.wait_ge(dve_head, HEADS + 1)

            def take_f(t):
                for j in range(2):
                    act.wait_ge(ft_full, 2 * t + j + 1)
                    f(f_hi[:, 4 * j:4 * j + 4, t * P:(t + 1) * P],
                      ps[:, 4 + 2 * (t % 2) + j, :].rearrange("p (k n) -> p k n", k=4),
                      ACT.Copy).then_inc(f_hi_ready, 1)

            for t in range(TB):
                b = 2 * (t % 2)
                act.wait_ge(mix_full, 2 * t + 2)
                if t >= 1:
                    act.wait_ge(h1_spilled, 16 * t)
                    act.wait_ge(f_ready, t)
                act_own.do(act, f(h1_blk[:], psf[:, b * HALF:(b + 2) * HALF], ACT.Square,
                                  accum_out=stat_a[:, t:t + 1]))
                f(stat_b[:, t:t + 1], stat_a[:, t:t + 1], ACT.Sqrt, bias=EPS, scale=1.0 / D).then_inc(sd1_ready, 1)
                act.wait_ge(h1_ready, t + 1)
                if t >= 1:
                    act.wait_ge(ft_full, 2 * t)
                act_own.do(act, f(f_blk[:], h1_blk[:], ACT.Square, accum_out=stat_c[:, t:t + 1]))
                f(stat_d[:, t:t + 1], stat_c[:, t:t + 1], ACT.Sqrt, bias=EPS, scale=1.0 / D).then_inc(sd2_ready, 1)
                if t >= 1:
                    take_f(t - 1)
            take_f(TB - 1)

            with act.Fori(0, FG, 1) as g:
                for b in range(4):
                    act.wait_ge(gate_full, 4 * g + b + 1)
                    act.wait_ge(hid_ready, 4 * g + b + 1)
                    f(silu_g[:, b, :], ps[:, b, :], ACT.Silu).then_inc(silu_ready, 1)
                act.wait_ge(y_added, 16 * g + 16)
                for b in range(4):
                    m, n = b % 2, b // 2
                    act.wait_ge(hid_ready, 4 * g + b + 5)
                    f(hid_hi[:, m, half(n)], hid[:, b % 2, :], ACT.Copy).then_inc(hid_hi_ready, 1)

            for j in range(4):
                act.wait_ge(pt2_full, j + 1)
                f(p_hi[:, j // 2, half(j % 2)], ps[:, j, :], ACT.Copy).then_inc(p_hi_ready, 1)

            def h2_norm(t):
                act.wait_ge(y_added, 16 * FG + 2 * t + 2)
                if t == 0:
                    act.wait_ge(down_full, 16 * FG)
                act_own.do(act, f(junk2[:], y[:, t, :], ACT.Square, accum_out=stat_a[:, t:t + 1]))
                f(stat_b[:, t:t + 1], stat_a[:, t:t + 1], ACT.Sqrt, bias=EPS, scale=1.0 / D).then_inc(h2_sd, 1)

            for t in range(TB):
                h2_norm(t)
                for n in range(2):
                    j = 2 * t + n
                    act.wait_ge(pp_full, j + 1)
                    f(pp[:, t, half(n)], ps[:, j % 8, :], ACT.Copy).then_inc(pp_taken, 1)
            for t in range(TB):
                for j in range(2):
                    act.wait_ge(h2t_full, 2 * t + j + 1)
                    f(h2_hi[:, 4 * j:4 * j + 4, t * P:(t + 1) * P],
                      ps[:, 2 * (t % 4) + j, :].rearrange("p (k n) -> p k n", k=4),
                      ACT.Copy).then_inc(h2_hi_ready, 1)
            act.wait_ge(h2_ready, TB)

            def x3_part(j):
                act.wait_ge(x3_ready, j + 1)
                m, n = 2 * (j // 4) + j % 2, (j // 2) % 2
                f(x3_hi[:, m, half(n)], x3[:, j % 2, :], ACT.Copy).then_inc(x3_hi_ready, 1)

            for j in range(16):
                act.wait_ge(pg_full, j + 1)
                if j >= 2:
                    act.wait_ge(x3_ready, j - 1)
                f(sig[:, j % 2, :], ps[:, j % 8, :], ACT.Sigmoid).then_inc(sig_ready, 1)
                if j >= 1:
                    x3_part(j - 1)
            x3_part(15)

            with act.Fori(0, GROUPS, 1) as g:
                n8 = 8 * g
                for j in range(8):
                    n = j % 2
                    act.wait_ge(pu_full, n8 + j + 1)
                    act.wait_ge(pm_ready, n8 + j + 1)
                    f(u_buf[:, n, HALO:W1], ps[:, j, :], ACT.Copy).then_inc(pu_taken, 1)
                    if j >= 1:
                        act.wait_ge(pm_ready, n8 + j + 2)
                        f(m_hi[:, (j - 1) // 2, half((j - 1) % 2)], win[:, 0, HALO:W1], ACT.Copy).then_inc(pm_hi_ready, 1)
                act.wait_ge(pm_ready, n8 + 10)
                f(m_hi[:, 3, half(1)], win[:, 0, HALO:W1], ACT.Copy).then_inc(pm_hi_ready, 1)
                act.wait_ge(out_full, 32 * g + 16)
                for j in range(8):
                    act.wait_ge(z_full, n8 + j + 1)
                    f(z[:, j // 2, half(j % 2)], ps[:, j, :], ACT.Silu).then_inc(z_taken, 1)
                for j in range(8):
                    m, n = j % 4, j // 4
                    act.wait_ge(gt_ready, n8 + j + 1)
                    f(g_hi[:, m, half(n)], gt[:], ACT.Copy).then_inc(g_hi_ready, 1)
            for t in range(TB):
                act.wait_ge(ln_mean, t + 1)
                act_own.do(act, f(ln_sink[:], y2[:, t, :], ACT.Square, bias=neg_mean[:, t:t + 1],
                                  accum_out=stat_a[:, t:t + 1]))
                f(stat_b[:, t:t + 1], stat_a[:, t:t + 1], ACT.Sqrt, bias=LN_EPS, scale=1.0 / D).then_inc(ln_sd, 1)
                act.wait_ge(ln_shift, t + 1)
                f(y2[:, t, :], y2[:, t, :], ACT.Identity, bias=shift[:, t:t + 1],
                  scale=stat_c[:, t:t + 1]).then_inc(ln_normed, 1)

        def dve_program(dve):
            v = nc.vector
            own = dve_own

            def half(n):
                return slice(n * HALF, (n + 1) * HALF)

            def x_scale(t):
                dve.wait_ge(x_sd, t + 1)
                own.do(dve, v.reciprocal(stat_c[:, t:t + 1], stat_b[:, t:t + 1]))
                v.scalar_tensor_tensor(x_nat[:, t, :], x_nat[:, t, :], stat_c[:, t:t + 1], pre_gain[:],
                                       ALU.mult, ALU.mult).then_inc(xn_ready, 1)

            dve.wait_ge(pre_gain_in, 16)
            x_scale(0)
            x_scale(1)
            for t in range(TB):
                if t + 2 < TB:
                    x_scale(t + 2)
                for j in range(2):
                    dve.wait_ge(u_hi_ready, 2 * t + j + 1)
                    ts = slice(t * P, (t + 1) * P)
                    v.tensor_tensor(u_lo[:, 4 * j:4 * j + 4, ts],
                                    ps[:, 4 + 2 * (t % 2) + j, :].rearrange("p (k n) -> p k n", k=4),
                                    u_hi[:, 4 * j:4 * j + 4, ts].bitcast(F32), ALU.subtract).then_inc(u_split, 1)
            dve.wait_ge(pos_in, 32)
            dve.wait_ge(consts, N_CONSTS)
            own.do(dve, v.tensor_copy(ang[:], pos_i[:]))
            own.do(dve, v.tensor_scalar(ang[:], ang[:], inv_freq, None, ALU.mult))
            own.do(dve, v.tensor_scalar(turns[:], ang[:], 1.0 / (2.0 * 3.141592653589793), ROUND, ALU.mult, ALU.add))
            own.do(dve, v.tensor_scalar(turns[:], turns[:], ROUND, None, ALU.subtract))
            for part in (TWO_PI_A, TWO_PI_B, TWO_PI_C):
                own.do(dve, v.scalar_tensor_tensor(ang[:], turns[:], -part, ang[:], ALU.mult, ALU.add))
            v.tensor_scalar(ang[:], ang[:], PI_SAFE, -PI_SAFE, ALU.min, ALU.max).then_inc(rot_ang, 1)
            dve.wait_ge(rot_sin, 2)
            own.do(dve, v.tensor_tensor(rot[0:64, :], rot[0:64, :], rot[0:64, :], ALU.mult))
            own.do(dve, v.tensor_scalar(rot[0:64, :], rot[0:64, :], -2.0, 1.0, ALU.mult, ALU.add))
            own.do(dve, v.tensor_scalar(rot[64:P, :], rot[64:P, :], sin_sign[64:P, :], None, ALU.mult))

            dve.wait_ge(in_taken, 4)
            for m in range(2):
                own.do(dve, v.tensor_tensor(sq[:, m, :], c_q[:, m, :], c_q[:, m, :], ALU.mult))
            own.mark(v.tensor_tensor(sq[:, 0, :], sq[:, 0, :], sq[:, 1, :], ALU.add))
            own.wait(dve)
            v.memset(raw[:, :, 0:CONV - 1], 0.0).then_inc(sq_ready, 1)
            dve.wait_ge(in_taken, 6)
            v.tensor_tensor(sq[:, 1, :], c_kv[:], c_kv[:], ALU.mult).then_inc(sq_ready, 1)
            dve.wait_ge(in_taken, 8)
            dve.wait_ge(cols_in, 16 * (6 + CONV))
            own.do(dve, v.tensor_scalar(f_row[:], f_row[:], gate_bias[0:HEADS, 1:2], None, ALU.add))
            v.scalar_tensor_tensor(e_row[:], f_row[:], -1.0, f_row[:], ALU.mult, ALU.max).then_inc(gates_abs, 1)
            own.mark(v.tensor_scalar(i_row[:], i_row[:], gate_bias[0:HEADS, 0:1], None, ALU.add))
            v.tensor_tensor(k_pe[:], k_pe[:], rot[:], ALU.mult).then_inc(kpe_prod, 1)
            dve.wait_ge(gates_log, 1)
            own.do(dve, v.scalar_tensor_tensor(f_row[:], f_row[:], 0.0, e_row[:], ALU.min, ALU.subtract))
            for c in range(TB):
                cs = slice(c * P, (c + 1) * P)
                own.mark(v.tensor_tensor_scan(b_row[:, cs], ones[0:HEADS, :], f_row[:, cs], 0.0, ALU.mult, ALU.add))
            own.do(dve, v.tensor_tensor_scan(m_row[:], f_row[:], i_row[:], 0.0, ALU.add, ALU.max))
            own.do(dve, v.tensor_tensor(i_row[:], i_row[:], b_row[:], ALU.subtract))
            v.tensor_tensor(b_row[:], b_row[:], m_row[:], ALU.subtract).then_inc(gates_rows, 1)
            dve.wait_ge(kpe_shift, 1)
            v.tensor_tensor(k_pe[0:64, :], k_pe[0:64, :], k_tmp[0:64, :], ALU.add).then_inc(kpe_sum, 1)

            for c in range(8):
                dve.wait_ge(in_taken, 8 + 2 * c + 2)
                rows, o = raw[:, c % 2, :], m_qk[:, c, :]
                own.do(dve, v.tensor_scalar(o, rows[:, 0:S], conv_w[:, c, 0:1], conv_b[:, c:c + 1], ALU.mult, ALU.add))
                for j in range(1, CONV):
                    ins = v.scalar_tensor_tensor(o, rows[:, j:j + S], conv_w[:, c, j:j + 1], o, ALU.mult, ALU.add)
                    if j < CONV - 1:
                        own.do(dve, ins)
                    else:
                        ins.then_inc(conv_done, 1)
            dve.wait_ge(in_taken, 26)
            own.do(dve, v.reciprocal(sd_q[:], sd_q[:]))
            for m in range(2):
                own.mark(v.scalar_tensor_tensor(c_q[:, m, :], c_q[:, m, :], q_gain[:, m:m + 1], sd_q[:],
                                                ALU.mult, ALU.mult))
            dve.wait_ge(in_taken, 28)
            own.do(dve, v.reciprocal(sd_kv[:], sd_kv[:]))
            v.scalar_tensor_tensor(c_kv[:], c_kv[:], kv_gain, sd_kv[:], ALU.mult, ALU.mult).then_inc(latent_ready, 1)

            dve.wait_ge(in_full, 44)
            v.memset(vo[:, :, P:P + 1], 1.0).then_inc(dve_head, 1)
            def rotary_queries(h):
                for n in range(2):
                    dve.wait_ge(up_full, 8 * h + 3 + n)
                    own.mark(v.tensor_scalar(q_pe[0:64, half(n)], ps[0:64, 6 - n, :], QK_SCALE, None, ALU.mult))
                    own.mark(v.tensor_scalar(q_pe[64:96, half(n)], ps[32:64, 6 - n, :], QK_SCALE, None, ALU.mult))
                    own.mark(v.tensor_scalar(q_pe[96:P, half(n)], ps[0:32, 6 - n, :], QK_SCALE, None, ALU.mult))
                own.wait(dve)
                v.tensor_tensor(q_pe[:], q_pe[:], rot[:], ALU.mult).then_inc(qp_ready, 1)

            def chunk_exponents(h, i):
                if i >= 2:
                    dve.wait_ge(dt_ready, 8 * h + i - 1)
                v.scalar_tensor_tensor(e_buf[:, i % 2, :], r_b[:, i * P:(i + 1) * P], u_col[:, i:i + 1], causal_t[:],
                                       ALU.add, ALU.add).then_inc(e_ready, 1)

            def head_steps(h):
                dve.wait_ge(head_g, 48 * h + 48)
                chunk_exponents(h, 0)
                for s in range(TB):
                    w, i = s % 2, Q_ORDER[s]
                    cs, wide, o = slice(s * P, (s + 1) * P), (i + 1) * P, score_bank(i)
                    dve.wait_ge(st_full, 8 * h + s + 1)
                    dve.wait_ge(dt_ready, 8 * h + s + 1)
                    if s >= 2:
                        dve.wait_ge(num_full, 8 * h + s - 1)
                    weigh = v.tensor_tensor(s_t[:, w, :], ps[:, 5, 0:P], d_t[:, w, :], ALU.mult)
                    if s >= 1:
                        own.mark(weigh)
                        dve.wait_ge(ib_ready, 8 * h + s + 1)
                        weigh = v.tensor_tensor(q_in[:, w, :], mq_h[:, cs], inter[:, w, :], ALU.mult)
                    weigh.then_inc(st_ready, 1)
                    dve.wait_ge(s_full, 8 * h + s + 1)
                    own.do(dve, v.tensor_tensor(psf[:, o + i * P:o + wide], psf[:, o + i * P:o + wide], causal[:], ALU.add))
                    v.tensor_reduce(neg_max[:, i:i + 1], psf[:, o:o + wide], AX.X, ALU.max, negate=True).then_inc(nm_ready, 1)
                    if s + 1 < TB:
                        chunk_exponents(h, s + 1)
                    dve.wait_ge(probs_done, 8 * h + s + 1)
                    own.do(dve, v.reciprocal(row_inv[:, i:i + 1], row_sum[:, i:i + 1]))
                    v.tensor_scalar(probs[:, w, 0:wide], probs[:, w, 0:wide], row_inv[:, i:i + 1], None,
                                    ALU.mult).then_inc(p_ready, 1)
                    dve.wait_ge(cn_full, 8 * h + s + 1)
                    v.tensor_copy(h_nat[:, s, :], ps[:, 7, 0:P + 1]).then_inc(num_taken, 1)
                    if s == 0:
                        v.tensor_copy(state[:], ps[:, 7, 2 * P:3 * P + 1]).then_inc(cn_done, 1)
                    else:
                        dve.wait_ge(cn_done, 8 * h + s)
                        v.scalar_tensor_tensor(state[:], state[:], inter[:, w, P - 1:P], ps[:, 7, 2 * P:3 * P + 1],
                                               ALU.mult, ALU.add).then_inc(cn_done, 1)

            def head_sums(h):
                dve.wait_ge(num_taken, 8 * h + 8)
                dve.wait_ge(heads_in, 32)
                own.do(dve, v.scalar_tensor_tensor(den, h_nat[:, :, P], -1.0, h_nat[:, :, P], ALU.mult, ALU.max))
                own.do(dve, v.tensor_tensor(den, den, floor_col[:, bass.ds(8 * h, TB)], ALU.max))
                own.do(dve, v.reciprocal(den_inv, den))
                dve.wait_ge(hsq_ready, h + 1)
                own.do(dve, v.tensor_tensor(var8, var8, den_inv, ALU.mult))
                v.tensor_tensor(var8, var8, den_inv, ALU.mult).then_inc(hvar_ready, 1)

            def finish_head(h):
                dve.wait_ge(act_head, h + 2)
                own.do(dve, v.reciprocal(rs8, sd8))
                own.do(dve, v.tensor_tensor(h_scale, rs8, den_inv, ALU.mult))
                scale = h_scale.rearrange("p (t n) -> p t n", n=1).to_broadcast([P, TB, P])
                v.tensor_tensor(h_nat[:, :, 0:P], h_nat[:, :, 0:P], scale, ALU.mult).then_inc(hs_ready, 1)
                for n in range(2):
                    dve.wait_ge(ht_full, 2 * h + n + 1)
                    rows = mix[:, bass.ds(h + 4, 1), half(n)].rearrange("p a n -> p (a n)")
                    ins = v.scalar_tensor_tensor(rows, ps[:, 2 + n, :], head_gain[:, bass.ds(h, 1)], rows, ALU.mult, ALU.mult)
                    if n == 0:
                        own.mark(ins)
                    else:
                        ins.then_inc(dve_head, 1)

            def split_mix(t, e):
                k, rows = slice(4 * e, 4 * e + 4), mix[:, :, t * P:(t + 1) * P]
                if t >= 2 and e == 0:
                    dve.wait_ge(mix_full, 2 * t - 2)
                own.do(dve, v.tensor_copy(mix_hi[t % 2][:, k, :], rows[:, k, :]))
                v.tensor_tensor(mix_lo[t % 2][:, k, :], rows[:, k, :], mix_hi[t % 2][:, k, :].bitcast(F32),
                                ALU.subtract).then_inc(msplit_ready, 1)

            rotary_queries(0)
            start = own.at
            with dve.Fori(0, HEADS - 1, 1) as h:
                own.at = start + OWN_HEAD * h
                head_steps(h)
                head_sums(h)
                rotary_queries(h + 1)
                finish_head(h)
            own.at = start + OWN_HEAD * (HEADS - 1)
            head_steps(HEADS - 1)
            head_sums(HEADS - 1)
            dve.wait_ge(o_taken, 8 * (HEADS - 1) + 1)
            dve.wait_ge(mqkv_ready, 3 * HEADS)
            split_mix(0, 0)
            finish_head(HEADS - 1)

            dve.wait_ge(o_taken, 8 * HEADS)
            dve.wait_ge(dve_head, HEADS + 1)
            dve.wait_ge(gains_in, 32)

            def split_f(t):
                for j in range(2):
                    dve.wait_ge(f_hi_ready, 2 * t + j + 1)
                    ts = slice(t * P, (t + 1) * P)
                    v.tensor_tensor(f_lo[:, 4 * j:4 * j + 4, ts],
                                    ps[:, 4 + 2 * (t % 2) + j, :].rearrange("p (k n) -> p k n", k=4),
                                    f_hi[:, 4 * j:4 * j + 4, ts].bitcast(F32), ALU.subtract).then_inc(f_split, 1)

            split_mix(0, 1)
            split_mix(1, 0)
            split_mix(1, 1)
            for t in range(TB):
                b = 2 * (t % 2)
                dve.wait_ge(sd1_ready, t + 1)
                own.do(dve, v.reciprocal(stat_e[:, t:t + 1], stat_b[:, t:t + 1]))
                v.scalar_tensor_tensor(h1_blk[:], psf[:, b * HALF:(b + 2) * HALF], stat_e[:, t:t + 1], post_gain[:],
                                       ALU.mult, ALU.mult).then_inc(mix_taken, 1)
                dve.wait_ge(mix_taken, t + 1)
                dve.wait_ge(xblk_in, 16 * t + 16)
                v.tensor_tensor(h1_blk[:], h1_blk[:], x_blk[:], ALU.add).then_inc(h1_ready, 1)
                if t + 2 < TB:
                    split_mix(t + 2, 0)
                    split_mix(t + 2, 1)
                if t == TB - 2:
                    dve.wait_ge(msplit_ready, 2 * TB)
                    for j in range(16):
                        v.memset(y[:, j // 2, half(j % 2)], 0.0).then_inc(y_added, 1)
                dve.wait_ge(sd2_ready, t + 1)
                own.do(dve, v.reciprocal(stat_f[:, t:t + 1], stat_d[:, t:t + 1]))
                v.scalar_tensor_tensor(f_blk[:], h1_blk[:], stat_f[:, t:t + 1], ffn_gain[:],
                                       ALU.mult, ALU.mult).then_inc(f_ready, 1)
                if t >= 1:
                    split_f(t - 1)
            split_f(TB - 1)

            dve.wait_ge(f_ready, TB)
            for j in range(4):
                v.memset(hid[:, 0, j:j + 1], 0.0).then_inc(hid_ready, 1)
            dve.wait_ge(hid_ready, 4)
            start = own.at
            with dve.Fori(0, FG, 1) as g:
                for b in range(4):
                    m, n = b % 2, b // 2
                    dve.wait_ge(up2_full, 4 * g + b + 1)
                    dve.wait_ge(silu_ready, 4 * g + b + 1)
                    v.tensor_tensor(hid[:, b % 2, :], ps[:, 4 + b, :], silu_g[:, b, :], ALU.mult).then_inc(hid_ready, 1)
                    dve.wait_ge(hid_hi_ready, 4 * g + b + 1)
                    v.tensor_tensor(hid_lo[:, m, half(n)], hid[:, b % 2, :], hid_hi[:, m, half(n)].bitcast(F32),
                                    ALU.subtract).then_inc(hid_split, 1)
                for j in range(16):
                    dve.wait_ge(down_full, 16 * g + j + 1)
                    rows = y[:, j // 2, half(j % 2)]
                    v.tensor_tensor(rows, ps[:, j % 8, :], rows, ALU.add).then_inc(y_added, 1)

            for j in range(4):
                dve.wait_ge(p_hi_ready, j + 1)
                o = (slice(None), j // 2, half(j % 2))
                v.tensor_tensor(p_lo[o], ps[:, j, :], p_hi[o].bitcast(F32), ALU.subtract).then_inc(p_split, 1)
            dve.wait_ge(fpg_in, 16)
            for t in range(TB):
                dve.wait_ge(h2_sd, t + 1)
                own.do(dve, v.reciprocal(stat_c[:, t:t + 1], stat_b[:, t:t + 1]))
                own.do(dve, v.scalar_tensor_tensor(y[:, t, :], y[:, t, :], stat_c[:, t:t + 1], ffn_post_gain[:],
                                                   ALU.mult, ALU.mult))
                dve.wait_ge(h1_back[t % 3], 16 * (t // 3) + 16)
                v.tensor_tensor(y[:, t, :], y[:, t, :], h1_in[t % 3][:], ALU.add).then_inc(h2_ready, 1)
            for t in range(TB):
                for j in range(2):
                    dve.wait_ge(h2_hi_ready, 2 * t + j + 1)
                    ts = slice(t * P, (t + 1) * P)
                    v.tensor_tensor(h2_lo[:, 4 * j:4 * j + 4, ts],
                                    ps[:, 2 * (t % 4) + j, :].rearrange("p (k n) -> p k n", k=4),
                                    h2_hi[:, 4 * j:4 * j + 4, ts].bitcast(F32), ALU.subtract).then_inc(h2_split, 1)
            for j in range(16):
                m, n = 2 * (j // 4) + j % 2, (j // 2) % 2
                o = (slice(None), m, half(n))
                dve.wait_ge(sig_ready, j + 1)
                if j >= 2:
                    dve.wait_ge(x3_hi_ready, j - 1)
                t = x3[:, j % 2, :]
                own.do(dve, v.tensor_tensor(t, sig[:, j % 2, :], pp[o], ALU.mult))
                own.do(dve, v.tensor_tensor(t, t, h2_lo[o].bitcast(F32), ALU.add))
                v.tensor_tensor(t, t, h2_hi[o].bitcast(F32), ALU.add).then_inc(x3_ready, 1)
                dve.wait_ge(x3_hi_ready, j + 1)
                v.tensor_tensor(x3_lo[o], t, x3_hi[o].bitcast(F32), ALU.subtract).then_inc(x3_split, 1)

            def row_mean(t):
                dve.wait_ge(y2_added, 16 + 32 * (GROUPS - 1) + 16 + 2 * t + 2)
                own.do(dve, v.tensor_tensor(neg_mean[:, t:t + 1], row_sums[:, 2 * t:2 * t + 1],
                                            row_sums[:, 2 * t + 1:2 * t + 2], ALU.add))
                v.tensor_scalar(neg_mean[:, t:t + 1], neg_mean[:, t:t + 1], -1.0 / D, None, ALU.mult).then_inc(ln_mean, 1)
                dve.wait_ge(ln_sd, t + 1)
                own.do(dve, v.reciprocal(stat_c[:, t:t + 1], stat_b[:, t:t + 1]))
                v.tensor_tensor(shift[:, t:t + 1], neg_mean[:, t:t + 1], stat_c[:, t:t + 1], ALU.mult).then_inc(ln_shift, 1)

            def add_bias(t):
                if t == 0:
                    dve.wait_ge(ln_in, 32)
                if t < TB - 1:
                    dve.wait_ge(ln_gained, t + 1)
                else:
                    dve.wait_ge(ln_normed, t + 1)
                    own.do(dve, v.tensor_tensor(y2[:, t, :], y2[:, t, :], ln_gain[:], ALU.mult))
                v.tensor_tensor(y2[:, t, :], y2[:, t, :], ln_bias[:], ALU.add).then_inc(out_ready, 1)

            for j in range(16):
                dve.wait_ge(out_full, j + 1)
                v.tensor_scalar(y2[:, j // 2, half(j % 2)], ps[:, j % 8, :], ALPHA, None, ALU.mult).then_inc(y2_added, 1)
            dve.wait_ge(x3_split, 16)
            v.memset(u_buf[:, 0, 0:HALO], 0.0).then_inc(pm_ready, 1)
            v.memset(u_buf[:, 1, 0:HALO], 0.0).then_inc(pm_ready, 1)
            dve.wait_ge(pm_ready, 2)
            for g, width in enumerate(WINDOWS):
                n8 = 8 * g
                for j in range(8):
                    n, m = j % 2, j // 2
                    dve.wait_ge(pu_taken, n8 + j + 1)
                    u = u_buf[:, n, :]
                    if n == 0:
                        own.do(dve, v.tensor_copy(u_buf[:, 1, 0:HALO], u[:, HALF:W1]))
                    if n8 + j >= 1:
                        dve.wait_ge(pm_split, n8 + j)
                    src, reach, steps = u, 1, g + 1
                    for step in range(steps):
                        dst = win[:, (steps - step) % 2, :]
                        own.do(dve, v.tensor_tensor(dst[:, reach * 2 - 1:W1], src[:, reach * 2 - 1:W1],
                                                    src[:, reach - 1:W1 - reach], ALU.add))
                        src, reach = dst, reach * 2
                    ins = v.scalar_tensor_tensor(win[:, 0, HALO:W1], src[:, HALO:W1], 1.0 / width, u[:, HALO:W1],
                                                 ALU.mult, ALU.subtract)
                    if n == 0:
                        own.do(dve, ins)
                        first = slice(HALO, HALO + width)
                        own.do(dve, v.tensor_tensor(win[:, 0, first], src[:, first], inv_count[:, 0:width], ALU.mult))
                        ins = v.tensor_tensor(win[:, 0, first], win[:, 0, first], u[:, first], ALU.subtract)
                    ins.then_inc(pm_ready, 1)
                    dve.wait_ge(pm_hi_ready, n8 + j + 1)
                    o = (slice(None), m, half(n))
                    v.tensor_tensor(m_lo[o], win[:, 0, HALO:W1], m_hi[o].bitcast(F32), ALU.subtract).then_inc(pm_split, 1)
                for j in range(8):
                    m, n = j % 4, j // 4
                    dve.wait_ge(grp_full, n8 + j + 1)
                    dve.wait_ge(z_taken, n8 + 2 * m + n + 1)
                    if n8 + j >= 1:
                        dve.wait_ge(g_split, n8 + j)
                    v.scalar_tensor_tensor(gt[:], ps[:, j, :], pool_gain[:, 4 * g + m:4 * g + m + 1], z[:, m, half(n)],
                                           ALU.mult, ALU.mult).then_inc(gt_ready, 1)
                    dve.wait_ge(g_hi_ready, n8 + j + 1)
                    lo = g_lo0[:, m, :] if n == 0 else m_lo[:, m, 0:HALF]
                    v.tensor_tensor(lo, gt[:], g_hi[:, m, half(n)].bitcast(F32), ALU.subtract).then_inc(g_split, 1)
                for j in range(32):
                    q = 32 * g + j
                    dve.wait_ge(out_full, 16 + q + 1)
                    rows = y2[:, (j % 16) // 2, half(j % 2)]
                    if j >= 16 or g >= 1:
                        dve.wait_ge(y2_added, q + 1)
                    if g < GROUPS - 1 or j < 16:
                        v.tensor_tensor(rows, ps[:, j % 8, :], rows, ALU.add).then_inc(y2_added, 1)
                        continue
                    v.scalar_tensor_tensor(rows, ps[:, j % 8, :], 1.0, rows, ALU.mult, ALU.add,
                                           accum_out=row_sums[:, j - 16:j - 15]).then_inc(y2_added, 1)
                    t = (j - 16) // 2
                    if j % 2 == 1:
                        row_mean(t)
                        if t >= 1:
                            add_bias(t - 1)
            add_bias(TB - 1)

        N_CONSTS = 11 + HALO
        OWN_HEAD = 6 + 8 + 7 + 8 + 4 + 2 + 1

        block = ctx.enter_context(nc.Block())

        @block.sync
        def _(sp):
            sp_program(sp)

        @block.gpsimd
        def _(pool):
            pool_program(pool)

        @block.tensor
        def _(pe):
            pe_program(pe)

        @block.scalar
        def _(act):
            act_program(act)

        @block.vector
        def _(dve):
            dve_program(dve)


_INS = ["x", "p", "positions", "attn_pre_norm", "attn_post_norm", "w_in", "q_norm", "kv_norm", "w_uq", "w_ukv",
        "conv_w", "conv_b", "gate_bias_i", "gate_bias_f", "mlstm_norm", "w_out", "ffn_pre_norm", "ffn_post_norm",
        "w_gate", "w_up", "w_down", "w_ple_proj", "w_ple_gate", "ln_g_2", "ln_b_2", "pool_w_in_2", "pool_w_grp_2",
        "pool_scale_2", "pool_w_out_2"]


def kernel(**inputs):
    import numpy as _np
    import concourse.bacc as _bacc
    from concourse import mybir as _mybir
    from concourse.bass_utils import run_bass_kernel_spmd as _run

    nc = _bacc.Bacc("TRN2", target_bir_lowering=False, num_devices=1)
    arrays, aps = {}, {}
    given = {name: _np.ascontiguousarray(inputs[name]) for name in _INS}
    freq = _np.float32(10000.0) ** (-_np.arange(0, ROPE, 2, dtype=_np.float32) / _np.float32(ROPE))
    given["inv_freq"] = _np.ascontiguousarray(_np.tile(freq.astype(_np.float32), 4)[:, None])
    for name, x in given.items():
        arrays[f"in_{name}"] = x
        aps[name] = nc.dram_tensor(f"in_{name}", x.shape, _mybir.dt.from_np(x.dtype), kind="ExternalInput").ap()
    out = nc.dram_tensor("out_0", (1, S, D), _mybir.dt.float32, kind="ExternalOutput").ap()
    build(nc, aps, out)
    r = _run(nc, [arrays], core_ids=[0])
    return r.results[0]["out_0"]
```

```python
from contextlib import ExitStack

import concourse.bass as bass
from concourse import mybir

F32 = mybir.dt.float32
F32R = mybir.dt.float32r
I32 = mybir.dt.int32
ACT = mybir.ActivationFunctionType
ALU = mybir.AluOpType
AX = mybir.AxisListType

P = 128
S = 1024
D = 1024
HALF = 512
TB = S // P
KD = D // P
EPS = 1e-6
LN_EPS = 1e-5
NEG = -1e30

Q_ORDER = (0, 7, 3, 6, 2, 5, 1, 4)
PLE = 256
HEADS = 4
NOPE, ROPE, VH = 128, 64, 128
QLORA, KVLORA = 256, 128
QK_SCALE = float(NOPE + ROPE) ** -0.5
MH_SCALE = 128.0 ** -0.5
CONV = 4
DFF = 2816
FG = DFF // 256
DP = 2048
GROUPS = 4
GW = DP // GROUPS
WINDOWS = (2, 4, 8, 16)
HALO = 16
ALPHA = 2.0 ** 0.25
LN_LAST = 2
H2_AFTER = {5: 2, 6: 3, 8: 4, 10: 5, 12: 6, 13: 7}
STORE_ORDER = (0, 1, 2, 3, 4, 6, 7, 5)
POOL_BIAS = (1, 3, 4, 5)

KB = 1024
PI_SAFE = 3.1415925
TWO_PI_A = 6.28125
TWO_PI_B = 0.0019350051879882812
TWO_PI_C = 2.0 * 3.141592653589793 - TWO_PI_A - TWO_PI_B
SMALL = {"allow_slow_non_contiguous": True}
ROUND = 12582912.0


class Chain:

    def __init__(self, sem):
        self.sem, self.at = sem, 0

    def mark(self, instruction):
        instruction.then_inc(self.sem, 1)
        self.at = self.at + 1

    def wait(self, engine):
        engine.wait_ge(self.sem, self.at)

    def do(self, engine, instruction):
        self.mark(instruction)
        self.wait(engine)


def build(nc, a, out):
    ctx = ExitStack()
    with ctx:
        def sem(name):
            return ctx.enter_context(nc.semaphore(name))

        ARENA = 200 * KB + 8000
        base = 16512
        ctx.enter_context(nc.sbuf_tensor("arena", [P, ARENA // 4], F32))

        def at(name, shape, offset, dt=F32):
            return nc.alloc_sbuf_tensor_at(name, shape, dt, offset=base + offset)

        A, B, C, E, M = 56 * KB, 120 * KB, 152 * KB, 184 * KB, 200 * KB
        SLOT = [0, 16 * KB, 32 * KB, C, C + 16 * KB]
        S2 = SLOT[2]
        w_hi = [at(f"w_hi{s}", [P, 2048], SLOT[s], F32R) for s in range(5)]
        w_lo = [at(f"w_lo{s}", [P, 2048], SLOT[s] + 8 * KB, F32R) for s in range(5)]
        stage = at("stage", [P, 2, 1024], 48 * KB)

        ident = at("ident", [P, P], M)
        ident_r = at("ident_r", [P, P], M + 512, F32R)
        causal_r = at("causal_r", [P, P], M + 1024, F32R)
        causal_t = at("causal_t", [P, P], M + 1536)
        ones = at("ones", [P, P], M + 2048)
        SPARE = M + 2560
        causal = at("causal", [P, P], SPARE)
        cols = at("cols", [P, 304], SPARE + 4224)
        used = [0]

        def col(n):
            c = used[0]
            used[0] += n
            assert used[0] <= 304
            return cols[:, c:c + n]

        q_gain, kv_gain = col(2), col(1)
        conv_at = used[0]
        conv_w, conv_b = col(32).rearrange("p (c j) -> p c j", j=CONV), col(8)
        inv_freq, sin_sign = col(1), col(1)
        gate_bias = col(2)
        pool_gain = col(16)
        inv_count = col(HALO)
        stat_a, stat_b, stat_c = col(8), col(8), col(8)
        stat_d, stat_e, stat_f = col(8), col(8), col(8)
        token = col(1)
        u_col, m_prev = col(8), col(8)
        floor_col = cols[:, conv_at:conv_at + HEADS * TB]
        head_gain = cols[:, conv_at + HEADS * TB:conv_at + HEADS * TB + HEADS]
        neg_max, row_sum, row_inv = col(8), col(8), col(8)
        den, den_inv, var8, sd8, rs8, h_scale = col(8), col(8), col(8), col(8), col(8), col(8)
        row_sums, neg_mean, shift, neg_inv_d = col(16), stat_e, stat_f, col(1)

        x_nat = at("x_nat", [P, TB, D], C)
        pre_gain = at("pre_gain", [P, D], E)
        junk0 = at("junk0", [P, D], B + 16 * KB)
        u_hi = at("u_hi", [P, KD, S], A, F32R)
        u_lo = at("u_lo", [P, KD, S], A + 32 * KB, F32R)
        pos_i = at("pos_i", [P, S], E + 4 * KB, I32)
        ang = at("ang", [P, S], E + 8 * KB)
        turns = at("turns", [P, S], E + 12 * KB)
        rot = at("rot", [P, S], SPARE)
        c_q = at("c_q", [P, 2, S], S2)
        c_kv = at("c_kv", [P, S], S2 + 8 * KB)
        c_q_hi = at("c_q_hi", [P, 2, S], SLOT[0], F32R)
        c_q_lo = at("c_q_lo", [P, 2, S], S2, F32R)
        c_kv_hi = at("c_kv_hi", [P, S], SLOT[0] + 8 * KB, F32R)
        c_kv_lo = at("c_kv_lo", [P, S], S2 + 8 * KB, F32R)
        k_pe = at("k_pe", [P, S], S2 + 12 * KB)
        raw = at("raw", [P, 2, S + CONV - 1], B)
        sd_q = at("sd_q", [P, S], B + 8448)
        sd_kv = at("sd_kv", [P, S], B + 16 * KB)
        k_tmp = at("k_tmp", [P, S], B + 16 * KB)
        i_row = at("i_row", [HEADS, S], B + 20 * KB)
        f_row = at("f_row", [HEADS, S], B + 24 * KB)
        b_row = at("b_row", [HEADS, S], B + 28 * KB)
        e_row = at("e_row", [HEADS, S], E + 8 * KB)
        m_row = at("m_row", [HEADS, S], E + 12 * KB)
        sq = at("sq", [P, 2, S], E)
        m_qk = at("m_qk", [P, 8, S], C)
        m_v = at("m_v", [P, TB, HEADS * P], E)
        mix = at("mix", [P, 8, S], B)
        WQ = NOPE + 2 * ROPE
        wq_h = at("wq_h", [P, 2, WQ], B + 12544)
        wkv_h = at("wkv_h", [P, NOPE + VH], B + 12544 + 8 * WQ)
        wq_lo = at("wq_lo", [P, 2, WQ], B + 12544, F32R)
        wkv_lo = at("wkv_lo", [P, NOPE + VH], B + 12544 + 8 * WQ, F32R)
        wq_hi = at("wq_hi", [P, 2, WQ], SLOT[0] + 12 * KB, F32R)
        wkv_hi = at("wkv_hi", [P, NOPE + VH], SLOT[0] + 12 * KB + 8 * WQ, F32R)
        q_n_hi = at("q_n_hi", [P, S], A, F32R)
        q_n_lo = at("q_n_lo", [P, S], SLOT[1], F32R)
        q_pe = at("q_pe", [P, S], A + 4 * KB)
        q_pe_lo = at("q_pe_lo", [P, S], A + 4 * KB, F32R)
        q_pe_hi = at("q_pe_hi", [P, S], SLOT[1] + 4 * KB, F32R)
        k_n_hi = at("k_n_hi", [P, S], A + 8 * KB, F32R)
        k_n_lo = at("k_n_lo", [P, S], SLOT[1] + 8 * KB, F32R)
        k_pe_hi = at("k_pe_hi", [P, S], A + 36 * KB, F32R)
        k_pe_lo = at("k_pe_lo", [P, S], SLOT[1] + 12 * KB, F32R)
        v_n = at("v_n", [P, TB, P], A + 12 * KB)
        probs = at("probs", [P, 2, S], A + 16 * KB)
        probs_t = at("probs_t", [P, TB, P], A + 24 * KB)
        mq_h = at("mq_h", [P, S], A + 28 * KB)
        mk_h = at("mk_h", [P, S], A + 32 * KB)
        r_b = at("r_b", [P, S], A + 40 * KB)
        h_nat = at("h_nat", [P, TB, P + 1], A + 44 * KB)
        sink = at("sink", [P, P], A + 44 * KB + 4 * TB * (P + 1))
        O1 = A + 49 * KB
        vo = at("vo", [P, TB, P + 1], O1)
        k_nat = at("k_nat", [P, TB, P], O1 + 4 * TB * (P + 1))
        O2 = O1 + 4 * TB * (2 * P + 1)
        state = at("state", [P, P + 1], O2)
        e_buf, d_t, inter, s_t, q_in, k_w = (
            at(name, [P, 2, P], O2 + 544 + KB * j)
            for j, name in enumerate(("e_buf", "d_t", "inter", "s_t", "q_in", "k_w")))
        mix_hi = [at(f"mix_hi{b}", [P, 8, P], E + 8 * KB * b, F32R) for b in range(2)]
        mix_lo = [at(f"mix_lo{b}", [P, 8, P], E + 8 * KB * b + 4 * KB, F32R) for b in range(2)]
        x_blk = at("x_blk", [P, D], SLOT[1])
        h1_blk = at("h1_blk", [P, D], SLOT[1] + 4 * KB)
        f_blk = at("f_blk", [P, D], SLOT[1] + 8 * KB)
        ffn_gain = at("ffn_gain", [P, D], SLOT[1] + 12 * KB)
        post_gain = at("post_gain", [P, D], SPARE)
        f_hi = at("f_hi", [P, KD, S], A, F32R)
        f_lo = at("f_lo", [P, KD, S], A + 32 * KB, F32R)
        y = at("y", [P, TB, D], B)
        silu_g = at("silu_g", [P, 4, HALF], C)
        hid = at("hid", [P, 2, HALF], C + 8 * KB)
        hid_hi = at("hid_hi", [P, 2, S], E, F32R)
        hid_lo = at("hid_lo", [P, 2, S], E + 8 * KB, F32R)
        p_nat = at("p_nat", [P, TB, PLE], A)
        p_hi = at("p_hi", [P, 2, S], S2, F32R)
        p_lo = at("p_lo", [P, 2, S], S2 + 8 * KB, F32R)
        junk2 = at("junk2", [P, D], A + 24 * KB)
        h1_in = at("h1_in", [P, TB, D], A + 32 * KB)
        ffn_post_gain = at("ffn_post_gain", [P, D], SPARE)
        pp = at("pp", [P, KD, S], C)
        h2_hi = at("h2_hi", [P, KD, S], A, F32R)
        h2_lo = at("h2_lo", [P, KD, S], A + 32 * KB, F32R)
        sig = at("sig", [P, 2, HALF], S2)
        x3 = at("x3", [P, 2, HALF], S2 + 4 * KB)
        x3_hi = at("x3_hi", [P, KD, S], C, F32R)
        x3_lo = at("x3_lo", [P, KD, S], B, F32R)
        y2 = at("y2", [P, TB, D], A)
        m_hi = at("m_hi", [P, 4, S], A + 32 * KB, F32R)
        m_lo = at("m_lo", [P, 4, S], A + 48 * KB, F32R)
        z = at("z", [P, 4, S], E)
        g_hi = at("g_hi", [P, 4, S], E, F32R)
        g_lo0 = at("g_lo0", [P, 4, HALF], S2, F32R)
        W1 = HALO + HALF
        u_buf = at("u_buf", [P, 2, W1], SPARE)
        win = at("win", [P, 2, W1], S2 + 8 * KB)
        gt = at("gt", [P, HALF], S2 + 8 * KB + 4352)
        ln_gain = at("ln_gain", [P, D], C)
        ln_bias = at("ln_bias", [P, D], C + 4 * KB)
        ln_dev = at("ln_dev", [P, 2, D], C + 16 * KB)
        ln_sink = at("ln_sink", [P, D], C + 8 * KB)

        ps = ctx.enter_context(nc.psum_tensor("ps", [P, 8, HALF], F32))
        psf = ps[:].rearrange("p b n -> p (b n)")

        gate_dram = nc.dram_tensor("gate_rows", [4, HEADS, S], F32, kind="Internal").ap()
        h1_dram = nc.dram_tensor("h1_rows", [S, D], F32, kind="Internal").ap()

        staged = [sem("staged0"), sem("staged1")]
        parted = [sem("parted0"), sem("parted1")]
        pool_hi = Chain(sem("pool_hi"))
        consts = sem("consts")
        cols_in = sem("cols_in")
        pre_gain_in = sem("pre_gain_in")
        pos_in = sem("pos_in")
        x_in = [sem(f"x_in{t}") for t in range(TB)]
        x_sd, xn_ready, ut_full, u_hi_ready, u_split = map(sem, (
            "x_sd", "xn_ready", "ut_full", "u_hi_ready", "u_split"))
        in_full, in_taken = sem("in_full"), sem("in_taken")
        sq_ready, gates_abs, gates_log, gates_rows, gates_spilled = map(sem, (
            "sq_ready", "gates_abs", "gates_log", "gates_rows", "gates_spilled"))
        kpe_prod, kpe_shift, kpe_sum = map(sem, ("kpe_prod", "kpe_shift", "kpe_sum"))
        rot_ang, rot_sin = sem("rot_ang"), sem("rot_sin")
        conv_done, latent_ready = map(sem, ("conv_done", "latent_ready"))
        head_w, head_g, heads_in = sem("head_w"), sem("head_g"), sem("heads_in")
        act_head, dve_head = sem("act_head"), sem("dve_head")
        up_full, up_taken, qp_ready, mqkv_ready = map(sem, (
            "up_full", "up_taken", "qp_ready", "mqkv_ready"))
        s_full, nm_ready, probs_done, p_ready = map(sem, (
            "s_full", "nm_ready", "probs_done", "p_ready"))
        pt_full, pt_taken, o_full, o_taken = map(sem, ("pt_full", "pt_taken", "o_full", "o_taken"))
        st_full, mk_full, e_ready, dt_ready, ib_ready, st_ready, mk_nat, kw_ready, qin_ready = map(sem, (
            "st_full", "mk_full", "e_ready", "dt_ready", "ib_ready", "st_ready", "mk_nat", "kw_ready", "qin_ready"))
        num_full, num_taken, cn_full, cn_done = map(sem, (
            "num_full", "num_taken", "cn_full", "cn_done"))
        kpe_split, latent_split, heads_split, up_split = map(sem, (
            "kpe_split", "latent_split", "heads_split", "up_split"))
        hsq_ready, hvar_ready, hs_ready, ht_full = map(sem, ("hsq_ready", "hvar_ready", "hs_ready", "ht_full"))
        msplit_ready, mix_full, mix_taken, mix_used = map(sem, (
            "msplit_ready", "mix_full", "mix_taken", "mix_used"))
        gains_in, xblk_in, h1_ready, h1_spilled = map(sem, (
            "gains_in", "xblk_in", "h1_ready", "h1_spilled"))
        sd1_ready, sd2_ready, f_ready, ft_full, f_hi_ready, f_split = map(sem, (
            "sd1_ready", "sd2_ready", "f_ready", "ft_full", "f_hi_ready", "f_split"))
        gate_full, up2_full, down_full, silu_ready, hid_ready, hid_hi_ready, hid_split, y_added = map(sem, (
            "gate_full", "ffn_up_full", "down_full", "silu_ready", "hid_ready", "hid_hi_ready",
            "hid_split", "y_added"))
        p_in, pt2_full, p_hi_ready, p_split, pp_full, pp_taken = map(sem, (
            "p_in", "ple_t_full", "p_hi_ready", "p_split", "pp_full", "pp_taken"))
        fpg_in = sem("fpg_in")
        h1_back = [sem(f"h1_back{b}") for b in range(4)]
        h2_sd, h2_normed, h2_ready, h2t_full, h2_hi_ready, h2_split = map(sem, (
            "h2_sd", "h2_normed", "h2_ready", "h2t_full", "h2_hi_ready", "h2_split"))
        pg_full, sig_ready, x3_ready, x3_hi_ready, x3_split = map(sem, (
            "pg_full", "sig_ready", "x3_ready", "x3_hi_ready", "x3_split"))
        out_full, y2_added, out_tile_used = map(sem, ("out_full", "y2_added", "out_tile_used"))
        pu_full, pu_taken, pm_ready, pm_hi_ready, pm_split = map(sem, (
            "pu_full", "pu_taken", "pm_ready", "pm_hi_ready", "pm_split"))
        z_full, z_taken, grp_full, gt_ready, g_hi_ready, g_split = map(sem, (
            "z_full", "z_taken", "grp_full", "gt_ready", "g_hi_ready", "g_split"))
        ln_in, ln_mean, ln_sd, ln_shift, ln_normed, ln_gained, out_ready, pool_rows_ready, out_stored = map(sem, (
            "ln_in", "ln_mean", "ln_sd", "ln_shift", "ln_normed", "ln_gained", "out_ready", "pool_rows_ready", "out_stored"))
        dve_own = Chain(sem("dve_own"))
        act_own = Chain(sem("act_own"))

        T_OUT, T_FFN, T_PLE, T_PG, T_POOL = 10, 14, 47, 48, 52

        def k_rows(w):
            return w.rearrange("(k p) n -> p k n", p=P)

        w_in, w_out, w_gate, w_up, w_down = a["w_in"][0], a["w_out"][0], a["w_gate"][0], a["w_up"][0], a["w_down"][0]
        w_pp, w_pg = a["w_ple_proj"][0], a["w_ple_gate"][0]
        pw_in, pw_grp, pw_out = a["pool_w_in_2"][0], a["pool_w_grp_2"][0], a["pool_w_out_2"][0]

        def half_cols(w, h, c0):
            return k_rows(w)[:, 4 * h:4 * h + 4, bass.ds(c0, 256)]

        def half_rows(w, h, r0):
            return w[bass.ds(r0 + P * h, P), :]

        def wcols(s, k, m):
            c = k * 256 + m * P
            return w_hi[s][:, c:c + P], w_lo[s][:, c:c + P]

        def score_bank(i):
            return 6 * HALF if i < 4 else P if i == 4 else 0

        slot_of = (0, 2, 4, 3)

        def msplit_at(t, e):
            return (1 + t + 2 * e if t < 2 else 2 * t + e + 1)

        def sp_program(sp):
            def load(t, sources):
                for h in range(2):
                    sp.wait_ge(parted[h], t)
                    src, view = sources(h)
                    sp.dma_start(view, src).then_inc(staged[h], 16)

            def cols_tile(w, c0):
                return lambda h: (half_cols(w, h, c0), stage[:, h, :].rearrange("p (k n) -> p k n", k=4))

            def rows_tile(w, r0):
                return lambda h: (half_rows(w, h, r0), stage[:, h, :])

            def x_rows(t):
                sp.dma_start(x_nat[:, t, :], a["x"][0, t * P:(t + 1) * P, :]).then_inc(x_in[t], 16)

            def column(dst, src):
                sp.dma_start(dst, src, **SMALL).then_inc(cols_in, 16)

            src, view = zip(*(cols_tile(w_in, 0)(h) for h in range(2)))
            for t in range(2):
                x_rows(t)
            for h in range(2):
                sp.dma_start(view[h], src[h]).then_inc(staged[h], 16)
            for t in range(2, TB):
                x_rows(t)
            sp.dma_start(pos_i[:], a["positions"][0].partition_broadcast(P)).then_inc(pos_in, 16)
            sp.dma_start(inv_freq, a["inv_freq"]).then_inc(pos_in, 16)
            column(gate_bias[0:HEADS, 0:1], a["gate_bias_i"][0].rearrange("(h c) -> h c", c=1))
            column(gate_bias[0:HEADS, 1:2], a["gate_bias_f"][0].rearrange("(h c) -> h c", c=1))
            column(q_gain, a["q_norm"][0].rearrange("(c p) -> p c", p=P))
            column(kv_gain, a["kv_norm"][0].rearrange("(c p) -> p c", p=P))
            for h in range(2):
                sp.wait_ge(parted[h], 1)
                view = stage[:, h, :].rearrange("p (k n) -> p k n", k=4)
                rows = k_rows(w_in)[:, 4 * h:4 * h + 4, :]
                sp.dma_start(view[:, :, 0:192], rows[:, :, 256:448]).then_inc(staged[h], 16)
                sp.dma_start(view[:, :, 192:196], rows[:, :, 2496:2500]).then_inc(staged[h], 16)
                sp.dma_start(view[:, :, 224:228], rows[:, :, 2500:2504]).then_inc(staged[h], 16)
            for j in range(CONV):
                column(conv_w[:, :, j], a["conv_w"][0, j].rearrange("(c p) -> p c", p=P))
            column(conv_b, a["conv_b"][0].rearrange("(c p) -> p c", p=P))
            column(pool_gain, a["pool_scale_2"][0].rearrange("(c p) -> p c", p=P))
            with sp.Fori(1, 5, 1) as i:
                for e in range(2):
                    load(2 * i + e, cols_tile(w_in, 512 * i - 64 + 256 * e))
            load(T_OUT, rows_tile(w_out, 0))

            def head_weights(h):
                wq = a["w_uq"][0].rearrange("(k p) n -> p k n", p=P)
                c0, c1, half = h * (NOPE + ROPE), NOPE + ROPE, ROPE // 2
                sp.dma_start(wq_h[:, :, 0:c1], wq[:, :, bass.ds(c0, c1)]).then_inc(head_w, 16)
                sp.dma_start(wq_h[:, :, c1:c1 + half], wq[:, :, bass.ds(c0 + NOPE + half, half)]).then_inc(head_w, 16)
                sp.dma_start(wq_h[:, :, c1 + half:WQ], wq[:, :, bass.ds(c0 + NOPE, half)]).then_inc(head_w, 16)
                sp.dma_start(wkv_h[:], a["w_ukv"][0][:, bass.ds(h * (NOPE + VH), NOPE + VH)]).then_inc(head_w, 16)

            def head_gates(h):
                r0, u0, m0 = (gate_dram[j] for j in (0, 1, 3))
                sp.dma_start(r_b[:], r0[bass.ds(h, 1), :].rearrange("a t -> (a t)").partition_broadcast(P)).then_inc(head_g, 16)
                sp.dma_start(u_col, u0[bass.ds(h, 1), :].rearrange("a (c p) -> p (a c)", p=P), **SMALL).then_inc(head_g, 16)
                last = m0[bass.ds(h, 1), :].rearrange("a (c p) -> (a c) p", p=P)[0:TB - 1, P - 1]
                sp.dma_start(m_prev[:, 1:TB], last.partition_broadcast(P), **SMALL).then_inc(head_g, 16)

            sp.wait_ge(in_taken, 24)
            head_weights(0)
            sp.wait_ge(gates_spilled, 64)
            sp.wait_ge(in_full, 44)
            head_gates(0)
            sp.wait_ge(conv_done, 8)
            sp.dma_start(floor_col, gate_dram[2].rearrange("h (c p) -> p (h c)", p=P), **SMALL).then_inc(heads_in, 16)
            sp.dma_start(head_gain, a["mlstm_norm"][0].rearrange("(h p) -> p h", p=P), **SMALL).then_inc(heads_in, 16)
            with sp.Fori(0, HEADS - 1, 1) as h:
                sp.wait_ge(up_full, 8 * h + 8)
                head_weights(h + 1)
                sp.wait_ge(dt_ready, 8 * h + 8)
                sp.wait_ge(ib_ready, 8 * h + 8)
                head_gates(h + 1)

            for j in range(1, 4):
                load(T_OUT + j, rows_tile(w_out, 256 * j))
            sp.wait_ge(qp_ready, HEADS)
            sp.dma_start(post_gain[:], a["attn_post_norm"][0].partition_broadcast(P)).then_inc(gains_in, 16)
            sp.wait_ge(s_full, 8 * HEADS)
            sp.dma_start(x_blk[:], a["x"][0, 0:P, :]).then_inc(xblk_in, 16)
            sp.dma_start(ffn_gain[:], a["ffn_pre_norm"][0].partition_broadcast(P)).then_inc(gains_in, 16)
            load(T_FFN, cols_tile(w_gate, 0))
            for t in range(TB):
                sp.wait_ge(h1_ready, t + 1)
                sp.dma_start(h1_dram[t * P:(t + 1) * P, :], h1_blk[:]).then_inc(h1_spilled, 16)
                if t + 1 < TB:
                    sp.dma_start(x_blk[:], a["x"][0, (t + 1) * P:(t + 2) * P, :]).then_inc(xblk_in, 16)
            sp.wait_ge(f_ready, TB)
            sp.dma_start(ffn_post_gain[:], a["ffn_post_norm"][0].partition_broadcast(P)).then_inc(fpg_in, 16)
            with sp.Fori(0, FG - 1, 1) as g:
                load(T_FFN + 3 * g + 1, cols_tile(w_up, 256 * g))
                load(T_FFN + 3 * g + 2, rows_tile(w_down, 256 * g))
                load(T_FFN + 3 * g + 3, cols_tile(w_gate, 256 * g + 256))
            load(T_PLE - 2, cols_tile(w_up, 256 * (FG - 1)))
            load(T_PLE - 1, rows_tile(w_down, 256 * (FG - 1)))
            load(T_PLE, rows_tile(w_pp, 0))
            sp.wait_ge(up2_full, 4 * FG)
            sp.wait_ge(h1_spilled, 16 * TB)
            for b in range(4):
                rows = h1_dram[2 * b * P:2 * (b + 1) * P, :].rearrange("(t p) n -> p t n", p=P)
                sp.dma_start(h1_in[:, 2 * b:2 * b + 2, :], rows).then_inc(h1_back[b], 16)
            sp.dma_start(p_nat[:], a["p"][0, 0].rearrange("(t p) c -> p t c", p=P)).then_inc(p_in, 16)
            load(T_PG, cols_tile(w_pg, 0))
            for j in range(1, 4):
                load(T_PG + j, cols_tile(w_pg, 256 * j))
            with sp.Fori(0, 2, 1) as i:
                for e in range(2):
                    t0, c0 = T_POOL + 14 * i + 7 * e, 1024 * i + GW * e
                    load(t0, cols_tile(pw_in, c0))
                    load(t0 + 1, cols_tile(pw_in, c0 + 256))
                    load(t0 + 2, cols_tile(pw_in, c0 + DP))
                    load(t0 + 3, cols_tile(pw_in, c0 + DP + 256))
                    grp = pw_grp.rearrange("g c d -> (g c) d")
                    load(t0 + 4, lambda h: (
                        grp[bass.ds(c0 + 256 * h, 256), :].rearrange("(k p) n -> p k n", p=P),
                        stage[:, h, :].rearrange("p (k n) -> p k n", k=2)))
                    load(t0 + 5, rows_tile(pw_out, c0))
                    load(t0 + 6, rows_tile(pw_out, c0 + 256))
            sp.wait_ge(z_full, 32)
            sp.dma_start(ln_gain[:], a["ln_g_2"][0].partition_broadcast(P)).then_inc(ln_in, 16)
            sp.dma_start(ln_bias[:], a["ln_b_2"][0].partition_broadcast(P)).then_inc(ln_in, 16)
            for t in STORE_ORDER:
                earlier = sum(e < t for e in POOL_BIAS)
                if t in POOL_BIAS:
                    sp.wait_ge(pool_rows_ready, earlier + 1)
                else:
                    sp.wait_ge(out_ready, t - earlier + 1)
                sp.dma_start(out[0, t * P:(t + 1) * P, :], y2[:, t, :]).then_inc(out_stored, 16)
            sp.wait_ge(out_stored, 16 * TB)

        def pool_program(pool):
            g = nc.gpsimd
            own = Chain(consts)
            g.memset(ones[:], 1.0).then_inc(consts, 1)
            own.at = 1
            own.do(pool, g.memset(ident[:], 0.0))
            own.do(pool, g.memset(causal[:], 0.0))
            own.do(pool, g.memset(causal_t[:], 0.0))
            own.do(pool, g.affine_select(out=ident[:], in_=ident[:], compare_op=ALU.not_equal, fill=1.0,
                                         base=0, pattern=[[-1, P]], channel_multiplier=1))
            own.mark(g.affine_select(out=causal[:], in_=causal[:], compare_op=ALU.is_ge, fill=NEG,
                                     base=0, pattern=[[-1, P]], channel_multiplier=1))
            own.mark(g.affine_select(out=causal_t[:], in_=causal_t[:], compare_op=ALU.is_ge, fill=NEG,
                                     base=0, pattern=[[1, P]], channel_multiplier=-1))
            own.mark(g.tensor_copy(ident_r[:], ident[:]))
            own.wait(pool)
            own.mark(g.tensor_copy(causal_r[:], causal[:]))
            own.mark(g.memset(sin_sign[0:96, :], -1.0))
            own.wait(pool)
            own.do(pool, g.memset(sin_sign[96:P, :], 1.0))
            own.mark(g.memset(m_prev[:, 0:1], 0.0))
            for t in range(HALO):
                own.mark(g.memset(inv_count[:, t:t + 1], 1.0 / (t + 1)))
            own.mark(g.memset(neg_inv_d, -1.0 / D))
            assert own.at == N_CONSTS

            def part_half(t, slot, staged_at, h):
                pool.wait_ge(staged[h], staged_at)
                g.tensor_tensor(token, ones[:, 0:1], ones[:, 0:1], ALU.mult)
                hi, lo = w_hi[slot][:, 1024 * h:1024 * h + 1024], w_lo[slot][:, 1024 * h:1024 * h + 1024]
                pool_hi.do(pool, g.tensor_scalar(hi, stage[:, h, :], 1.0, 0.0, ALU.mult, ALU.add))
                g.tensor_tensor(lo, stage[:, h, :], hi.bitcast(F32), ALU.subtract).then_inc(parted[h], 1)

            def part(t, slot, staged_at):
                for h in range(2):
                    part_half(t, slot, staged_at, h)

            def landed(t):
                return 16 * t + 48

            pool.wait_ge(staged[0], 16)
            pool_hi.mark(g.tensor_scalar(w_hi[0][:, 0:1024], stage[:, 0, :], 1.0, 0.0, ALU.mult, ALU.add))
            pool.wait_ge(staged[1], 16)
            pool_hi.do(pool, g.tensor_scalar(w_hi[0][:, 1024:2048], stage[:, 1, :], 1.0, 0.0, ALU.mult, ALU.add))
            g.tensor_tensor(w_lo[0][:, 0:1024], stage[:, 0, :], w_hi[0][:, 0:1024].bitcast(F32),
                            ALU.subtract).then_inc(parted[0], 1)
            part(1, 1, 64)
            start = pool_hi.at
            with pool.Fori(1, 4, 1) as i:
                pool_hi.at = start + 4 * (i - 1)
                for e in range(2):
                    pool.wait_ge(in_full, 8 * i + 4 * e - 4)
                    part(2 * i + e, e, landed(2 * i + e))
            pool_hi.at = start + 12
            for t in (8, 9):
                pool.wait_ge(in_full, 4 * t)
                part(t, t % 2, landed(t))

            def chunk_exponents(h, i):
                if i == 0:
                    pool.wait_ge(head_g, 48 * h + 48)
                if i >= 2:
                    pool.wait_ge(dt_ready, 8 * h + i - 1)
                g.tensor_tensor(e_buf[:, i % 2, :], r_b[:, i * P:(i + 1) * P], causal_t[:], ALU.add).then_inc(e_ready, 1)

            def carried_queries(h, i):
                pool.wait_ge(ib_ready, 8 * h + i + 1)
                if i >= 2:
                    pool.wait_ge(num_full, 8 * h + i - 1)
                g.tensor_tensor(q_in[:, i % 2, :], mq_h[:, i * P:(i + 1) * P], inter[:, i % 2, :],
                                ALU.mult).then_inc(qin_ready, 1)

            def head_steps(h, between=None):
                chunk_exponents(h, 0)
                chunk_exponents(h, 1)
                for i in range(1, TB):
                    carried_queries(h, i)
                    if i + 1 < TB:
                        chunk_exponents(h, i + 1)
                    if between:
                        between(i)

            def split_head_weights(h):
                pool.wait_ge(head_w, 64 * h + 64)
                g.tensor_tensor(token, ones[:, 0:1], ones[:, 0:1], ALU.mult)
                pool_hi.mark(g.tensor_scalar(wq_hi[:], wq_h[:], 1.0, 0.0, ALU.mult, ALU.add))
                pool_hi.do(pool, g.tensor_scalar(wkv_hi[:], wkv_h[:], 1.0, 0.0, ALU.mult, ALU.add))
                pool_hi.mark(g.tensor_tensor(wq_lo[:], wq_h[:], wq_hi[:].bitcast(F32), ALU.subtract))
                g.tensor_tensor(wkv_lo[:], wkv_h[:], wkv_hi[:].bitcast(F32), ALU.subtract).then_inc(heads_split, 1)

            pool.wait_ge(in_full, 40)
            split_head_weights(0)
            pool.wait_ge(in_full, 44)
            pool.wait_ge(act_head, 1)
            pool_hi.do(pool, g.tensor_scalar(k_pe_hi[:], k_pe[:], 1.0, 0.0, ALU.mult, ALU.add))
            g.tensor_tensor(k_pe_lo[:], k_pe[:], k_pe_hi[:].bitcast(F32), ALU.subtract).then_inc(kpe_split, 1)
            start = pool_hi.at
            with pool.Fori(0, HEADS - 1, 1) as h:
                pool_hi.at = start + 3 * h
                head_steps(h, lambda i: split_head_weights(h + 1) if i == 3 else None)
            pool_hi.at = start + 3 * (HEADS - 1)
            def late_weights(i):
                if i == 1:
                    pool.wait_ge(up_full, 8 * HEADS)
                    pool.wait_ge(mqkv_ready, 3 * HEADS)
                if i < TB - 1:
                    j, e = (i - 1) // 2, (i - 1) % 2
                    part_half(T_OUT + j, slot_of[j], landed(T_OUT + j), e)

            head_steps(HEADS - 1, late_weights)
            part(T_OUT + 3, slot_of[3], landed(T_OUT + 3))
            pool.wait_ge(msplit_ready, 2 * TB)
            for j in range(16):
                g.memset(y[:, j // 2, (j % 2) * HALF:(j % 2 + 1) * HALF], 0.0).then_inc(y_added, 1)
            pool.wait_ge(mix_used, 1)
            part(T_FFN, 0, landed(T_FFN))
            pool.wait_ge(ft_full, 2 * TB)
            pool.wait_ge(h1_spilled, 16 * TB)
            part(T_FFN + 1, 1, landed(T_FFN + 1))
            part(T_FFN + 2, 2, landed(T_FFN + 2))
            start = pool_hi.at
            with pool.Fori(1, FG, 1) as i:
                pool_hi.at = start + 6 * (i - 1)
                pool.wait_ge(gate_full, 4 * i)
                part(T_FFN + 3 * i, 0, landed(T_FFN + 3 * i))
                pool.wait_ge(up2_full, 4 * i)
                part(T_FFN + 3 * i + 1, 1, landed(T_FFN + 3 * i + 1))
                pool.wait_ge(down_full, 16 * i)
                part(T_FFN + 3 * i + 2, 2, landed(T_FFN + 3 * i + 2))
            pool_hi.at = start + 6 * (FG - 1)
            pool.wait_ge(gate_full, 4 * FG)
            part(T_PLE, 0, landed(T_PLE))
            pool.wait_ge(up2_full, 4 * FG)
            for t in range(TB):
                pool.wait_ge(h1_back[t // 2], 16)
                pool.wait_ge(h2_normed, t + 1)
                g.tensor_tensor(y[:, t, :], y[:, t, :], h1_in[:, t, :], ALU.add).then_inc(h2_ready, 1)
            part(T_PG, 1, landed(T_PG))
            pool.wait_ge(pp_full, 16)
            part(T_PG + 1, 0, landed(T_PG + 1))
            pool.wait_ge(pg_full, 4)
            part(T_PG + 2, 1, landed(T_PG + 2))
            pool.wait_ge(pg_full, 8)
            part(T_PG + 3, 0, landed(T_PG + 3))
            start = pool_hi.at
            with pool.Fori(0, 2, 1) as i:
                pool_hi.at = start + 28 * i
                for e in range(2):
                    before = [(out_tile_used, 2 * i + e + 1), (out_full, 32 * i + 16 * e + 16),
                              (pu_full, 16 * i + 8 * e + 4), (pu_full, 16 * i + 8 * e + 8),
                              (z_full, 16 * i + 8 * e + 4), (z_full, 16 * i + 8 * e + 8),
                              (grp_full, 16 * i + 8 * e + 8)]
                    for j, (s, n) in enumerate(before):
                        pool.wait_ge(s, n)
                        t = T_POOL + 14 * i + 7 * e + j
                        part(t, (1 + 7 * e + j) % 2, landed(t))
            pool.wait_ge(ln_in, 32)
            for t in range(TB - LN_LAST):
                pool.wait_ge(ln_normed, t + 1)
                g.tensor_tensor(y2[:, t, :], y2[:, t, :], ln_gain[:], ALU.mult).then_inc(ln_gained, 1)
                if t in POOL_BIAS:
                    pool.wait_ge(ln_gained, t + 1)
                    g.tensor_tensor(y2[:, t, :], y2[:, t, :], ln_bias[:], ALU.add).then_inc(pool_rows_ready, 1)

        def pe_program(pe):
            mm, tr = nc.tensor.matmul, nc.tensor.transpose

            def tile_ready(t):
                pe.wait_ge(parted[0], t + 1)
                pe.wait_ge(parted[1], t + 1)

            def three(out_ap, terms, start=True, stop=True):
                n = 3 * len(terms)
                j = 0
                for lh, ll, rh, rl in terms:
                    for l, r in ((lh, rh), (lh, rl), (ll, rh)):
                        last = mm(out_ap, l, r, start=(start and j == 0), stop=(stop and j == n - 1))
                        j += 1
                return last

            def proj_t(bank, s, m, n, x_h, x_l):
                ts = slice(n * HALF, n * HALF + HALF)
                return three(ps[:, bank, :], [(*wcols(s, k, m), x_h[:, k, ts], x_l[:, k, ts]) for k in range(KD)])

            def x_transposed(t):
                pe.wait_ge(xn_ready, t + 1)
                if t >= 2:
                    pe.wait_ge(u_split, 2 * (t - 2) + 2)
                for k in range(KD):
                    b, c = 4 + 2 * (t % 2) + k // 4, (k % 4) * P
                    last = tr(ps[:, b, c:c + P], x_nat[:, t, k * P:(k + 1) * P], ident[:])
                    if k % 4 == 3:
                        last.then_inc(ut_full, 1)

            def in_tile(t, s, q0, bank0, first=False):
                tile_ready(t)
                for m in range(2):
                    for n in range(2):
                        j = 2 * m + n
                        if not first:
                            pe.wait_ge(in_taken, q0 + j - 7)
                        proj_t(bank0 + j, s, m, n, u_hi, u_lo).then_inc(in_full, 1)

            pe.wait_ge(consts, N_CONSTS)
            for t in range(2):
                x_transposed(t)
            tile_ready(0)
            QUARTER = S // 4
            for j in range(8):
                q, m = j // 2, j % 2
                pe.wait_ge(u_split, 4 * q + 4)
                ts = slice(q * QUARTER, (q + 1) * QUARTER)
                c = (q % 2) * QUARTER
                last = three(ps[:, 2 * (q // 2) + m, c:c + QUARTER],
                             [(*wcols(0, k, m), u_hi[:, k, ts], u_lo[:, k, ts]) for k in range(KD)])
                if q % 2 == 1:
                    last.then_inc(in_full, 1)
                if m == 0 and q < 3:
                    x_transposed(2 * q + 2)
                    x_transposed(2 * q + 3)
            in_tile(1, 1, 4, 4, first=True)
            with pe.Fori(1, 3, 1) as i:
                in_tile(2 * i, 0, 8 * i, 0)
                in_tile(2 * i + 1, 1, 8 * i + 4, 4)
            pe.wait_ge(sq_ready, 2)
            for j in range(4):
                pe.wait_ge(in_taken, 24 + j - 7)
                mm(ps[:, j, :], ones[:], sq[:, j // 2, (j % 2) * HALF:(j % 2 + 1) * HALF],
                   start=True, stop=True).then_inc(in_full, 1)

            def in_rows(t, s, q0, bank0):
                tile_ready(t)
                for j in range(4):
                    pe.wait_ge(in_taken, q0 + j - 7)
                    for e in range(2):
                        ts, c = slice((2 * j + e) * P, (2 * j + e + 1) * P), 2 * P * e
                        last = three(ps[:, bank0 + j, c:c + 2 * P],
                                     [(u_hi[:, k, ts], u_lo[:, k, ts], w_hi[s][:, 256 * k:256 * k + 256],
                                       w_lo[s][:, 256 * k:256 * k + 256]) for k in range(KD)])
                    last.then_inc(in_full, 1)

            in_rows(6, 0, 28, 4)
            in_rows(7, 1, 32, 0)
            in_tile(8, 0, 36, 4)
            in_tile(9, 1, 40, 0)

            def latent_rows(o, c, n):
                cs, ts = slice(c, c + P), slice(n * HALF, (n + 1) * HALF)
                return three(o, [(wq_hi[:, k, cs], wq_lo[:, k, cs], c_q_hi[:, k, ts], c_q_lo[:, k, ts]) for k in range(2)])

            def up_queries(h, first=False):
                pe.wait_ge(heads_split, h + 1)
                if not first:
                    pe.wait_ge(probs_done, 8 * h)
                for n in range(2):
                    latent_rows(ps[:, n, :], 0, n).then_inc(up_full, 1)

            def up_rotary(h, first=False):
                if not first:
                    pe.wait_ge(st_ready, 8 * h)
                for n in range(2):
                    latent_rows(ps[:, 6 - n, :], NOPE, n).then_inc(up_full, 1)

            def up_keys_values(h, first=False):
                for n, b in enumerate((7, 4)):
                    if not first and n == 0:
                        pe.wait_ge(num_taken, 8 * h)
                        pe.wait_ge(cn_done, 8 * h)
                    if not first and n == 1:
                        pe.wait_ge(o_taken, 8 * h)
                    ts = slice(n * HALF, (n + 1) * HALF)
                    three(ps[:, b, :], [(wkv_hi[:, 0:NOPE], wkv_lo[:, 0:NOPE], c_kv_hi[:, ts], c_kv_lo[:, ts])]).then_inc(up_full, 1)
                if not first:
                    pe.wait_ge(pt_taken, 8 * h)
                for t in range(TB):
                    ts, cs = slice(t * P, (t + 1) * P), slice(NOPE, NOPE + VH)
                    last = three(ps[:, 2 + t // 4, (t % 4) * P:(t % 4 + 1) * P],
                                 [(c_kv_hi[:, ts], c_kv_lo[:, ts], wkv_hi[:, cs], wkv_lo[:, cs])])
                    if t % 4 == 3:
                        last.then_inc(up_full, 1)

            def chunk_rows(h):
                pe.wait_ge(mqkv_ready, 3 * h + 2)
                pe.wait_ge(up_split, 4 * h + 2)
                for t in range(TB):
                    last = tr(ps[:, t // 4, (t % 4) * P:(t % 4 + 1) * P], mk_h[:, t * P:(t + 1) * P], ident[:])
                    if t % 4 == 3:
                        last.then_inc(mk_full, 1)

            def head_rows(h, banks):
                pe.wait_ge(hs_ready, h + 1)
                for t in range(TB):
                    last = tr(ps[:, banks[t // 4], (t % 4) * P:(t % 4 + 1) * P], h_nat[:, t, 0:P], ident[:])
                    if t % 4 == 3:
                        last.then_inc(ht_full, 1)

            def scores(h, s):
                i = Q_ORDER[s]
                blk, o = slice(i * P, (i + 1) * P), score_bank(i)
                if s >= 2:
                    pe.wait_ge(probs_done, 8 * h + s - 1)
                edge = HALF - o % HALF
                for c0, c1 in ((0, min(edge, (i + 1) * P)), (edge, (i + 1) * P)):
                    if c0 >= c1:
                        continue
                    cs = slice(c0, c1)
                    passes = [(q, k) for q, k in ((q_n_hi, k_n_hi), (q_n_hi, k_n_lo), (q_n_lo, k_n_hi),
                                                  (q_pe_hi, k_pe_hi), (q_pe_hi, k_pe_lo), (q_pe_lo, k_pe_hi))]
                    for j, (q, k) in enumerate(passes):
                        last = mm(psf[:, o + c0:o + c1], q[:, blk], k[:, cs], start=(j == 0), stop=(j == 5))
                        if j == 0 and c1 == (i + 1) * P:
                            mm(psf[:, o + i * P:o + c1], ident_r[:], causal_r[:], start=False, stop=False)
                last.then_inc(s_full, 1)

            def probs_transposed(h, s):
                pe.wait_ge(p_ready, 8 * h + s + 1)
                if s == 0:
                    pe.wait_ge(dve_head, h + 1)
                else:
                    pe.wait_ge(pt_taken, 8 * h + s)
                for j in range(Q_ORDER[s] + 1):
                    last = tr(psf[:, 1024 + j * P:1024 + (j + 1) * P],
                              probs[:, s % 2, j * P:(j + 1) * P], ident[:])
                last.then_inc(pt_full, 1)

            def values(h, s):
                i = Q_ORDER[s]
                pe.wait_ge(pt_taken, 8 * h + s + 1)
                if s >= 1:
                    pe.wait_ge(o_taken, 8 * h + s)
                for j in range(i + 1):
                    last = mm(ps[:, 4, 0:P], v_n[:, j, :], probs_t[:, j, :], start=(j == 0), stop=(j == i))
                last.then_inc(o_full, 1)

            def chunk_scores(h, i):
                blk = slice(i * P, (i + 1) * P)
                mm(ps[:, 5, 0:P], mk_h[:, blk], mq_h[:, blk], start=True, stop=True).then_inc(st_full, 1)

            def chunk_state(h, i):
                pe.wait_ge(st_ready, 8 * h + i + 1)
                pe.wait_ge(kw_ready, 8 * h + i + 1)
                if i >= 1:
                    pe.wait_ge(qin_ready, 7 * h + i)
                    pe.wait_ge(num_taken, 8 * h + i)
                    pe.wait_ge(cn_done, 8 * h + i)
                last = mm(ps[:, 7, 0:P + 1], s_t[:, i % 2, :], vo[:, i, :], start=True, stop=(i == 0))
                if i >= 1:
                    last = mm(ps[:, 7, 0:P + 1], q_in[:, i % 2, :], state[:], start=False, stop=True)
                last.then_inc(num_full, 1)
                mm(ps[:, 7, 2 * P:3 * P + 1], k_w[:, i % 2, :], vo[:, i, :], start=True, stop=True).then_inc(cn_full, 1)

            def head_steps(h):
                pe.wait_ge(up_taken, 6 * h + 6)
                pe.wait_ge(up_split, 4 * h + 4)
                pe.wait_ge(qp_ready, h + 1)
                pe.wait_ge(mk_nat, 2 * h + 2)
                pe.wait_ge(mqkv_ready, 3 * h + 3)
                chunk_scores(h, 0)
                scores(h, 0)
                for s in range(TB):
                    if s + 1 < TB:
                        scores(h, s + 1)
                    if 1 <= s < TB - 1:
                        values(h, s - 1)
                    chunk_state(h, s)
                    if s == TB - 1:
                        values(h, s - 1)
                    if s + 1 < TB:
                        chunk_scores(h, s + 1)
                        probs_transposed(h, s)

            pe.wait_ge(in_taken, 44)
            pe.wait_ge(latent_split, 1)
            up_queries(0, first=True)
            up_rotary(0, first=True)
            up_keys_values(0, first=True)
            chunk_rows(0)
            pe.wait_ge(kpe_split, 1)
            with pe.Fori(0, HEADS - 1, 1) as h:
                head_steps(h)
                up_queries(h + 1)
                probs_transposed(h, TB - 1)
                up_rotary(h + 1)
                values(h, TB - 1)
                up_keys_values(h + 1)
                chunk_rows(h + 1)
                pe.wait_ge(up_taken, 6 * h + 12)
                head_rows(h, (2, 3))
            head_steps(HEADS - 1)
            probs_transposed(HEADS - 1, TB - 1)

            def f_transposed(t):
                pe.wait_ge(f_ready, t + 1)
                if t >= 2:
                    pe.wait_ge(f_split, 2 * t - 2)
                for k in range(KD):
                    b = 4 + 2 * (t % 2) + k // 4
                    last = tr(ps[:, b, (k % 4) * P:(k % 4 + 1) * P], f_blk[:, k * P:(k + 1) * P], ident[:])
                    if k % 4 == 3:
                        last.then_inc(ft_full, 1)

            def mixed(t, e):
                pe.wait_ge(msplit_ready, msplit_at(t, e))
                for k in range(4 * e, 4 * e + 4):
                    s = slot_of[k // 2]
                    for n in range(2):
                        o, c = ps[:, 2 * (t % 2) + n, :], (k % 2) * 1024 + n * HALF
                        l_hi, l_lo = mix_hi[t % 2][:, k, :], mix_lo[t % 2][:, k, :]
                        mm(o, l_hi, w_hi[s][:, c:c + HALF], start=(k == 0), stop=False)
                        mm(o, l_hi, w_lo[s][:, c:c + HALF], start=False, stop=False)
                        last = mm(o, l_lo, w_hi[s][:, c:c + HALF], start=False, stop=(k == 7))
                        if k == 7:
                            last.then_inc(mix_full, 1)
                    if t == TB - 1 and k == 1:
                        last.then_inc(mix_used, 1)

            tile_ready(T_OUT + 1)
            mixed(0, 0)
            values(HEADS - 1, TB - 1)
            head_rows(HEADS - 1, (5, 6))
            mixed(1, 0)
            tile_ready(T_OUT + 3)
            mixed(0, 1)
            mixed(1, 1)
            for t in range(2, TB):
                pe.wait_ge(mix_taken, t - 1)
                mixed(t, 0)
                if t == 2:
                    f_transposed(0)
                mixed(t, 1)
                f_transposed(t - 1)

            def gate_rows(g, b):
                pe.wait_ge(y_added, 16 * g + b + 9)
                proj_t(b, 0, b % 2, b // 2, f_hi, f_lo).then_inc(gate_full, 1)

            def up_and_down(g):
                tile_ready(T_FFN + 3 * g + 1)
                for b in range(4):
                    pe.wait_ge(y_added, 16 * g + b + 13)
                    proj_t(4 + b, 1, b % 2, b // 2, f_hi, f_lo).then_inc(up2_full, 1)
                tile_ready(T_FFN + 3 * g + 2)
                for t in range(TB):
                    if t % 4 == 0:
                        pe.wait_ge(hid_split, 4 * g + 2 + t // 2)
                    for n in range(2):
                        j = 2 * t + n
                        if j < 4:
                            pe.wait_ge(silu_ready, 4 * g + j + 1)
                        elif j < 8:
                            pe.wait_ge(hid_split, 4 * g + 4)
                        else:
                            pe.wait_ge(y_added, 16 * g + 16 + j - 7)
                        terms = [(hid_hi[:, k, t * P:(t + 1) * P], hid_lo[:, k, t * P:(t + 1) * P],
                                  w_hi[2][:, k * 1024 + n * HALF:k * 1024 + (n + 1) * HALF],
                                  w_lo[2][:, k * 1024 + n * HALF:k * 1024 + (n + 1) * HALF]) for k in range(2)]
                        three(ps[:, j % 8, :], terms).then_inc(down_full, 1)

            tile_ready(T_FFN)
            pe.wait_ge(f_split, TB)
            pe.wait_ge(mix_taken, TB - 1)
            for b in range(4):
                if b == 1:
                    f_transposed(TB - 1)
                if b == 2:
                    pe.wait_ge(mix_taken, TB)
                    pe.wait_ge(f_split, 2 * TB)
                gate_rows(0, b)
            up_and_down(0)
            with pe.Fori(1, FG, 1) as g:
                tile_ready(T_FFN + 3 * g)
                for b in range(4):
                    gate_rows(g, b)
                up_and_down(g)

            pe.wait_ge(p_in, 16)
            for c in range(2):
                for t in range(TB):
                    b = 2 * c + t // 4
                    if t % 4 == 0:
                        pe.wait_ge(y_added, 16 * FG + 9 + b)
                    last = tr(ps[:, b, (t % 4) * P:(t % 4 + 1) * P], p_nat[:, t, c * P:(c + 1) * P], ident[:])
                    if t % 4 == 3:
                        last.then_inc(pt2_full, 1)

            def h2_transposed(t):
                pe.wait_ge(h2_ready, t + 1)
                if t >= 2:
                    pe.wait_ge(h2_split, 2 * (t - 2) + 2)
                for k in range(KD):
                    b = 4 + 2 * (t % 2) + k // 4
                    last = tr(ps[:, b, (k % 4) * P:(k % 4 + 1) * P], y[:, t, k * P:(k + 1) * P], ident[:])
                    if k % 4 == 3:
                        last.then_inc(h2t_full, 1)

            pe.wait_ge(y_added, 16 * FG + 16)
            h2_transposed(0)
            h2_transposed(1)
            tile_ready(T_PLE)
            pe.wait_ge(p_split, 4)
            for j in range(16):
                m, n = j // 2, j % 2
                if j >= 4:
                    pe.wait_ge(pp_taken, j - 3)
                ts = slice(n * HALF, (n + 1) * HALF)
                terms = [(w_hi[0][:, k * 1024 + m * P:k * 1024 + (m + 1) * P],
                          w_lo[0][:, k * 1024 + m * P:k * 1024 + (m + 1) * P],
                          p_hi[:, k, ts], p_lo[:, k, ts]) for k in range(2)]
                three(ps[:, j % 4, :], terms).then_inc(pp_full, 1)
                if j in H2_AFTER:
                    h2_transposed(H2_AFTER[j])

            def x3_rows(t):
                for n in range(2):
                    j = 2 * t + n
                    if j >= 8:
                        pe.wait_ge(y2_added, j - 7)
                    for k in range(4):
                        ts = slice(t * P, (t + 1) * P)
                        o = ps[:, j % 8, k * P:(k + 1) * P]
                        first = mm(o, x3_hi[:, 4 * n + k, ts], ident_r[:], start=True, stop=False)
                        if j + k == 0:
                            first.then_inc(out_tile_used, 1)
                        last = mm(o, x3_lo[:, 4 * n + k, ts], ident_r[:], start=False, stop=True)
                    last.then_inc(out_full, 1)

            pe.wait_ge(h2_split, 2 * TB)
            for i in range(4):
                tile_ready(T_PG + i)
                for j in range(4):
                    b = 4 * (i % 2) + j
                    if i == 0:
                        pe.wait_ge(pp_taken, 12 + j + 1)
                    if i >= 2:
                        pe.wait_ge(sig_ready, 4 * (i - 2) + j + 1)
                    proj_t(b, (1 + i) % 2, j % 2, j // 2, h2_hi, h2_lo).then_inc(pg_full, 1)
                    if i == 3 and j == 2:
                        pe.wait_ge(sig_ready, 12)
                        pe.wait_ge(x3_split, 14)
                        x3_rows(0)
                        x3_rows(1)

            pe.wait_ge(sig_ready, 16)
            for t in range(2, TB):
                if t == 4:
                    pe.wait_ge(x3_split, 16)
                x3_rows(t)
            with pe.Fori(0, 2, 1) as i:
                for e in range(2):
                    t0 = T_POOL + 14 * i + 7 * e
                    n8, n16 = 16 * i + 8 * e, 32 * i + 16 * e
                    for j in range(2):
                        tile_ready(t0 + j)
                        for m in range(2):
                            for n in range(2):
                                b = 4 * j + 2 * m + n
                                pe.wait_ge(y2_added, n16 + b + 9)
                                proj_t(b, (1 + e + j) % 2, m, n, x3_hi, x3_lo).then_inc(pu_full, 1)
                    for j in range(2):
                        tile_ready(t0 + 2 + j)
                        for m in range(2):
                            for n in range(2):
                                b = 4 * j + 2 * m + n
                                pe.wait_ge(pu_taken, n8 + b + 1)
                                proj_t(b, (1 + e + j) % 2, m, n, x3_hi, x3_lo).then_inc(z_full, 1)
                    tile_ready(t0 + 4)
                    s = (1 + e) % 2
                    pe.wait_ge(pm_split, n8 + 8)
                    for n in range(2):
                        for m in range(4):
                            b = 4 * n + m
                            pe.wait_ge(z_taken, n8 + b + 1)
                            ts = slice(n * HALF, (n + 1) * HALF)
                            terms = [(w_hi[s][:, k * 512 + m * P:k * 512 + (m + 1) * P],
                                      w_lo[s][:, k * 512 + m * P:k * 512 + (m + 1) * P],
                                      m_hi[:, k, ts], m_lo[:, k, ts]) for k in range(4)]
                            three(ps[:, b, :], terms).then_inc(grp_full, 1)
                    for hf in range(2):
                        for r in range(2):
                            tile_ready(t0 + 5 + r)
                            s = (e + r) % 2
                            if r == 0:
                                pe.wait_ge(g_split, n8 + 4 + 4 * hf)
                            for j in range(8 * hf, 8 * hf + 8):
                                t, n = j // 2, j % 2
                                if r == 0 and hf == 0:
                                    pe.wait_ge(gt_ready, n8 + j + 1)
                                elif r == 0:
                                    pe.wait_ge(y2_added, n16 + 16 + j - 7)
                                terms = []
                                for k in range(2):
                                    ts = slice(t * P, (t + 1) * P)
                                    lo = (g_lo0[:, 2 * r + k, ts] if hf == 0
                                          else m_lo[:, 2 * r + k, t * P - HALF:(t + 1) * P - HALF])
                                    c = k * 1024 + n * HALF
                                    terms.append((g_hi[:, 2 * r + k, ts], lo,
                                                  w_hi[s][:, c:c + HALF], w_lo[s][:, c:c + HALF]))
                                last = three(ps[:, j % 8, :], terms, start=(r == 0), stop=(r == 1))
                                if r == 1:
                                    last.then_inc(out_full, 1)
                            if r == 0 and hf == 1:
                                last.then_inc(out_tile_used, 1)

        def act_program(act):
            f = nc.scalar.activation
            dma = act.dma_start

            dma(pre_gain[:], a["attn_pre_norm"][0].partition_broadcast(P)).then_inc(pre_gain_in, 16)

            def x_norm(t):
                act.wait_ge(x_in[t], 16)
                act_own.do(act, f(junk0[:], x_nat[:, t, :], ACT.Square, accum_out=stat_a[:, t:t + 1]))
                f(stat_b[:, t:t + 1], stat_a[:, t:t + 1], ACT.Sqrt, bias=EPS, scale=1.0 / D).then_inc(x_sd, 1)

            act.wait_ge(consts, 1)
            act_own.do(act, f(stat_b[:, 0:1], ones[:, 0:1], ACT.Sqrt))
            act.wait_ge(consts, N_CONSTS)
            for q in range(TB // 2):
                x_norm(2 * q)
                x_norm(2 * q + 1)
                for t in (2 * q, 2 * q + 1):
                    for j in range(2):
                        act.wait_ge(ut_full, 2 * t + j + 1)
                        f(u_hi[:, 4 * j:4 * j + 4, t * P:(t + 1) * P],
                          ps[:, 4 + 2 * (t % 2) + j, :].rearrange("p (k n) -> p k n", k=4),
                          ACT.Copy).then_inc(u_hi_ready, 1)
            act.wait_ge(rot_ang, 1)
            f(rot[0:64, :], ang[0:64, :], ACT.Sin, scale=0.5).then_inc(rot_sin, 1)
            f(rot[64:P, :], ang[64:P, :], ACT.Sin).then_inc(rot_sin, 1)

            def half(n):
                return slice(n * HALF, (n + 1) * HALF)

            for n in range(2):
                for m in range(2):
                    act.wait_ge(in_full, 2 * n + m + 1)
                    f(c_q[:, m, half(n)], ps[:, 2 * n + m, :], ACT.Copy).then_inc(in_taken, 1)
            for n in range(2):
                act.wait_ge(in_full, 5 + n)
                f(c_kv[:, half(n)], ps[:, 4 + n, :], ACT.Copy).then_inc(in_taken, 1)
            for n in range(2):
                act.wait_ge(in_full, 7 + n)
                b = 6 + n
                f(k_pe[0:64, half(n)], ps[0:64, b, :], ACT.Copy)
                f(k_pe[64:96, half(n)], ps[32:64, b, :], ACT.Copy)
                f(k_pe[96:P, half(n)], ps[0:32, b, :], ACT.Copy)
                f(i_row[:, half(n)], ps[64:64 + HEADS, b, :], ACT.Copy)
                f(f_row[:, half(n)], ps[96:96 + HEADS, b, :], ACT.Copy).then_inc(in_taken, 1)
            act.wait_ge(gates_abs, 1)
            act_own.do(act, f(e_row[:], e_row[:], ACT.Exp, scale=-1.0))
            f(e_row[:], e_row[:], ACT.Ln, bias=1.0).then_inc(gates_log, 1)
            act.wait_ge(kpe_prod, 1)
            f(k_tmp[0:64, :], k_pe[64:P, :], ACT.Copy).then_inc(kpe_shift, 1)

            def raw_rows(c):
                for n in range(2):
                    q = 8 + 2 * c + n
                    act.wait_ge(in_full, q + 1)
                    if c >= 2:
                        act.wait_ge(conv_done, c - 1)
                    f(raw[:, c % 2, CONV - 1 + n * HALF:CONV - 1 + (n + 1) * HALF], ps[:, q % 8, :],
                      ACT.Copy).then_inc(in_taken, 1)

            def silu_rows(c):
                act.wait_ge(conv_done, c + 1)
                f(m_qk[:, c, :], m_qk[:, c, :], ACT.Silu)

            raw_rows(0)
            raw_rows(1)
            act.wait_ge(gates_rows, 1)
            act_own.do(act, f(e_row[:], m_row[:], ACT.Exp, scale=-1.0))
            for j, row in enumerate((b_row, i_row, e_row, m_row)):
                dma(gate_dram[j], row[:]).then_inc(gates_spilled, 16)
            act.wait_ge(kpe_sum, 1)
            f(k_pe[64:P, :], k_pe[0:64, :], ACT.Copy).then_inc(act_head, 1)
            silu_rows(0)
            for c in range(2, 8):
                raw_rows(c)
                silu_rows(c - 1)
            silu_rows(7)
            for j in range(4):
                act.wait_ge(in_full, 24 + j + 1)
                width = QLORA if j < 2 else KVLORA
                sd = sd_q if j < 2 else sd_kv
                f(sd[:, half(j % 2)], ps[:, j, :], ACT.Sqrt, bias=EPS, scale=1.0 / width).then_inc(in_taken, 1)
            act.wait_ge(gates_spilled, 64)
            for q in range(28, 36):
                act.wait_ge(in_full, q + 1)
                t, c = 2 * (q % 4), 2 * P * ((q - 28) // 4)
                f(m_v[:, t:t + 2, c:c + 2 * P], ps[:, q % 8, :].rearrange("p (t n) -> p t n", t=2),
                  ACT.Copy).then_inc(in_taken, 1)
            act.wait_ge(latent_ready, 1)
            for c in range(HEADS):
                for n in range(2):
                    q = 36 + 2 * c + n
                    act.wait_ge(in_full, q + 1)
                    f(mix[:, 4 + c, half(n)], ps[:, q % 8, :], ACT.Sigmoid).then_inc(in_taken, 1)

            act.wait_ge(in_full, 44)
            act.wait_ge(in_taken, 44)
            def head_copies(h, first=False):
                if not first:
                    act.wait_ge(st_ready, 8 * h)
                    act.wait_ge(qin_ready, 7 * h)
                f(mq_h[:], m_qk[:, bass.ds(h, 1), :], ACT.Copy).then_inc(mqkv_ready, 1)
                f(mk_h[:], m_qk[:, bass.ds(h + 4, 1), :], ACT.Copy, scale=MH_SCALE).then_inc(mqkv_ready, 1)

            def copy_values(h, first=False):
                if not first:
                    act.wait_ge(cn_full, 8 * h)
                f(vo[:, :, 0:P], m_v[:, :, bass.ds(h * P, P)], ACT.Copy).then_inc(mqkv_ready, 1)

            def take_queries(h):
                for j in (0, 1):
                    act.wait_ge(up_full, 8 * h + j + 1)
                    f(q_n_hi[:, half(j)], ps[:, j, :], ACT.Copy, scale=QK_SCALE).then_inc(up_taken, 1)

            def take_keys_values(h):
                for j in (0, 1):
                    act.wait_ge(up_full, 8 * h + j + 5)
                    f(k_n_hi[:, half(j)], ps[:, (7, 4)[j], :], ACT.Copy).then_inc(up_taken, 1)
                for j in (0, 1):
                    act.wait_ge(up_full, 8 * h + j + 7)
                    f(v_n[:, 4 * j:4 * j + 4, :], ps[:, 2 + j, :].rearrange("p (t n) -> p t n", t=4),
                      ACT.Copy).then_inc(up_taken, 1)

            def take_chunk_rows(h):
                for j in range(2):
                    act.wait_ge(mk_full, 2 * h + j + 1)
                    f(k_nat[:, 4 * j:4 * j + 4, :], ps[:, j, :].rearrange("p (t n) -> p t n", t=4),
                      ACT.Copy).then_inc(mk_nat, 1)

            def take_probs_t(h, s):
                i = Q_ORDER[s]
                act.wait_ge(pt_full, 8 * h + s + 1)
                if s >= 1:
                    act.wait_ge(o_full, 8 * h + s)
                f(probs_t[:, 0:i + 1, :], psf[:, 1024:1024 + (i + 1) * P].rearrange("p (t n) -> p t n", n=P),
                  ACT.Copy).then_inc(pt_taken, 1)

            def take_out(h, s):
                i = Q_ORDER[s]
                act.wait_ge(o_full, 8 * h + s + 1)
                f(mix[:, bass.ds(h, 1), i * P:(i + 1) * P], ps[:, 4, 0:P], ACT.Copy).then_inc(o_taken, 1)

            def chunk_weights(h, i):
                act.wait_ge(e_ready, 8 * h + i + 1)
                if i >= 2:
                    act.wait_ge(cn_done, 8 * h + i - 1)
                f(d_t[:, i % 2, :], e_buf[:, i % 2, :], ACT.Exp, bias=u_col[:, i:i + 1]).then_inc(dt_ready, 1)
                f(inter[:, i % 2, :], r_b[:, i * P:(i + 1) * P], ACT.Exp, bias=m_prev[:, i:i + 1]).then_inc(ib_ready, 1)

            def row_squares(h, i):
                act.wait_ge(num_taken, 8 * h + i + 1)
                return f(sink[:], h_nat[:, i, 0:P], ACT.Square, accum_out=var8[:, i:i + 1])

            def head_steps(h):
                chunk_weights(h, 0)
                for s in range(TB):
                    w, i = s % 2, Q_ORDER[s]
                    act.wait_ge(dt_ready, 8 * h + s + 1)
                    if s >= 2:
                        act.wait_ge(cn_full, 8 * h + s - 1)
                    f(k_w[:, w, :], k_nat[:, s, :], ACT.Copy, scale=d_t[:, w, P - 1:P]).then_inc(kw_ready, 1)
                    if s >= 1:
                        take_probs_t(h, s - 1)
                    act.wait_ge(nm_ready, 8 * h + s + 1)
                    if s >= 2:
                        act.wait_ge(pt_full, 8 * h + s - 1)
                    o = score_bank(i)
                    f(probs[:, w, 0:(i + 1) * P], psf[:, o:o + (i + 1) * P], ACT.Exp, bias=neg_max[:, i:i + 1],
                      accum_out=row_sum[:, i:i + 1]).then_inc(probs_done, 1)
                    if s + 1 < TB:
                        chunk_weights(h, s + 1)
                    if s >= 1:
                        take_out(h, s - 1)
                        act_own.mark(row_squares(h, s - 1))
                        act_own.wait(act)

            def finish_head(h):
                act.wait_ge(hvar_ready, h + 1)
                f(sd8, var8, ACT.Sqrt, bias=EPS, scale=1.0 / P).then_inc(act_head, 1)

            act.wait_ge(dve_head, 1)
            head_copies(0, first=True)
            copy_values(0, first=True)
            take_queries(0)
            take_keys_values(0)
            take_chunk_rows(0)
            own_start = act_own.at
            with act.Fori(0, HEADS - 1, 1) as h:
                act_own.at = own_start + (TB - 1) * h
                head_steps(h)
                head_copies(h + 1)
                take_queries(h + 1)
                take_probs_t(h, TB - 1)
                row_squares(h, TB - 1).then_inc(hsq_ready, 1)
                take_out(h, TB - 1)
                copy_values(h + 1)
                finish_head(h)
                take_keys_values(h + 1)
                take_chunk_rows(h + 1)
            act_own.at = own_start + (TB - 1) * (HEADS - 1)
            head_steps(HEADS - 1)
            take_probs_t(HEADS - 1, TB - 1)
            row_squares(HEADS - 1, TB - 1).then_inc(hsq_ready, 1)
            finish_head(HEADS - 1)
            take_out(HEADS - 1, TB - 1)

            act.wait_ge(dve_head, HEADS + 1)

            def take_f(t):
                for j in range(2):
                    act.wait_ge(ft_full, 2 * t + j + 1)
                    f(f_hi[:, 4 * j:4 * j + 4, t * P:(t + 1) * P],
                      ps[:, 4 + 2 * (t % 2) + j, :].rearrange("p (k n) -> p k n", k=4),
                      ACT.Copy).then_inc(f_hi_ready, 1)

            for t in range(TB):
                b = 2 * (t % 2)
                act.wait_ge(mix_full, 2 * t + 2)
                if t >= 1:
                    act.wait_ge(h1_spilled, 16 * t)
                    act.wait_ge(f_ready, t)
                act_own.do(act, f(h1_blk[:], psf[:, b * HALF:(b + 2) * HALF], ACT.Square,
                                  accum_out=stat_a[:, t:t + 1]))
                f(stat_b[:, t:t + 1], stat_a[:, t:t + 1], ACT.Sqrt, bias=EPS, scale=1.0 / D).then_inc(sd1_ready, 1)
                act.wait_ge(h1_ready, t + 1)
                if t >= 1:
                    act.wait_ge(ft_full, 2 * t)
                act_own.do(act, f(f_blk[:], h1_blk[:], ACT.Square, accum_out=stat_c[:, t:t + 1]))
                f(stat_d[:, t:t + 1], stat_c[:, t:t + 1], ACT.Sqrt, bias=EPS, scale=1.0 / D).then_inc(sd2_ready, 1)
                if t >= 1:
                    take_f(t - 1)
            take_f(TB - 1)

            with act.Fori(0, FG, 1) as g:
                for b in range(4):
                    act.wait_ge(gate_full, 4 * g + b + 1)
                    act.wait_ge(hid_ready, 4 * g + b + 1)
                    f(silu_g[:, b, :], ps[:, b, :], ACT.Silu).then_inc(silu_ready, 1)
                act.wait_ge(y_added, 16 * g + 16)
                for b in range(4):
                    m, n = b % 2, b // 2
                    act.wait_ge(hid_ready, 4 * g + b + 5)
                    f(hid_hi[:, m, half(n)], hid[:, b % 2, :], ACT.Copy).then_inc(hid_hi_ready, 1)

            def h2_norm(t):
                if t == 0:
                    act.wait_ge(up2_full, 4 * FG)
                act.wait_ge(y_added, 16 * FG + 2 * t + 2)
                act_own.do(act, f(junk2[:], y[:, t, :], ACT.Square, accum_out=stat_a[:, t:t + 1]))
                f(stat_b[:, t:t + 1], stat_a[:, t:t + 1], ACT.Sqrt, bias=EPS, scale=1.0 / D).then_inc(h2_sd, 1)

            def h2_part(t):
                for j in range(2):
                    act.wait_ge(h2t_full, 2 * t + j + 1)
                    f(h2_hi[:, 4 * j:4 * j + 4, t * P:(t + 1) * P],
                      ps[:, 4 + 2 * (t % 2) + j, :].rearrange("p (k n) -> p k n", k=4),
                      ACT.Copy).then_inc(h2_hi_ready, 1)

            for t in range(TB - 1):
                h2_norm(t)
            for j in range(4):
                act.wait_ge(pt2_full, j + 1)
                f(p_hi[:, j // 2, half(j % 2)], ps[:, j, :], ACT.Copy).then_inc(p_hi_ready, 1)
            h2_norm(TB - 1)
            h2_part(0)
            h2_part(1)
            act.wait_ge(down_full, 16 * FG)
            for j in range(16):
                act.wait_ge(pp_full, j + 1)
                f(pp[:, j // 2, half(j % 2)], ps[:, j % 4, :], ACT.Copy).then_inc(pp_taken, 1)
                if j in H2_AFTER:
                    h2_part(H2_AFTER[j])
            act.wait_ge(h2_ready, TB)

            def x3_part(j):
                act.wait_ge(x3_ready, j + 1)
                m, n = 2 * (j // 4) + j % 2, (j // 2) % 2
                f(x3_hi[:, m, half(n)], x3[:, j % 2, :], ACT.Copy).then_inc(x3_hi_ready, 1)

            for j in range(16):
                act.wait_ge(pg_full, j + 1)
                if j >= 2:
                    act.wait_ge(x3_ready, j - 1)
                f(sig[:, j % 2, :], ps[:, j % 8, :], ACT.Sigmoid).then_inc(sig_ready, 1)
                x3_part(j)
            for j in range(16):
                act.wait_ge(out_full, j + 1)
                f(y2[:, j // 2, half(j % 2)], ps[:, j % 8, :], ACT.Copy, scale=ALPHA).then_inc(y2_added, 1)

            with act.Fori(0, GROUPS, 1) as g:
                n8 = 8 * g
                for j in range(8):
                    n = j % 2
                    act.wait_ge(pu_full, n8 + j + 1)
                    act.wait_ge(pm_ready, n8 + j + 1)
                    f(u_buf[:, n, HALO:W1], ps[:, j, :], ACT.Copy).then_inc(pu_taken, 1)
                    if j >= 1:
                        act.wait_ge(pm_ready, n8 + j + 2)
                        f(m_hi[:, (j - 1) // 2, half((j - 1) % 2)], win[:, 0, HALO:W1], ACT.Copy).then_inc(pm_hi_ready, 1)
                act.wait_ge(pm_ready, n8 + 10)
                f(m_hi[:, 3, half(1)], win[:, 0, HALO:W1], ACT.Copy).then_inc(pm_hi_ready, 1)
                act.wait_ge(out_full, 16 * g + 16)
                for j in range(8):
                    act.wait_ge(z_full, n8 + j + 1)
                    f(z[:, j // 2, half(j % 2)], ps[:, j, :], ACT.Silu).then_inc(z_taken, 1)
                for j in range(8):
                    m, n = j % 4, j // 4
                    act.wait_ge(gt_ready, n8 + j + 1)
                    f(g_hi[:, m, half(n)], gt[:], ACT.Copy).then_inc(g_hi_ready, 1)
            for t in range(TB):
                act.wait_ge(ln_mean, t + 1)
                act_own.do(act, f(ln_sink[:], y2[:, t, :], ACT.Square, bias=neg_mean[:, t:t + 1],
                                  accum_out=stat_a[:, t:t + 1]))
                f(stat_b[:, t:t + 1], stat_a[:, t:t + 1], ACT.Sqrt, bias=LN_EPS, scale=1.0 / D).then_inc(ln_sd, 1)
                if t < TB - LN_LAST:
                    act.wait_ge(ln_shift, t + 1)
                    f(y2[:, t, :], y2[:, t, :], ACT.Identity, bias=shift[:, t:t + 1],
                      scale=stat_c[:, t:t + 1]).then_inc(ln_normed, 1)

        def dve_program(dve):
            v = nc.vector
            own = dve_own

            def half(n):
                return slice(n * HALF, (n + 1) * HALF)

            def x_scale(t):
                dve.wait_ge(x_sd, t + 1)
                own.do(dve, v.reciprocal(stat_c[:, t:t + 1], stat_b[:, t:t + 1]))
                v.scalar_tensor_tensor(x_nat[:, t, :], x_nat[:, t, :], stat_c[:, t:t + 1], pre_gain[:],
                                       ALU.mult, ALU.mult).then_inc(xn_ready, 1)

            dve.wait_ge(pre_gain_in, 16)
            for q in range(TB // 2):
                x_scale(2 * q)
                x_scale(2 * q + 1)
                for t in (2 * q, 2 * q + 1):
                    if t == 1:
                        dve.wait_ge(pool_hi.sem, 2)
                        w0 = slice(1024, 2048)
                        v.tensor_tensor(w_lo[0][:, w0], stage[:, 1, :], w_hi[0][:, w0].bitcast(F32),
                                        ALU.subtract).then_inc(parted[1], 1)
                    for j in range(2):
                        dve.wait_ge(u_hi_ready, 2 * t + j + 1)
                        ts = slice(t * P, (t + 1) * P)
                        v.tensor_tensor(u_lo[:, 4 * j:4 * j + 4, ts],
                                        ps[:, 4 + 2 * (t % 2) + j, :].rearrange("p (k n) -> p k n", k=4),
                                        u_hi[:, 4 * j:4 * j + 4, ts].bitcast(F32), ALU.subtract).then_inc(u_split, 1)
            dve.wait_ge(pos_in, 32)
            dve.wait_ge(consts, N_CONSTS)
            own.do(dve, v.tensor_copy(ang[:], pos_i[:]))
            own.do(dve, v.tensor_scalar(ang[:], ang[:], inv_freq, None, ALU.mult))
            own.do(dve, v.tensor_scalar(turns[:], ang[:], 1.0 / (2.0 * 3.141592653589793), ROUND, ALU.mult, ALU.add))
            own.do(dve, v.tensor_scalar(turns[:], turns[:], ROUND, None, ALU.subtract))
            for part in (TWO_PI_A, TWO_PI_B, TWO_PI_C):
                own.do(dve, v.scalar_tensor_tensor(ang[:], turns[:], -part, ang[:], ALU.mult, ALU.add))
            v.tensor_scalar(ang[:], ang[:], PI_SAFE, -PI_SAFE, ALU.min, ALU.max).then_inc(rot_ang, 1)
            dve.wait_ge(rot_sin, 2)
            own.do(dve, v.tensor_tensor(rot[0:64, :], rot[0:64, :], rot[0:64, :], ALU.mult))
            own.do(dve, v.tensor_scalar(rot[0:64, :], rot[0:64, :], -2.0, 1.0, ALU.mult, ALU.add))
            own.do(dve, v.tensor_scalar(rot[64:P, :], rot[64:P, :], sin_sign[64:P, :], None, ALU.mult))

            dve.wait_ge(in_taken, 4)
            for m in range(2):
                own.do(dve, v.tensor_tensor(sq[:, m, :], c_q[:, m, :], c_q[:, m, :], ALU.mult))
            own.mark(v.tensor_tensor(sq[:, 0, :], sq[:, 0, :], sq[:, 1, :], ALU.add))
            own.wait(dve)
            v.memset(raw[:, :, 0:CONV - 1], 0.0).then_inc(sq_ready, 1)
            dve.wait_ge(in_taken, 6)
            v.tensor_tensor(sq[:, 1, :], c_kv[:], c_kv[:], ALU.mult).then_inc(sq_ready, 1)
            dve.wait_ge(in_taken, 8)
            dve.wait_ge(cols_in, 16 * (6 + CONV))
            own.do(dve, v.tensor_scalar(f_row[:], f_row[:], gate_bias[0:HEADS, 1:2], None, ALU.add))
            v.scalar_tensor_tensor(e_row[:], f_row[:], -1.0, f_row[:], ALU.mult, ALU.max).then_inc(gates_abs, 1)
            own.mark(v.tensor_scalar(i_row[:], i_row[:], gate_bias[0:HEADS, 0:1], None, ALU.add))
            v.tensor_tensor(k_pe[:], k_pe[:], rot[:], ALU.mult).then_inc(kpe_prod, 1)
            dve.wait_ge(gates_log, 1)
            own.do(dve, v.scalar_tensor_tensor(f_row[:], f_row[:], 0.0, e_row[:], ALU.min, ALU.subtract))
            for c in range(TB):
                cs = slice(c * P, (c + 1) * P)
                own.mark(v.tensor_tensor_scan(b_row[:, cs], ones[0:HEADS, :], f_row[:, cs], 0.0, ALU.mult, ALU.add))
            own.do(dve, v.tensor_tensor_scan(m_row[:], f_row[:], i_row[:], 0.0, ALU.add, ALU.max))
            own.do(dve, v.tensor_tensor(i_row[:], i_row[:], b_row[:], ALU.subtract))
            v.tensor_tensor(b_row[:], b_row[:], m_row[:], ALU.subtract).then_inc(gates_rows, 1)
            dve.wait_ge(kpe_shift, 1)
            v.tensor_tensor(k_pe[0:64, :], k_pe[0:64, :], k_tmp[0:64, :], ALU.add).then_inc(kpe_sum, 1)

            for c in range(8):
                dve.wait_ge(in_taken, 8 + 2 * c + 2)
                rows, o = raw[:, c % 2, :], m_qk[:, c, :]
                own.do(dve, v.tensor_scalar(o, rows[:, 0:S], conv_w[:, c, 0:1], conv_b[:, c:c + 1], ALU.mult, ALU.add))
                for j in range(1, CONV):
                    ins = v.scalar_tensor_tensor(o, rows[:, j:j + S], conv_w[:, c, j:j + 1], o, ALU.mult, ALU.add)
                    if j < CONV - 1:
                        own.do(dve, ins)
                    else:
                        ins.then_inc(conv_done, 1)
            dve.wait_ge(in_taken, 26)
            own.do(dve, v.reciprocal(sd_q[:], sd_q[:]))
            for m in range(2):
                own.mark(v.scalar_tensor_tensor(c_q[:, m, :], c_q[:, m, :], q_gain[:, m:m + 1], sd_q[:],
                                                ALU.mult, ALU.mult))
            dve.wait_ge(in_taken, 28)
            own.do(dve, v.reciprocal(sd_kv[:], sd_kv[:]))
            v.scalar_tensor_tensor(c_kv[:], c_kv[:], kv_gain, sd_kv[:], ALU.mult, ALU.mult).then_inc(latent_ready, 1)

            dve.wait_ge(latent_ready, 1)
            dve.wait_ge(in_full, 40)
            own.mark(v.tensor_copy(c_q_hi[:], c_q[:]))
            own.do(dve, v.tensor_copy(c_kv_hi[:], c_kv[:]))
            own.mark(v.tensor_tensor(c_q_lo[:], c_q[:], c_q_hi[:].bitcast(F32), ALU.subtract))
            v.tensor_tensor(c_kv_lo[:], c_kv[:], c_kv_hi[:].bitcast(F32), ALU.subtract).then_inc(latent_split, 1)

            dve.wait_ge(in_full, 44)
            v.memset(vo[:, :, P:P + 1], 1.0).then_inc(dve_head, 1)
            def rotary_queries(h):
                for n in range(2):
                    dve.wait_ge(up_full, 8 * h + 3 + n)
                    own.do(dve, v.scalar_tensor_tensor(q_pe[:, half(n)], ps[:, 6 - n, :], QK_SCALE, rot[:, half(n)],
                                                       ALU.mult, ALU.mult))
                    own.do(dve, v.tensor_copy(q_pe_hi[:, half(n)], q_pe[:, half(n)]))
                    lo = v.tensor_tensor(q_pe_lo[:, half(n)], q_pe[:, half(n)], q_pe_hi[:, half(n)].bitcast(F32), ALU.subtract)
                    if n == 0:
                        own.mark(lo)
                    else:
                        lo.then_inc(qp_ready, 1)

            def split_queries(h):
                for n in range(2):
                    dve.wait_ge(up_taken, 6 * h + n + 1)
                    v.scalar_tensor_tensor(q_n_lo[:, half(n)], ps[:, n, :], QK_SCALE, q_n_hi[:, half(n)].bitcast(F32),
                                           ALU.mult, ALU.subtract).then_inc(up_split, 1)

            def split_keys(h):
                for n in range(2):
                    dve.wait_ge(up_taken, 6 * h + n + 3)
                    v.tensor_tensor(k_n_lo[:, half(n)], ps[:, (7, 4)[n], :], k_n_hi[:, half(n)].bitcast(F32),
                                    ALU.subtract).then_inc(up_split, 1)

            def split_mix(t, e):
                k, rows = slice(4 * e, 4 * e + 4), mix[:, :, t * P:(t + 1) * P]
                if t >= 2 and e == 0:
                    dve.wait_ge(mix_full, 2 * t - 2)
                own.do(dve, v.tensor_copy(mix_hi[t % 2][:, k, :], rows[:, k, :]))
                v.tensor_tensor(mix_lo[t % 2][:, k, :], rows[:, k, :], mix_hi[t % 2][:, k, :].bitcast(F32),
                                ALU.subtract).then_inc(msplit_ready, 1)

            def row_maxima(h, s):
                i = Q_ORDER[s]
                o = score_bank(i)
                dve.wait_ge(s_full, 8 * h + s + 1)
                v.tensor_reduce(neg_max[:, i:i + 1], psf[:, o:o + (i + 1) * P], AX.X, ALU.max, negate=True).then_inc(nm_ready, 1)

            def head_steps(h, late=False):
                for s in range(TB):
                    w, i = s % 2, Q_ORDER[s]
                    wide = (i + 1) * P
                    dve.wait_ge(st_full, 8 * h + s + 1)
                    dve.wait_ge(dt_ready, 8 * h + s + 1)
                    if s >= 2:
                        dve.wait_ge(num_full, 8 * h + s - 1)
                    v.tensor_tensor(s_t[:, w, :], ps[:, 5, 0:P], d_t[:, w, :], ALU.mult).then_inc(st_ready, 1)
                    if s == 0:
                        row_maxima(h, 0)
                    dve.wait_ge(probs_done, 8 * h + s + 1)
                    own.do(dve, v.reciprocal(row_inv[:, i:i + 1], row_sum[:, i:i + 1]))
                    v.tensor_scalar(probs[:, w, 0:wide], probs[:, w, 0:wide], row_inv[:, i:i + 1], None,
                                    ALU.mult).then_inc(p_ready, 1)
                    if late and s == TB - 2:
                        dve.wait_ge(o_taken, 8 * h + 1)
                        dve.wait_ge(mqkv_ready, 3 * HEADS)
                        split_mix(0, 0)
                    if s + 1 < TB:
                        row_maxima(h, s + 1)
                    dve.wait_ge(cn_full, 8 * h + s + 1)
                    v.tensor_copy(h_nat[:, s, :], ps[:, 7, 0:P + 1]).then_inc(num_taken, 1)
                    if s == 0:
                        v.tensor_copy(state[:], ps[:, 7, 2 * P:3 * P + 1]).then_inc(cn_done, 1)
                    else:
                        dve.wait_ge(cn_done, 8 * h + s)
                        v.scalar_tensor_tensor(state[:], state[:], inter[:, w, P - 1:P], ps[:, 7, 2 * P:3 * P + 1],
                                               ALU.mult, ALU.add).then_inc(cn_done, 1)

            def head_sums(h, late=False):
                dve.wait_ge(num_taken, 8 * h + 8)
                dve.wait_ge(heads_in, 32)
                own.do(dve, v.scalar_tensor_tensor(den, h_nat[:, :, P], -1.0, h_nat[:, :, P], ALU.mult, ALU.max))
                own.do(dve, v.tensor_tensor(den, den, floor_col[:, bass.ds(8 * h, TB)], ALU.max))
                own.do(dve, v.reciprocal(den_inv, den))
                dve.wait_ge(hsq_ready, h + 1)
                own.do(dve, v.tensor_tensor(var8, var8, den_inv, ALU.mult))
                v.tensor_tensor(var8, var8, den_inv, ALU.mult).then_inc(hvar_ready, 1)
                if late:
                    dve.wait_ge(o_taken, 8 * h + Q_ORDER.index(1) + 1)
                    split_mix(1, 0)

            def norm_head(h):
                dve.wait_ge(act_head, h + 2)
                own.do(dve, v.reciprocal(rs8, sd8))
                own.do(dve, v.tensor_tensor(h_scale, rs8, den_inv, ALU.mult))
                scale = h_scale.rearrange("p (t n) -> p t n", n=1).to_broadcast([P, TB, P])
                v.tensor_tensor(h_nat[:, :, 0:P], h_nat[:, :, 0:P], scale, ALU.mult).then_inc(hs_ready, 1)

            def gate_head(h, banks=(2, 3)):
                for n in range(2):
                    dve.wait_ge(ht_full, 2 * h + n + 1)
                    rows = mix[:, bass.ds(h + 4, 1), half(n)].rearrange("p a n -> p (a n)")
                    ins = v.scalar_tensor_tensor(rows, ps[:, banks[n], :], head_gain[:, bass.ds(h, 1)], rows, ALU.mult, ALU.mult)
                    if n == 0:
                        own.mark(ins)
                    else:
                        ins.then_inc(dve_head, 1)

            split_queries(0)
            rotary_queries(0)
            split_keys(0)
            start = own.at
            with dve.Fori(0, HEADS - 1, 1) as h:
                own.at = start + OWN_HEAD * h
                head_steps(h)
                split_queries(h + 1)
                head_sums(h)
                rotary_queries(h + 1)
                norm_head(h)
                split_keys(h + 1)
                gate_head(h)
            own.at = start + OWN_HEAD * (HEADS - 1)
            head_steps(HEADS - 1, late=True)
            head_sums(HEADS - 1, late=True)
            norm_head(HEADS - 1)
            gate_head(HEADS - 1, (5, 6))

            dve.wait_ge(o_taken, 8 * HEADS)
            dve.wait_ge(dve_head, HEADS + 1)
            dve.wait_ge(gains_in, 32)

            def split_f(t):
                for j in range(2):
                    dve.wait_ge(f_hi_ready, 2 * t + j + 1)
                    ts = slice(t * P, (t + 1) * P)
                    v.tensor_tensor(f_lo[:, 4 * j:4 * j + 4, ts],
                                    ps[:, 4 + 2 * (t % 2) + j, :].rearrange("p (k n) -> p k n", k=4),
                                    f_hi[:, 4 * j:4 * j + 4, ts].bitcast(F32), ALU.subtract).then_inc(f_split, 1)

            split_mix(0, 1)
            split_mix(1, 1)
            for t in range(TB):
                b = 2 * (t % 2)
                dve.wait_ge(sd1_ready, t + 1)
                own.do(dve, v.reciprocal(stat_e[:, t:t + 1], stat_b[:, t:t + 1]))
                v.scalar_tensor_tensor(h1_blk[:], psf[:, b * HALF:(b + 2) * HALF], stat_e[:, t:t + 1], post_gain[:],
                                       ALU.mult, ALU.mult).then_inc(mix_taken, 1)
                dve.wait_ge(mix_taken, t + 1)
                dve.wait_ge(xblk_in, 16 * t + 16)
                v.tensor_tensor(h1_blk[:], h1_blk[:], x_blk[:], ALU.add).then_inc(h1_ready, 1)
                if t + 2 < TB:
                    split_mix(t + 2, 0)
                    split_mix(t + 2, 1)
                dve.wait_ge(sd2_ready, t + 1)
                own.do(dve, v.reciprocal(stat_f[:, t:t + 1], stat_d[:, t:t + 1]))
                v.scalar_tensor_tensor(f_blk[:], h1_blk[:], stat_f[:, t:t + 1], ffn_gain[:],
                                       ALU.mult, ALU.mult).then_inc(f_ready, 1)
                if t >= 1:
                    split_f(t - 1)
            split_f(TB - 1)

            dve.wait_ge(f_ready, TB)
            for j in range(4):
                v.memset(hid[:, 0, j:j + 1], 0.0).then_inc(hid_ready, 1)
            dve.wait_ge(hid_ready, 4)
            start = own.at
            def ffn_group(g, last=False):
                for b in range(4):
                    m, n = b % 2, b // 2
                    dve.wait_ge(up2_full, 4 * g + b + 1)
                    dve.wait_ge(silu_ready, 4 * g + b + 1)
                    v.tensor_tensor(hid[:, b % 2, :], ps[:, 4 + b, :], silu_g[:, b, :], ALU.mult).then_inc(hid_ready, 1)
                    dve.wait_ge(hid_hi_ready, 4 * g + b + 1)
                    v.tensor_tensor(hid_lo[:, m, half(n)], hid[:, b % 2, :], hid_hi[:, m, half(n)].bitcast(F32),
                                    ALU.subtract).then_inc(hid_split, 1)
                for j in range(16):
                    dve.wait_ge(down_full, 16 * g + j + 1)
                    rows = y[:, j // 2, half(j % 2)]
                    v.tensor_tensor(rows, ps[:, j % 8, :], rows, ALU.add).then_inc(y_added, 1)
                    if last and j % 2 == 1 and 3 <= j <= 13:
                        post_norm(j // 2 - 1)

            def post_norm(t):
                if t == 0:
                    dve.wait_ge(fpg_in, 16)
                dve.wait_ge(h2_sd, t + 1)
                own.do(dve, v.reciprocal(stat_c[:, t:t + 1], stat_b[:, t:t + 1]))
                v.scalar_tensor_tensor(y[:, t, :], y[:, t, :], stat_c[:, t:t + 1], ffn_post_gain[:],
                                       ALU.mult, ALU.mult).then_inc(h2_normed, 1)

            with dve.Fori(0, FG - 1, 1) as g:
                ffn_group(g)
            ffn_group(FG - 1, last=True)

            for j in range(4):
                dve.wait_ge(p_hi_ready, j + 1)
                o = (slice(None), j // 2, half(j % 2))
                v.tensor_tensor(p_lo[o], ps[:, j, :], p_hi[o].bitcast(F32), ALU.subtract).then_inc(p_split, 1)
            post_norm(TB - 2)
            post_norm(TB - 1)
            dve.wait_ge(h2_ready, TB)
            for t in range(TB):
                for j in range(2):
                    dve.wait_ge(h2_hi_ready, 2 * t + j + 1)
                    ts = slice(t * P, (t + 1) * P)
                    v.tensor_tensor(h2_lo[:, 4 * j:4 * j + 4, ts],
                                    ps[:, 4 + 2 * (t % 2) + j, :].rearrange("p (k n) -> p k n", k=4),
                                    h2_hi[:, 4 * j:4 * j + 4, ts].bitcast(F32), ALU.subtract).then_inc(h2_split, 1)
            for j in range(16):
                m, n = 2 * (j // 4) + j % 2, (j // 2) % 2
                o = (slice(None), m, half(n))
                dve.wait_ge(sig_ready, j + 1)
                if j >= 2:
                    dve.wait_ge(x3_hi_ready, j - 1)
                t = x3[:, j % 2, :]
                own.do(dve, v.tensor_tensor(t, sig[:, j % 2, :], pp[o], ALU.mult))
                own.do(dve, v.tensor_tensor(t, t, h2_lo[o].bitcast(F32), ALU.add))
                v.tensor_tensor(t, t, h2_hi[o].bitcast(F32), ALU.add).then_inc(x3_ready, 1)
                dve.wait_ge(x3_hi_ready, j + 1)
                v.tensor_tensor(x3_lo[o], t, x3_hi[o].bitcast(F32), ALU.subtract).then_inc(x3_split, 1)

            def row_mean(t):
                dve.wait_ge(y2_added, 16 * GROUPS + 2 * t + 2)
                v.scalar_tensor_tensor(neg_mean[:, t:t + 1], row_sums[:, 2 * t:2 * t + 1], row_sums[:, 2 * t + 1:2 * t + 2],
                                       neg_inv_d, ALU.add, ALU.mult).then_inc(ln_mean, 1)

            def row_shift(t):
                dve.wait_ge(ln_sd, t + 1)
                own.do(dve, v.reciprocal(stat_c[:, t:t + 1], stat_b[:, t:t + 1]))
                v.tensor_tensor(shift[:, t:t + 1], neg_mean[:, t:t + 1], stat_c[:, t:t + 1], ALU.mult).then_inc(ln_shift, 1)

            def add_bias(t):
                if t == 0:
                    dve.wait_ge(ln_in, 32)
                dve.wait_ge(ln_gained, t + 1)
                v.tensor_tensor(y2[:, t, :], y2[:, t, :], ln_bias[:], ALU.add).then_inc(out_ready, 1)

            def gain_deviations(t):
                dve.wait_ge(ln_mean, t + 1)
                own.mark(v.scalar_tensor_tensor(ln_dev[:, t % 2, :], y2[:, t, :], neg_mean[:, t:t + 1], ln_gain[:],
                                                ALU.add, ALU.mult))

            def scale_deviations(t):
                dve.wait_ge(ln_sd, t + 1)
                own.do(dve, v.reciprocal(stat_c[:, t:t + 1], stat_b[:, t:t + 1]))
                v.scalar_tensor_tensor(y2[:, t, :], ln_dev[:, t % 2, :], stat_c[:, t:t + 1], ln_bias[:],
                                       ALU.mult, ALU.add).then_inc(out_ready, 1)

            dve.wait_ge(x3_split, 16)
            v.memset(u_buf[:, 0, 0:HALO], 0.0).then_inc(pm_ready, 1)
            v.memset(u_buf[:, 1, 0:HALO], 0.0).then_inc(pm_ready, 1)
            dve.wait_ge(pm_ready, 2)
            for g, width in enumerate(WINDOWS):
                n8 = 8 * g
                for j in range(8):
                    n, m = j % 2, j // 2
                    dve.wait_ge(pu_taken, n8 + j + 1)
                    u = u_buf[:, n, :]
                    if n == 0:
                        own.do(dve, v.tensor_copy(u_buf[:, 1, 0:HALO], u[:, HALF:W1]))
                    if n8 + j >= 1:
                        dve.wait_ge(pm_split, n8 + j)
                    src, reach, steps = u, 1, g + 1
                    for step in range(steps):
                        dst = win[:, (steps - step) % 2, :]
                        own.do(dve, v.tensor_tensor(dst[:, reach * 2 - 1:W1], src[:, reach * 2 - 1:W1],
                                                    src[:, reach - 1:W1 - reach], ALU.add))
                        src, reach = dst, reach * 2
                    ins = v.scalar_tensor_tensor(win[:, 0, HALO:W1], src[:, HALO:W1], 1.0 / width, u[:, HALO:W1],
                                                 ALU.mult, ALU.subtract)
                    if n == 0:
                        own.do(dve, ins)
                        first = slice(HALO, HALO + width)
                        own.do(dve, v.tensor_tensor(win[:, 0, first], src[:, first], inv_count[:, 0:width], ALU.mult))
                        ins = v.tensor_tensor(win[:, 0, first], win[:, 0, first], u[:, first], ALU.subtract)
                    ins.then_inc(pm_ready, 1)
                    dve.wait_ge(pm_hi_ready, n8 + j + 1)
                    o = (slice(None), m, half(n))
                    v.tensor_tensor(m_lo[o], win[:, 0, HALO:W1], m_hi[o].bitcast(F32), ALU.subtract).then_inc(pm_split, 1)
                for j in range(8):
                    m, n = j % 4, j // 4
                    dve.wait_ge(grp_full, n8 + j + 1)
                    dve.wait_ge(z_taken, n8 + 2 * m + n + 1)
                    if n8 + j >= 1:
                        dve.wait_ge(g_split, n8 + j)
                    v.scalar_tensor_tensor(gt[:], ps[:, j, :], pool_gain[:, 4 * g + m:4 * g + m + 1], z[:, m, half(n)],
                                           ALU.mult, ALU.mult).then_inc(gt_ready, 1)
                    dve.wait_ge(g_hi_ready, n8 + j + 1)
                    lo = g_lo0[:, m, :] if n == 0 else m_lo[:, m, 0:HALF]
                    v.tensor_tensor(lo, gt[:], g_hi[:, m, half(n)].bitcast(F32), ALU.subtract).then_inc(g_split, 1)
                for j in range(16):
                    q, t = 16 * g + j, j // 2
                    dve.wait_ge(out_full, 16 + q + 1)
                    rows = y2[:, t, half(j % 2)]
                    dve.wait_ge(y2_added, max(q + 1, 16))
                    if g < GROUPS - 1:
                        v.tensor_tensor(rows, ps[:, j % 8, :], rows, ALU.add).then_inc(y2_added, 1)
                        continue
                    v.scalar_tensor_tensor(rows, ps[:, j % 8, :], 1.0, rows, ALU.mult, ALU.add,
                                           accum_out=row_sums[:, j:j + 1]).then_inc(y2_added, 1)
                    if j % 2 == 0 and 1 <= t <= TB - LN_LAST and t != TB // 2:
                        row_shift(t - 1)
                    if j % 2 == 1:
                        row_mean(t)
                        if t >= TB - LN_LAST:
                            gain_deviations(t)
                        if t == TB // 2 - 1:
                            row_shift(t)
                            for b in range(TB // 2):
                                if b not in POOL_BIAS:
                                    add_bias(b)
            for t in range(TB - LN_LAST, TB):
                scale_deviations(t)

        N_CONSTS = 13 + HALO
        OWN_HEAD = 8 + 4 + 5 + 2 + 1

        block = ctx.enter_context(nc.Block())

        @block.sync
        def _(sp):
            sp_program(sp)

        @block.gpsimd
        def _(pool):
            pool_program(pool)

        @block.tensor
        def _(pe):
            pe_program(pe)

        @block.scalar
        def _(act):
            act_program(act)

        @block.vector
        def _(dve):
            dve_program(dve)


_INS = ["x", "p", "positions", "attn_pre_norm", "attn_post_norm", "w_in", "q_norm", "kv_norm", "w_uq", "w_ukv",
        "conv_w", "conv_b", "gate_bias_i", "gate_bias_f", "mlstm_norm", "w_out", "ffn_pre_norm", "ffn_post_norm",
        "w_gate", "w_up", "w_down", "w_ple_proj", "w_ple_gate", "ln_g_2", "ln_b_2", "pool_w_in_2", "pool_w_grp_2",
        "pool_scale_2", "pool_w_out_2"]


def kernel(**inputs):
    import numpy as _np
    import concourse.bacc as _bacc
    from concourse import mybir as _mybir
    from concourse.bass_utils import run_bass_kernel_spmd as _run

    nc = _bacc.Bacc("TRN2", target_bir_lowering=False, num_devices=1)
    arrays, aps = {}, {}
    given = {name: _np.ascontiguousarray(inputs[name]) for name in _INS}
    freq = _np.float32(10000.0) ** (-_np.arange(0, ROPE, 2, dtype=_np.float32) / _np.float32(ROPE))
    given["inv_freq"] = _np.ascontiguousarray(_np.tile(freq.astype(_np.float32), 4)[:, None])
    for name, x in given.items():
        arrays[f"in_{name}"] = x
        aps[name] = nc.dram_tensor(f"in_{name}", x.shape, _mybir.dt.from_np(x.dtype), kind="ExternalInput").ap()
    out = nc.dram_tensor("out_0", (1, S, D), _mybir.dt.float32, kind="ExternalOutput").ap()
    build(nc, aps, out)
    r = _run(nc, [arrays], core_ids=[0])
    return r.results[0]["out_0"]
```
